# Optimizing a Trainium2 kernel written in Bass

```python
import jax, jax.numpy as jnp
from jax import lax
import numpy as np

D_MODEL = 1024
BATCH = 1
SEQ = 512
DEPTH = 2
DEC_BATCH = 8
DEC_SEQ = 8
PAST_LEN = 2048
PAGE_SIZE = 128

N_MLA = (DEPTH + 1) // 2
N_RWKV = DEPTH // 2
MLA_HEADS = 8
Q_RANK = 384
KV_RANK = 256
NOPE_DIM = 128
ROPE_DIM = 64
QK_DIM = NOPE_DIM + ROPE_DIM
V_DIM = 128
ROPE_THETA = 10000.0
ATTN_SCALE = QK_DIM ** -0.5
Q_BLOCK = 128
HEAD_SIZE = 64
RWKV_HEADS = D_MODEL // HEAD_SIZE
DECAY_LORA = 64
AAA_LORA = 64
MV_LORA = 32
GATE_LORA = 128
LNX_EPS = 64e-5
D_FF = 2816
RMS_EPS = 1e-6
POOL_NUM = 5
POOL_DEN = 4

kernel_name = 'hybrid_mla_rwkv7_macaron_step'

def rmsnorm(x, g, eps=RMS_EPS):
    xf = x.astype(jnp.float32)
    y = xf * lax.rsqrt(jnp.mean(xf * xf, axis=-1, keepdims=True) + eps)
    return (y * g.astype(jnp.float32)).astype(x.dtype)

def swiglu(h, w_gate, w_up, w_down):
    return (jax.nn.silu(h @ w_gate) * (h @ w_up)) @ w_down

def rope_tables(pos):
    inv = ROPE_THETA ** (-jnp.arange(0, ROPE_DIM, 2, dtype=jnp.float32) / ROPE_DIM)
    ang = pos.astype(jnp.float32)[:, None] * inv[None, :]
    return jnp.cos(ang), jnp.sin(ang)

def apply_rope(x, cos, sin):
    half = ROPE_DIM // 2
    xf = x.astype(jnp.float32)
    x1, x2 = xf[..., :half], xf[..., half:]
    return jnp.concatenate([x1 * cos - x2 * sin, x1 * sin + x2 * cos], axis=-1).astype(x.dtype)

def mla_project(h, pos, w_down, g_qlat, g_kvlat, w_uq, g_qn):
    b, l, _ = h.shape
    lat = h @ w_down
    cq = rmsnorm(lat[..., :Q_RANK], g_qlat)
    c = rmsnorm(lat[..., Q_RANK:Q_RANK + KV_RANK], g_kvlat)
    cos, sin = rope_tables(pos)
    kr = apply_rope(lat[..., Q_RANK + KV_RANK:], cos, sin)
    q = (cq @ w_uq).reshape(b, l, MLA_HEADS, QK_DIM)
    q = jnp.concatenate([q[..., :NOPE_DIM],
                         apply_rope(q[..., NOPE_DIM:], cos[:, None], sin[:, None])], axis=-1)
    return rmsnorm(q, g_qn), c, kr

def mla_keys(c, kr, w_uk, g_kn):
    k_nope = jnp.einsum('...tr,rhd->...thd', c, w_uk)
    k_rope = jnp.broadcast_to(kr[..., None, :], k_nope.shape[:-1] + (ROPE_DIM,)).astype(k_nope.dtype)
    return rmsnorm(jnp.concatenate([k_nope, k_rope], axis=-1), g_kn)

def mla_prompt_attend(q, c, kr, w_uk, w_uv, g_kn):
    b, l = q.shape[:2]
    k = mla_keys(c, kr, w_uk, g_kn)
    v = jnp.einsum('btr,rhd->bthd', c, w_uv)
    nb = l // Q_BLOCK
    qb = jnp.swapaxes(q.reshape(b, nb, Q_BLOCK, MLA_HEADS, QK_DIM), 0, 1)
    key_pos = jnp.arange(l)

    def block(args):
        qi, start = args
        s = jnp.einsum('bqhd,bkhd->bhqk', qi, k, preferred_element_type=jnp.float32) * ATTN_SCALE
        mask = (start + jnp.arange(Q_BLOCK))[:, None] >= key_pos[None, :]
        p = jax.nn.softmax(jnp.where(mask, s, -jnp.inf), axis=-1)
        return jnp.einsum('bhqk,bkhd->bqhd', p.astype(v.dtype), v)

    o = lax.map(block, (qb, jnp.arange(nb) * Q_BLOCK))
    return jnp.swapaxes(o, 0, 1).reshape(b, l, MLA_HEADS, V_DIM)

def mla_sample_attend(q, c_new, kr_new, cache_c, cache_kr, m, page_table, w_uk, w_uv, g_kn):
    s_len = q.shape[1]
    n_past = page_table.shape[1] * PAGE_SIZE
    mask = jnp.arange(n_past + s_len)[None, :] <= (n_past + jnp.arange(s_len))[:, None]

    def one_seq(args):
        pt, qs, cn, krn = args
        c_all = jnp.concatenate([cache_c[m, pt].reshape(n_past, KV_RANK).astype(cn.dtype), cn], axis=0)
        kr_all = jnp.concatenate([cache_kr[m, pt].reshape(n_past, ROPE_DIM).astype(krn.dtype), krn], axis=0)
        k = mla_keys(c_all, kr_all, w_uk, g_kn)
        s = jnp.einsum('qhd,thd->hqt', qs, k, preferred_element_type=jnp.float32) * ATTN_SCALE
        p = jax.nn.softmax(jnp.where(mask[None], s, -jnp.inf), axis=-1)
        o_lat = jnp.einsum('hqt,tr->qhr', p.astype(c_all.dtype), c_all)
        return jnp.einsum('qhr,rhd->qhd', o_lat, w_uv)

    return lax.map(one_seq, (page_table, q, c_new, kr_new))

def wkv_step(state, inp):
    r, w, k, v, a, b = inp
    sa = jnp.einsum('bhij,bhj->bhi', state, a)
    state = state * w[:, :, None, :] + sa[..., None] * b[:, :, None, :] + v[..., None] * k[:, :, None, :]
    return state, jnp.einsum('bhij,bhj->bhi', state, r)

def rwkv_time_mix(h, shift_prev, wkv0, v_first, mu, w_r, w_k, w_v, w_o, w0, w1, w2,
                  a0, a1, a2, g1, g2, k_k, k_a, r_k, lnx_w, lnx_b, vres):
    b, l, d = h.shape
    f32 = jnp.float32
    prev = jnp.concatenate([shift_prev[:, None, :].astype(h.dtype), h[:, :-1]], axis=1)
    xx = prev - h
    xr, xw, xk, xv, xa, xg = [h + xx * mu[i] for i in range(6)]
    r = xr @ w_r
    k = xk @ w_k
    v = xv @ w_v
    w_log = -jax.nn.softplus(-(w0 + jnp.tanh(xw @ w1) @ w2)) - 0.5
    decay = jnp.exp(-jnp.exp(w_log.astype(f32)))
    if vres is None:
        v_first = v
    else:
        v0, v1, v2 = vres
        v = v + (v_first - v) * jax.nn.sigmoid(v0 + (xv @ v1) @ v2)
    a = jax.nn.sigmoid(a0 + (xa @ a1) @ a2)
    g = jax.nn.sigmoid(xg @ g1) @ g2
    heads = lambda t: t.astype(f32).reshape(b, l, RWKV_HEADS, HEAD_SIZE)
    kk = heads(k * k_k)
    kk = kk / jnp.maximum(jnp.sqrt(jnp.sum(kk * kk, axis=-1, keepdims=True)), 1e-12)
    k = k * (1.0 + (a - 1.0) * k_a)
    rh, kh, vh, ah, wh = heads(r), heads(k), heads(v), heads(a), heads(decay)
    tm = lambda t: jnp.swapaxes(t, 0, 1)
    state, y = lax.scan(wkv_step, wkv0.astype(f32),
                        (tm(rh), tm(wh), tm(kh), tm(vh), tm(-kk), tm(kk * ah)))
    y = tm(y)
    mean = jnp.mean(y, axis=-1, keepdims=True)
    var = jnp.mean(jnp.square(y - mean), axis=-1, keepdims=True)
    y = ((y - mean) * lax.rsqrt(var + LNX_EPS)).reshape(b, l, d) * lnx_w.astype(f32) + lnx_b.astype(f32)
    bonus = jnp.sum(rh * kh * r_k.astype(f32).reshape(RWKV_HEADS, HEAD_SIZE), axis=-1, keepdims=True) * vh
    y = y + bonus.reshape(b, l, d)
    out = (y * g.astype(f32)).astype(h.dtype) @ w_o
    return out, state, h[:, -1], v_first

def setup_inputs(seed: int = 0) -> dict:
    key = jax.random.key(seed)
    ks = iter(jax.random.split(key, 80))
    f32 = jnp.float32

    def nrm(shape, scale):
        return jax.random.normal(next(ks), shape, f32) * scale

    def uni(shape, lo, hi):
        return jax.random.uniform(next(ks), shape, f32, minval=lo, maxval=hi)

    def gain(shape):
        return 1.0 + nrm(shape, 0.05)

    n_pages = PAST_LEN // PAGE_SIZE
    n_pool = (DEC_BATCH * n_pages * POOL_NUM) // POOL_DEN
    perm = jax.random.permutation(next(ks), n_pool)
    page_table = perm[:DEC_BATCH * n_pages].reshape(DEC_BATCH, n_pages).astype(jnp.int32)
    D = D_MODEL
    HQ = MLA_HEADS * QK_DIM
    HV = MLA_HEADS * V_DIM
    return {
        'x_prompt': nrm((BATCH, SEQ, D), 1.0),
        'x_sample': nrm((DEC_BATCH, DEC_SEQ, D), 1.0),
        'cache_kv_latent': nrm((N_MLA, n_pool, PAGE_SIZE, KV_RANK), 1.0),
        'cache_k_rope': nrm((N_MLA, n_pool, PAGE_SIZE, ROPE_DIM), 1.0),
        'state_wkv': nrm((N_RWKV, DEC_BATCH, RWKV_HEADS, HEAD_SIZE, HEAD_SIZE), 0.3),
        'state_shift': nrm((N_RWKV, DEC_BATCH, D), 1.0),
        'page_table': page_table,
        'ffn_norm': gain((DEPTH, 2, D)),
        'ffn_w_gate': nrm((DEPTH, 2, D, D_FF), D ** -0.5),
        'ffn_w_up': nrm((DEPTH, 2, D, D_FF), D ** -0.5),
        'ffn_w_down': nrm((DEPTH, 2, D_FF, D), D_FF ** -0.5),
        'mix_norm': gain((DEPTH, D)),
        'mla_w_down': nrm((N_MLA, D, Q_RANK + KV_RANK + ROPE_DIM), D ** -0.5),
        'mla_g_q_lat': gain((N_MLA, Q_RANK)),
        'mla_g_kv_lat': gain((N_MLA, KV_RANK)),
        'mla_w_uq': nrm((N_MLA, Q_RANK, HQ), Q_RANK ** -0.5),
        'mla_w_uk': nrm((N_MLA, KV_RANK, MLA_HEADS, NOPE_DIM), KV_RANK ** -0.5),
        'mla_w_uv': nrm((N_MLA, KV_RANK, MLA_HEADS, V_DIM), KV_RANK ** -0.5),
        'mla_g_qn': gain((N_MLA, QK_DIM)),
        'mla_g_kn': gain((N_MLA, QK_DIM)),
        'mla_w_o': nrm((N_MLA, HV, D), HV ** -0.5),
        'rwkv_mu': uni((N_RWKV, 6, D), 0.0, 1.0),
        'rwkv_w_r': nrm((N_RWKV, D, D), D ** -0.5),
        'rwkv_w_k': nrm((N_RWKV, D, D), D ** -0.5),
        'rwkv_w_v': nrm((N_RWKV, D, D), D ** -0.5),
        'rwkv_w_o': nrm((N_RWKV, D, D), D ** -0.5),
        'rwkv_w0': uni((N_RWKV, D), -6.5, -1.5),
        'rwkv_w1': nrm((N_RWKV, D, DECAY_LORA), D ** -0.5),
        'rwkv_w2': nrm((N_RWKV, DECAY_LORA, D), 0.1 * DECAY_LORA ** -0.5),
        'rwkv_a0': nrm((N_RWKV, D), 0.1),
        'rwkv_a1': nrm((N_RWKV, D, AAA_LORA), D ** -0.5),
        'rwkv_a2': nrm((N_RWKV, AAA_LORA, D), 0.1 * AAA_LORA ** -0.5),
        'rwkv_v0': nrm((N_RWKV - 1, D), 0.5),
        'rwkv_v1': nrm((N_RWKV - 1, D, MV_LORA), D ** -0.5),
        'rwkv_v2': nrm((N_RWKV - 1, MV_LORA, D), 0.1 * MV_LORA ** -0.5),
        'rwkv_g1': nrm((N_RWKV, D, GATE_LORA), D ** -0.5),
        'rwkv_g2': nrm((N_RWKV, GATE_LORA, D), GATE_LORA ** -0.5),
        'rwkv_k_k': 0.85 + nrm((N_RWKV, D), 0.05),
        'rwkv_k_a': gain((N_RWKV, D)),
        'rwkv_r_k': nrm((N_RWKV, D), 0.1),
        'rwkv_lnx_w': gain((N_RWKV, D)),
        'rwkv_lnx_b': nrm((N_RWKV, D), 0.02),
    }

def reference(x_prompt, x_sample, cache_kv_latent, cache_k_rope, state_wkv, state_shift, page_table,
              ffn_norm, ffn_w_gate, ffn_w_up, ffn_w_down, mix_norm,
              mla_w_down, mla_g_q_lat, mla_g_kv_lat, mla_w_uq, mla_w_uk, mla_w_uv, mla_g_qn, mla_g_kn, mla_w_o,
              rwkv_mu, rwkv_w_r, rwkv_w_k, rwkv_w_v, rwkv_w_o, rwkv_w0, rwkv_w1, rwkv_w2,
              rwkv_a0, rwkv_a1, rwkv_a2, rwkv_v0, rwkv_v1, rwkv_v2, rwkv_g1, rwkv_g2,
              rwkv_k_k, rwkv_k_a, rwkv_r_k, rwkv_lnx_w, rwkv_lnx_b):

    def trunk(x, pos, attend, shift0, wkv0):
        b, l, _ = x.shape
        lat_rows, rope_rows, wkv_out, shift_out = [], [], [], []
        v_first = None
        for i in range(DEPTH):
            h = rmsnorm(x, ffn_norm[i, 0])
            x = x + 0.5 * swiglu(h, ffn_w_gate[i, 0], ffn_w_up[i, 0], ffn_w_down[i, 0])
            h = rmsnorm(x, mix_norm[i])
            if i % 2 == 0:
                m = i // 2
                q, c, kr = mla_project(h, pos, mla_w_down[m], mla_g_q_lat[m], mla_g_kv_lat[m],
                                       mla_w_uq[m], mla_g_qn[m])
                o = attend(m, q, c, kr)
                x = x + o.reshape(b, l, MLA_HEADS * V_DIM) @ mla_w_o[m]
                lat_rows.append(c)
                rope_rows.append(kr)
            else:
                j = i // 2
                vres = None if j == 0 else (rwkv_v0[j - 1], rwkv_v1[j - 1], rwkv_v2[j - 1])
                o, st, sh, v_first = rwkv_time_mix(
                    h, shift0[j], wkv0[j], v_first, rwkv_mu[j], rwkv_w_r[j], rwkv_w_k[j], rwkv_w_v[j],
                    rwkv_w_o[j], rwkv_w0[j], rwkv_w1[j], rwkv_w2[j], rwkv_a0[j], rwkv_a1[j], rwkv_a2[j],
                    rwkv_g1[j], rwkv_g2[j], rwkv_k_k[j], rwkv_k_a[j], rwkv_r_k[j],
                    rwkv_lnx_w[j], rwkv_lnx_b[j], vres)
                x = x + o
                wkv_out.append(st)
                shift_out.append(sh)
            h = rmsnorm(x, ffn_norm[i, 1])
            x = x + 0.5 * swiglu(h, ffn_w_gate[i, 1], ffn_w_up[i, 1], ffn_w_down[i, 1])
        return x, jnp.stack(lat_rows), jnp.stack(rope_rows), jnp.stack(wkv_out), jnp.stack(shift_out)

    prompt_attend = lambda m, q, c, kr: mla_prompt_attend(q, c, kr, mla_w_uk[m], mla_w_uv[m], mla_g_kn[m])
    sample_attend = lambda m, q, c, kr: mla_sample_attend(q, c, kr, cache_kv_latent, cache_k_rope, m,
                                                          page_table, mla_w_uk[m], mla_w_uv[m], mla_g_kn[m])

    bp, lp = x_prompt.shape[:2]
    shift0_p = jnp.zeros((N_RWKV, bp, D_MODEL), x_prompt.dtype)
    wkv0_p = jnp.zeros((N_RWKV, bp, RWKV_HEADS, HEAD_SIZE, HEAD_SIZE), jnp.float32)
    y_prompt, p_lat, p_rope, p_wkv, p_shift = trunk(x_prompt, jnp.arange(lp), prompt_attend, shift0_p, wkv0_p)

    n_past = page_table.shape[1] * PAGE_SIZE
    pos_s = n_past + jnp.arange(x_sample.shape[1])
    y_sample, s_lat, s_rope, s_wkv, s_shift = trunk(x_sample, pos_s, sample_attend, state_shift, state_wkv)

    return (y_prompt, y_sample, p_lat, p_rope, p_wkv, p_shift, s_lat, s_rope, s_wkv, s_shift)


_drawn_inputs = setup_inputs


def setup_inputs(seed=0):
    import zlib

    import numpy as np

    out = dict(_drawn_inputs(seed))
    spreads = {}
    factors = {'mla_g_q_lat': 6.164,
     'mla_g_qn': 6.54,
     'mla_g_kn': 6.069,
     'rwkv_w1': 8.0,
     'rwkv_w2': 8.0,
     'rwkv_lnx_b': 6.788,
     'rwkv_lnx_w': 2.833}
    for name, (base, spread) in spreads.items():
        noise = np.random.default_rng([zlib.crc32(name.encode()), seed]).standard_normal(out[name].shape)
        drawn = base * np.exp(spread * noise) if base else spread * noise
        out[name] = __import__('jax').numpy.asarray(drawn.astype(out[name].dtype))
    for name, factor in factors.items():
        out[name] = (out[name] * factor).astype(out[name].dtype)
    return out
```

```python
import numpy as np
import concourse.bass as bass
from concourse import mybir
from contextlib import ExitStack

F32 = mybir.dt.float32
F32R = mybir.dt.float32r
I32 = mybir.dt.int32
ACT = mybir.ActivationFunctionType
ALU = mybir.AluOpType
AX = mybir.AxisListType

P = 128
D = 1024
KD = D // P
SEQ = 512
SB, SQ = 8, 8
NS = SB * SQ
T = SEQ + NS
HT = T // 2
FF = 2816
FT = FF // P
PARTS = (12, 10)
NFFN = 4
H = 8
QK, NOPE, ROPE, VD = 192, 128, 64, 128
QR_T, KV_T = 3, 2
KV = KV_T * P
PAGE, PAGES, POOL = 128, 16, 160
SCALE = QK ** -0.5
EPS = 1e-6
LN_EPS = 64e-5
HS = 64
CH = 64
NC_ = T // CH
ITEM = 16 * P

N_FFN = sum(PARTS) + 2 * KD
I_FFN0 = 0
I_LAT = I_FFN0 + N_FFN
I_UQ = I_LAT + 3
I_UK = I_UQ + H
I_UV = I_UK + 1
I_MO = I_UV + 1
I_FFN1 = I_MO + 4
I_FFN2 = I_FFN1 + N_FFN
I_R = I_FFN2 + N_FFN
I_K = I_R + 4
I_V = I_K + 4
I_RO = I_V + 4
I_FFN3 = I_RO + 4
N_ITEMS = I_FFN3 + N_FFN
I_FFN = (I_FFN0, I_FFN1, I_FFN2, I_FFN3)
NORM_OF_FFN = (0, 2, 3, 5)
XHAT_OF_NORM = {0: 0, 1: 1, 2: 2, 3: 3, 5: 4}

V_G = {n: 8 * n for n in range(6)}
V_GQL, V_GKV = 48, 51
V_GQN, V_GQR, V_GKN, V_GKR = 53, 54, 55, 56
V_EPS, V_LNEPS = 57, 58
V_MU = 64
V_W0, V_A0, V_KK, V_KA, V_RK, V_LW, V_LB = (112 + 8 * n for n in range(7))
NV = 168
N_STAGE_SEMS = 106
C_ID, C_ONE, C_BLK, C_FOLD = 0, 128, 256, 384
NCONST = 448
R_GRAM, R_LOW, R_B8, R_OFF, R_SCAN, R_SEQ = 0, 1152, 1728, 1792, 1984, 2560
NRC = 2568


class Map:

    def __init__(self, nc, base):
        self.nc, self.base = nc, base

    def at(self, name, col, shape, dtype=F32):
        return self.nc.alloc_sbuf_tensor_at(name, [P] + list(shape), dtype, offset=self.base + 4 * col)


def program(nc, a, o):
    ctx = ExitStack()
    names = {}

    def sem(name):
        names[name] = ctx.enter_context(nc.semaphore(name))
        return names[name]

    shared = [ctx.enter_context(nc.semaphore(f"stage_{k}")) for k in range(N_STAGE_SEMS)]
    taken = {"attention": 0, "recurrence": 0}

    def stage_sem(stage, name):
        taken[stage] += 1
        names[name] = shared[taken[stage] - 1]
        return names[name]

    m = Map(nc, -(-nc.sbuf_base // 32) * 32)

    X = m.at("X", 0, [KD, T])
    XH = m.at("XH", 4608, [KD, T], F32R)
    XL = m.at("XL", 9216, [KD, T], F32R)
    RAW = [m.at(f"RAW{s}", 13824 + 2048 * s, [ITEM]) for s in range(2)]
    WH = [m.at(f"WH{s}", 17920 + 2048 * s, [ITEM], F32R) for s in range(2)]
    WL = [m.at(f"WL{s}", 22016 + 2048 * s, [ITEM], F32R) for s in range(2)]
    RSTD = m.at("RSTD", 26112, [T])
    T1 = m.at("T1", 26688, [T])
    T2 = m.at("T2", 27264, [T])
    T3 = m.at("T3", 27840, [T])
    T4 = m.at("T4", 28416, [T])
    SQT = m.at("SQT", 28992, [T])
    SQACC = m.at("SQACC", 29568, [T])
    CONST = m.at("CONST", 30144, [NCONST])
    VEC = m.at("VEC", 30592, [NV])
    IDENT = CONST[:, C_ID:C_ID + P]
    ONES = CONST[:, C_ONE:C_ONE + P]
    BLK = CONST[:, C_BLK:C_BLK + P]
    FOLD = CONST[:, C_FOLD:C_FOLD + 64]
    A0 = 30800
    HH = m.at("HH", A0, [PARTS[0], T], F32R)
    HL = m.at("HL", A0 + PARTS[0] * T, [PARTS[0], T], F32R)

    PS = ctx.enter_context(nc.psum_tensor("PS", [P, 2, 4, 512], F32))

    def vec(c, rows=P):
        return VEC[0:rows, c:c + 1] if isinstance(c, int) else VEC[0:rows, bass.ds(c, 1)]

    def halves(ap):
        return ap.rearrange("p (a t) -> p a t", a=2)

    def banks(s, b, rows=P):
        return PS[0:rows, s, b:b + 2, 0:HT]

    const_in = sem("const_in")
    waits_passed = sem("waits_passed")
    x_in = sem("x_in")
    raw_in = [sem("raw_in_even"), sem("raw_in_odd")]
    rounded = sem("rounded")
    item_split = sem("item_split")
    multiplied = sem("multiplied")
    evacuated = sem("evacuated")
    xhat_hi = sem("xhat_hi")
    xhat_split = sem("xhat_split")
    sq_zero = sem("sq_zero")
    sq_tile = sem("sq_tile")
    sq_added = sem("sq_added")
    sum_sq = sem("sum_sq")
    root = sem("root")
    rstd_ok = sem("rstd_ok")
    gate_scaled = sem("gate_scaled")
    silu_done = sem("silu_done")
    hidden = sem("hidden")
    hidden_hi = sem("hidden_hi")
    hidden_split = sem("hidden_split")
    stored = sem("stored")
    stage_end = sem("stage_end")
    CREDIT = 2

    def barrier(eng, count):
        eng.drain().then_inc(stage_end, 1)
        eng.wait_ge(stage_end, 4 * count)

    block = ctx.enter_context(nc.Block())

    def load_items(sp, first, count, blocks, peel=0):
        for n in range(first, first + peel):
            sp.dma_start(RAW[n % 2][:, 0:blocks * P], a["w"][n, :, 0:blocks * P]).then_inc(raw_in[n % 2], 16)
        first, count = first + peel, count - peel
        if count >= 2:
            with sp.Fori(0, count // 2) as pair:
                i = pair * 2
                for u in range(2):
                    n = first + u
                    sp.wait_ge(item_split, n - 1 + i)
                    sp.dma_start(RAW[n % 2][:, 0:blocks * P].rearrange("p (o c) -> p o c", o=1),
                                 a["w"][bass.ds(n + i, 1), :, 0:blocks * P].rearrange("o p c -> p o c")).then_inc(raw_in[n % 2], 16)
        if count % 2:
            n = first + count - 1
            sp.wait_ge(item_split, n - 1)
            sp.dma_start(RAW[n % 2][:, 0:blocks * P], a["w"][n, :, 0:blocks * P]).then_inc(raw_in[n % 2], 16)

    def round_item(act, n, i=0):
        act.wait_ge(raw_in[n % 2], 16 * (n // 2 + 1) + 8 * i)
        if n >= 2:
            act.wait_ge(multiplied, n - 1 + i)
        act.activation(WH[n % 2][:], RAW[n % 2][:], ACT.Copy).then_inc(rounded, 1)

    def split_item(dve, n, i=0):
        dve.wait_ge(rounded, n + 1 + i)
        dve.tensor_tensor(WL[n % 2][:], RAW[n % 2][:], WH[n % 2][:].bitcast(F32), ALU.subtract).then_inc(item_split, 1)

    def multiply_item(pe, n, i, k_tiles, tiles, hi, lo, before=lambda k: None, cols=P):
        s = n % 2
        pe.wait_ge(item_split, n + 1 + i)
        pe.wait_ge(evacuated, n - 1 + CREDIT + i)
        for t in range(tiles):
            for k in range(k_tiles):
                if t == 0:
                    before(k)
                c = (t * k_tiles + k) * P
                for p, (w, x) in enumerate(((WH, hi), (WH, lo), (WL, hi))):
                    for half in range(2):
                        mm = pe.matmul(PS[:, s, 2 * t + half, 0:HT], w[s][:, c:c + P],
                                       x[:, k, half * HT:(half + 1) * HT],
                                       start=(k == 0 and p == 0), stop=(k == k_tiles - 1 and p == 2))
        mm.then_inc(multiplied, 1)

    def xhat_tile(act, dve, norm, d):
        j = 8 * XHAT_OF_NORM[norm] + d + 1
        g = vec(d + V_G[norm])
        one = slice(d, d + 1) if isinstance(d, int) else bass.ds(d, 1)
        if act is not None:
            act.activation(XH[:, one, :], X[:, one, :], ACT.Copy, scale=g).then_inc(xhat_hi, 1)
        if dve is not None:
            dve.wait_ge(xhat_hi, j)
            dve.scalar_tensor_tensor(out=XL[:, one, :], in0=X[:, one, :], scalar=g, in1=XH[:, one, :].bitcast(F32),
                                     op0=ALU.mult, op1=ALU.subtract).then_inc(xhat_split, 1)

    def square_tile(pool, norm, d):
        one = slice(d, d + 1) if isinstance(d, int) else bass.ds(d, 1)
        x = X[:, one, :].rearrange("p o t -> p (o t)")
        pool.wait_ge(sq_added, 8 * norm + d)
        pool.tensor_tensor(SQT[:], x, x, ALU.mult).then_inc(sq_tile, 1)
        pool.wait_ge(sq_tile, 8 * norm + d + 1)
        pool.tensor_tensor(SQACC[:], SQACC[:], SQT[:], ALU.add).then_inc(sq_added, 1)

    def zero_squares(pool, norm):
        if norm:
            pool.wait_ge(sum_sq, norm)
        pool.memset(SQACC[:], 0.0).then_inc(sq_zero, 1)
        pool.wait_ge(sq_zero, norm + 1)

    def norm_sums(pe, norm, s):
        pe.wait_ge(sq_added, 8 * (norm + 1))
        for half in range(2):
            mm = pe.matmul(PS[:, s, 2 + half, 0:HT], ONES, SQACC[:, half * HT:(half + 1) * HT], start=True, stop=True)
        mm.then_inc(sum_sq, 1)

    def norm_root(act, norm, s):
        act.wait_ge(sum_sq, norm + 1)
        act.activation(halves(RSTD[:]), banks(s, 2), ACT.Sqrt, bias=vec(V_EPS), scale=1.0 / D).then_inc(root, 1)

    def norm_rstd(dve, norm):
        dve.wait_ge(root, norm + 1)
        dve.reciprocal(RSTD[:], RSTD[:]).then_inc(rstd_ok, 1)

    def hidden_steps(f):
        n, j = I_FFN[f], FT * f
        for cnt in PARTS:
            yield n, cnt, j
            n, j = n + cnt + KD, j + cnt

    def ffn_sp(sp, f):
        for n, cnt, _ in hidden_steps(f):
            load_items(sp, n, cnt, 16, peel=2 if n == 0 else 0)
            load_items(sp, n + cnt, KD, cnt)

    def ffn_pe(pe, f):
        norm = NORM_OF_FFN[f]
        base = 8 * XHAT_OF_NORM[norm]
        norm_sums(pe, norm, (I_FFN[f] + 1) % 2)
        for n, cnt, j in hidden_steps(f):
            with pe.Fori(0, cnt // 2) as pair:
                i = pair * 2
                for u in range(2):
                    if u:
                        pe.wait_ge(root, norm + 1)
                    multiply_item(pe, n + u, i, KD, 2, XH, XL,
                                  before=lambda k: pe.wait_ge(xhat_split, base + k + 1))
            with pe.Fori(0, KD // 2) as pair:
                i = pair * 2
                for u in range(2):
                    multiply_item(pe, n + cnt + u, i, cnt, 1, HH, HL,
                                  before=lambda k: pe.wait_ge(hidden_split, j + k + 1))

    def ffn_act(act, f, next_norm, last=False):
        norm_root(act, NORM_OF_FFN[f], (I_FFN[f] + 1) % 2)
        for part, (n, cnt, j) in enumerate(hidden_steps(f)):
            with act.Fori(0, cnt // 2) as pair:
                i = pair * 2
                for u in range(2):
                    round_item(act, n + u + 1, i)
                    act.wait_ge(gate_scaled, j + u + 1 + i)
                    act.activation(T4[:], T1[:], ACT.Silu).then_inc(silu_done, 1)
                    act.wait_ge(hidden, j + u + 1 + i)
                    act.activation(HH[:, bass.ds(i + u, 1), :].rearrange("p o t -> p (o t)"), T3[:], ACT.Copy).then_inc(hidden_hi, 1)
            n += cnt
            final = part == 1
            end = KD - 2 if final and last else KD
            with act.Fori(0, end // 2) as pair:
                i = pair * 2
                for u in range(2):
                    round_item(act, n + u + 1, i)
                    if final and next_norm is not None and next_norm in XHAT_OF_NORM:
                        act.wait_ge(evacuated, n + u + 1 + CREDIT + i)
                        xhat_tile(act, None, next_norm, i + u)
            if final and last:
                round_item(act, n + KD - 1)

    def ffn_dve(dve, f, next_norm, last=False):
        norm_rstd(dve, NORM_OF_FFN[f])
        dve.wait_ge(rstd_ok, NORM_OF_FFN[f] + 1)
        for part, (n, cnt, j) in enumerate(hidden_steps(f)):
            with dve.Fori(0, cnt // 2) as pair:
                i = pair * 2
                for u in range(2):
                    s = (n + u) % 2
                    split_item(dve, n + u + 1, i)
                    dve.wait_ge(multiplied, n + u + 1 + i)
                    dve.tensor_tensor(halves(T1[:]), banks(s, 0), halves(RSTD[:]), ALU.mult).then_inc(gate_scaled, 1)
                    dve.tensor_tensor(halves(T2[:]), banks(s, 2), halves(RSTD[:]), ALU.mult).then_inc(evacuated, 1)
                    dve.wait_ge(silu_done, j + u + 1 + i)
                    dve.wait_ge(evacuated, n + u + 1 + CREDIT + i)
                    dve.tensor_tensor(T3[:], T4[:], T2[:], ALU.mult).then_inc(hidden, 1)
                    dve.wait_ge(hidden_hi, j + u + 1 + i)
                    dve.tensor_tensor(HL[:, bass.ds(i + u, 1), :].rearrange("p o t -> p (o t)"), T3[:],
                                      HH[:, bass.ds(i + u, 1), :].rearrange("p o t -> p (o t)").bitcast(F32),
                                      ALU.subtract).then_inc(hidden_split, 1)
            n += cnt
            final = part == 1

            def down(u, i, more=True):
                s = (n + u) % 2
                if more:
                    split_item(dve, n + u + 1, i)
                dve.wait_ge(multiplied, n + u + 1 + i)
                x = X[:, bass.ds(i + u, 1), :] if not isinstance(i, int) else X[:, i + u:i + u + 1, :]
                x = x.rearrange("p o (a t) -> p (o a) t", a=2)
                dve.scalar_tensor_tensor(out=x, in0=banks(s, 0), scalar=0.5, in1=x,
                                         op0=ALU.mult, op1=ALU.add).then_inc(evacuated, 1)
                if final and next_norm is not None and next_norm in XHAT_OF_NORM:
                    xhat_tile(None, dve, next_norm, i + u)

            end = KD - 2 if final and last else KD
            with dve.Fori(0, end // 2) as pair:
                i = pair * 2
                for u in range(2):
                    down(u, i)
            if final and last:
                down(0, KD - 2)
                down(1, KD - 2, more=False)

    def norm_pool(pool, norm, first_item, tiles=1):
        zero_squares(pool, norm)
        with pool.Fori(0, KD // tiles, 1) as i:
            pool.wait_ge(evacuated, first_item + 1 + CREDIT + i)
            for u in range(tiles):
                square_tile(pool, norm, i * tiles + u)

    KC = m.at("KC", A0, [KV_T, T])
    CH_ = m.at("CH_", A0 + 1152, [KV_T, T], F32R)
    CL_ = m.at("CL_", A0 + 2304, [KV_T, T], F32R)
    KR = m.at("KR", A0 + 3456, [T])
    QN = m.at("QN", A0 + 4032, [H, T])
    QR = m.at("QR", A0 + 8640, [H, T])
    LAT = m.at("LAT", A0 + 13248, [6, T])
    CQH = m.at("CQH", A0 + 16704, [QR_T, T], F32R)
    CQL = m.at("CQL", A0 + 18432, [QR_T, T], F32R)
    SQL = m.at("SQL", A0 + 16704, [5, T])
    TAB = m.at("TAB", A0 + 20160, [T])
    B0 = A0 + 13248
    QS = m.at("QS", B0, [T])
    QSR = m.at("QSR", B0 + 576, [T])
    KS = m.at("KS", B0 + 1152, [SEQ])
    KSR = m.at("KSR", B0 + 1664, [SEQ])
    WKH = m.at("WKH", B0 + 2176, [KV_T, P], F32R)
    WKL = m.at("WKL", B0 + 2432, [KV_T, P], F32R)
    VS = m.at("VS", B0 + 2688, [4, P])
    UKT = m.at("UKT", B0 + 3200, [KV])
    PB = m.at("PB", B0 + 3456, [4, SEQ])
    PT = m.at("PT", B0 + 5504, [4, SEQ])
    QA = m.at("QA", B0 + 7552, [KV_T, SB, H, SQ])
    QRS = m.at("QRS", B0 + 8576, [SB, H, SQ])
    CAUSAL = m.at("CAUSAL", 28416 + 128, [P])
    QG = m.at("QG", 28416, [NS])
    SMALL = m.at("SMALL", 30760, [40])
    NMAX, RSUM = SMALL[:, 0:4], SMALL[:, 4:8]
    CN = m.at("CN", A0 + 4032, [KV])
    SNEW = m.at("SNEW", A0 + 4288, [SB, H, SQ])
    QH = m.at("QH", A0 + 4800, [3, SB, H * SQ], F32R)
    QL = m.at("QL", A0 + 6336, [3, SB, H * SQ], F32R)
    SQH = [m.at(f"SQH{s}", 28992 + 192 * s, [3, H * SQ], F32R) for s in range(2)]
    SQL_ = [m.at(f"SQL{s}", 29696 + 192 * s, [3, H * SQ], F32R) for s in range(2)]
    ROWS = [m.at(f"ROWS{s}", A0 + 7872 + 5120 * s, [PAGES, KV + ROPE]) for s in range(2)]
    CTH = [m.at(f"CTH{s}", A0 + 18112 + 384 * s, [3 * P], F32R) for s in range(2)]
    CTL = [m.at(f"CTL{s}", A0 + 18880 + 384 * s, [3 * P], F32R) for s in range(2)]
    SC = [m.at(f"SC{s}", A0 + 19648 + 1088 * s, [PAGES + 1, H * SQ]) for s in range(2)]
    SQ2 = m.at("SQ2", 26688, [2, 512])
    SS = [m.at(f"SS{s}", 27840 + 128 * s, [PAGES, H]) for s in range(2)]
    KSS = [m.at(f"KSS{s}", 28096 + 16 * s, [PAGES]) for s in range(2)]
    MXP = m.at("MXP", 28128, [H * SQ])
    MXC = m.at("MXC", 28192, [8])
    DG = m.at("DG", 28200, [H * SQ])
    PSUMS = m.at("PSUMS", 28264, [H * SQ])
    RDEN = m.at("RDEN", 28328, [H * SQ])
    QZT = m.at("QZT", 28416, [SB * H * SQ])
    SSN = m.at("SSN", 29384, [8])
    OL = m.at("OL", A0, [KV_T, H, SB, SQ])
    OLH = m.at("OLH", A0 + 1152, [KV_T, H * NS], F32R)
    OLL = m.at("OLL", A0 + 2304, [KV_T, H * NS], F32R)

    lat_ok = stage_sem("attention", "lat_ok")
    lat_sq = stage_sem("attention", "lat_sq")
    lat_sums = stage_sem("attention", "lat_sums")
    lat_root = stage_sem("attention", "lat_root")
    lat_rs = stage_sem("attention", "lat_rs")
    lat_norm = stage_sem("attention", "lat_norm")
    lat_hi = stage_sem("attention", "lat_hi")
    lat_split = stage_sem("attention", "lat_split")
    tab_in = stage_sem("attention", "tab_in")
    kr_tab = stage_sem("attention", "kr_tab")
    kr_fold = stage_sem("attention", "kr_fold")
    kr_ok = stage_sem("attention", "kr_ok")
    uv_ok = stage_sem("attention", "uv_ok")
    causal_in = stage_sem("attention", "causal_in")
    kr_sq = stage_sem("attention", "kr_sq")
    slices = stage_sem("attention", "slices")
    ukt_in = stage_sem("attention", "ukt_in")
    q_fold = stage_sem("attention", "q_fold")
    q_rope = stage_sem("attention", "q_rope")
    q_sq = stage_sem("attention", "q_sq")
    q_sums = stage_sem("attention", "q_sums")
    q_root = stage_sem("attention", "q_root")
    q_rs = stage_sem("attention", "q_rs")
    q_ok = stage_sem("attention", "q_ok")
    q_gain = stage_sem("attention", "q_gain")
    qa_mm = stage_sem("attention", "qa_mm")
    qa_ok = stage_sem("attention", "qa_ok")
    k_mm = stage_sem("attention", "k_mm")
    k_sq = stage_sem("attention", "k_sq")
    k_sums = stage_sem("attention", "k_sums")
    k_root = stage_sem("attention", "k_root")
    k_rs = stage_sem("attention", "k_rs")
    k_ok = stage_sem("attention", "k_ok")
    v_mm = stage_sem("attention", "v_mm")
    v_ok = stage_sem("attention", "v_ok")
    s_mm = stage_sem("attention", "s_mm")
    s_mask = stage_sem("attention", "s_mask")
    s_max = stage_sem("attention", "s_max")
    s_neg = stage_sem("attention", "s_neg")
    p_exp = stage_sem("attention", "p_exp")
    p_inv = stage_sem("attention", "p_inv")
    p_ok = stage_sem("attention", "p_ok")
    p_t = stage_sem("attention", "p_t")
    pt_act = stage_sem("attention", "pt_act")
    pt_dve = stage_sem("attention", "pt_dve")
    o_mm = stage_sem("attention", "o_mm")
    o_hi = stage_sem("attention", "o_hi")
    o_split = stage_sem("attention", "o_split")
    uk_, uv_ = I_UK % 2, I_UV % 2
    UKH, UKL = WH[uk_], WL[uk_]
    UVH, UVL = WH[uv_], WL[uv_]

    def bank(b, rows=slice(0, P)):
        return PS[rows, b // 4, b % 4, :]

    def lat_sp(sp):
        load_items(sp, I_LAT, 3, 16)
        sp.wait_ge(evacuated, I_LAT + CREDIT)
        sp.dma_start(TAB[:], a["rope"]).then_inc(tab_in, 16)
        load_items(sp, I_UQ, H, 6)
        load_items(sp, I_UK, 2, 16)

    def lat_pe(pe):
        norm_sums(pe, 1, (I_LAT + 1) % 2)
        for u in range(3):
            if u:
                pe.wait_ge(root, 2)
            multiply_item(pe, I_LAT + u, 0, KD, 2, XH, XL, before=lambda k: pe.wait_ge(xhat_split, 8 + k + 1))
        pe.wait_ge(evacuated, I_UQ + CREDIT)
        pe.wait_ge(lat_sq, 5)
        for half in range(2):
            for t in range(5):
                mm = pe.matmul(PS[:, 0, (0 if t < QR_T else 2) + half, 0:HT], ONES, SQL[:, t, half * HT:(half + 1) * HT],
                               start=t in (0, QR_T), stop=t in (QR_T - 1, 4))
        mm.then_inc(lat_sums, 1)
        pe.wait_ge(kr_tab, 1)
        for half in range(2):
            mm = pe.matmul(PS[0:64, 1, half, 0:HT], FOLD, T3[:, half * HT:(half + 1) * HT], start=True, stop=True)
        mm.then_inc(kr_fold, 1)
        pe.wait_ge(kr_ok, 1)
        with pe.Fori(0, H // 2) as pair:
            i = pair * 2
            for u in range(2):
                multiply_item(pe, I_UQ + u, i, QR_T, 2, CQH, CQL, before=lambda k: pe.wait_ge(lat_split, k + 1))

    def lat_act(act):
        norm_root(act, 1, (I_LAT + 1) % 2)
        for u in range(3):
            round_item(act, I_LAT + u + 1)
            for t in range(2 * u, min(2 * u + 2, 5)):
                act.wait_ge(lat_ok, t + 1)
                act.activation(SQL[:, t, :], LAT[:, t, :], ACT.Square).then_inc(lat_sq, 1)
        act.wait_ge(lat_sums, 1)
        act.activation(halves(T1[:]), banks(0, 0), ACT.Sqrt, bias=vec(V_EPS), scale=1.0 / (QR_T * P)).then_inc(lat_root, 1)
        act.activation(halves(T2[:]), banks(0, 2), ACT.Sqrt, bias=vec(V_EPS), scale=1.0 / KV).then_inc(lat_root, 1)
        act.wait_ge(kr_fold, 1)
        act.activation(halves(KR[0:64, :]), banks(1, 0, 64), ACT.Copy).then_inc(kr_ok, 1)
        for t in range(5):
            act.wait_ge(lat_norm, t + 1)
            if t < QR_T:
                act.activation(CQH[:, t, :], T3[:] if t % 2 == 0 else T4[:], ACT.Copy).then_inc(lat_hi, 1)
            else:
                act.activation(CH_[:, t - QR_T, :], KC[:, t - QR_T, :], ACT.Copy).then_inc(lat_hi, 1)
        with act.Fori(0, H // 2) as pair:
            i = pair * 2
            for u in range(2):
                round_item(act, I_UQ + u + 1, i)
        round_item(act, I_UV)

    def lat_dve(dve):
        norm_rstd(dve, 1)
        dve.wait_ge(rstd_ok, 2)
        for u in range(3):
            split_item(dve, I_LAT + u + 1)
            dve.wait_ge(multiplied, I_LAT + u + 1)
            s = (I_LAT + u) % 2
            dve.tensor_tensor(halves(LAT[:, 2 * u, :]), banks(s, 0), halves(RSTD[:]), ALU.mult).then_inc(lat_ok, 1)
            dve.tensor_tensor(halves(LAT[:, 2 * u + 1, :]), banks(s, 2), halves(RSTD[:]), ALU.mult).then_inc(lat_ok, 1)
            dve.wait_ge(lat_ok, 2 * u + 2)
            dve.sem_inc(evacuated, 1)
        dve.wait_ge(tab_in, 16)
        dve.tensor_tensor(T3[:], LAT[:, 5, :], TAB[:], ALU.mult).then_inc(kr_tab, 1)
        for n, t in enumerate((T1, T2)):
            dve.wait_ge(lat_root, n + 1)
            dve.reciprocal(t[:], t[:]).then_inc(lat_rs, 1)
        dve.wait_ge(lat_rs, 2)
        dve.wait_ge(kr_fold, 1)
        for t in range(5):
            f = (T3 if t % 2 == 0 else T4)[:] if t < QR_T else KC[:, t - QR_T, :]
            if t == 2:
                dve.wait_ge(lat_split, 1)
            dve.scalar_tensor_tensor(out=f, in0=LAT[:, t, :], scalar=vec(V_GQL + t), in1=(T1 if t < QR_T else T2)[:],
                                     op0=ALU.mult, op1=ALU.mult).then_inc(lat_norm, 1)
            dve.wait_ge(lat_hi, t + 1)
            hi, lo = (CQH, CQL) if t < QR_T else (CH_, CL_)
            k = t if t < QR_T else t - QR_T
            dve.tensor_tensor(lo[:, k, :], f, hi[:, k, :].bitcast(F32), ALU.subtract).then_inc(lat_split, 1)
        with dve.Fori(0, H // 2) as pair:
            i = pair * 2
            for u in range(2):
                n = I_UQ + u
                split_item(dve, n + 1, i)
                dve.wait_ge(multiplied, n + 1 + i)
                one = bass.ds(i + u, 1)
                dve.tensor_copy(QN[:, one, :].rearrange("p o (a t) -> p (o a) t", a=2), banks(n % 2, 0)).then_inc(qn_ok, 1)
                dve.tensor_tensor(QR[:, one, :].rearrange("p o (a t) -> p (o a) t", a=2), banks(n % 2, 2),
                                  halves(TAB[:]), ALU.mult).then_inc(evacuated, 1)
        split_item(dve, I_UV)

    qn_ok = stage_sem("attention", "qn_ok")

    def heads_sp(sp):
        sp.dma_start(o["lat"], KC[:]).then_inc(stored, 16)
        sp.dma_start(o["kr"], KR[0:64, :]).then_inc(stored, 16)
        sp.dma_start(CAUSAL[:], a["causal"]).then_inc(causal_in, 16)
        with sp.Fori(0, H) as h:
            sp.wait_ge(qa_mm, h)
            sp.dma_start(UKT[:].rearrange("p (o r) -> p o r", o=1), a["ukt"][:, bass.ds(h, 1), :]).then_inc(ukt_in, 16)

    def heads_pool(pool):
        with pool.Fori(0, H) as h:
            pool.wait_ge(k_mm, h)
            for src, dst in ((UKH, WKH), (UKL, WKL)):
                pool.tensor_copy(dst[:], src[:].rearrange("p (k h d) -> p k h d", k=KV_T, h=H)[:, :, bass.ds(h, 1), :]
                                 .rearrange("p k o d -> p k (o d)").bitcast(F32)).then_inc(slices, 1)

    def heads_pe(pe):
        with pe.Fori(0, H) as h:
            one = bass.ds(h, 1)
            pe.wait_ge(pt_act, h * 2)
            pe.wait_ge(pt_dve, h * 2)
            for half in range(2):
                mm = pe.matmul(PS[0:64, 0, half, 0:HT], FOLD, QR[:, one, half * HT:(half + 1) * HT].rearrange("p o t -> p (o t)"),
                               start=True, stop=True)
            mm.then_inc(q_fold, 1)
            pe.wait_ge(slices, h * 2 + 2)
            n = 0
            for k in range(KV_T):
                for w, x in ((WKH, CH_), (WKH, CL_), (WKL, CH_)):
                    mm = pe.matmul(bank(4), w[:, k, :], x[:, k, 0:SEQ], start=n == 0, stop=n == 5)
                    n += 1
            mm.then_inc(k_mm, 1)
            for t in range(4):
                n = 0
                for k in range(KV_T):
                    for x, w in ((CH_, UVH), (CH_, UVL), (CL_, UVH)):
                        rhs = w[:].rearrange("p (k h d) -> p k h d", k=KV_T, h=H)[:, k, one, :].rearrange("p o d -> p (o d)")
                        mm = pe.matmul(bank(6)[:, t * P:(t + 1) * P], x[:, k, t * P:(t + 1) * P], rhs, start=n == 0, stop=n == 5)
                        n += 1
            mm.then_inc(v_mm, 1)
            pe.wait_ge(q_sq, h * 2 + 2)
            for half in range(2):
                w = slice(half * HT, (half + 1) * HT)
                pe.matmul(PS[:, 0, 2 + half, 0:HT], ONES, T1[:, w], start=True, stop=False)
                mm = pe.matmul(PS[:, 0, 2 + half, 0:HT], ONES[0:64, :], T2[0:64, w], start=False, stop=True)
            mm.then_inc(q_sums, 1)
            pe.wait_ge(k_sq, h + 1)
            pe.wait_ge(o_split, h)
            pe.matmul(bank(5), ONES, T1[:, 0:SEQ], start=True, stop=False)
            pe.matmul(bank(5), ONES[0:64, :], SQT[0:64, 0:SEQ], start=False, stop=True).then_inc(k_sums, 1)
            pe.wait_ge(q_gain, h * 2 + 2)
            pe.wait_ge(ukt_in, h * 16 + 16)
            for k in range(KV_T):
                mm = pe.matmul(bank(7)[:, k * NS:(k + 1) * NS], UKT[:, k * P:(k + 1) * P], QG[:], start=True, stop=True)
            mm.then_inc(qa_mm, 1)
            pe.wait_ge(k_ok, h * 2 + 2)
            pe.wait_ge(v_ok, h + 1)
            pe.wait_ge(qa_ok, h + 1)
            for b in range(4):
                q, n = slice(b * P, (b + 1) * P), (b + 1) * P
                pe.matmul(bank(4 + b)[:, 0:n], QS[:, q], KS[:, 0:n], start=True, stop=False)
                pe.matmul(bank(4 + b)[:, 0:n], QSR[0:64, q], KSR[0:64, 0:n], start=False, stop=True).then_inc(s_mm, 1)
            for b in range(4):
                pe.wait_ge(p_ok, h * 4 + b + 1)
                for k in range(b + 1):
                    mm = pe.transpose(bank(k)[:, b * P:(b + 1) * P], PB[:, b, k * P:(k + 1) * P], IDENT)
                mm.then_inc(p_t, 1)
            pe.wait_ge(pt_act, h * 2 + 2)
            pe.wait_ge(pt_dve, h * 2 + 2)
            for k in range(4):
                mm = pe.matmul(bank(5)[:, k * P:SEQ], VS[:, k, :], PT[:, k, k * P:SEQ], start=k == 0, stop=k == 3)
            mm.then_inc(o_mm, 1)

    def heads_act(act):
        act.activation(SQT[0:64, 0:SEQ], KR[0:64, 0:SEQ], ACT.Square).then_inc(kr_sq, 1)
        act.wait_ge(kr_sq, 1)
        with act.Fori(0, H) as h:
            one = bass.ds(h, 1)
            act.activation(T1[:], QN[:, one, :].rearrange("p o t -> p (o t)"), ACT.Square).then_inc(q_sq, 1)
            act.wait_ge(q_fold, h + 1)
            act.activation(halves(QSR[0:64, :]), banks(0, 0, 64), ACT.Copy).then_inc(q_rope, 1)
            act.activation(halves(T2[0:64, :]), banks(0, 0, 64), ACT.Square).then_inc(q_sq, 1)
            act.wait_ge(v_mm, h + 1)
            act.activation(VS[:].rearrange("p b d -> p (b d)"), bank(6), ACT.Copy).then_inc(v_ok, 1)
            act.wait_ge(q_sums, h + 1)
            act.activation(T1[:, 0:SEQ], bank(4), ACT.Square).then_inc(k_sq, 1)
            act.activation(halves(T3[:]), banks(0, 2), ACT.Sqrt, bias=vec(V_EPS), scale=1.0 / QK).then_inc(q_root, 1)
            act.wait_ge(k_sums, h + 1)
            act.activation(T2[:, 0:SEQ], bank(5), ACT.Sqrt, bias=vec(V_EPS), scale=1.0 / QK).then_inc(k_root, 1)
            act.wait_ge(qa_mm, h + 1)
            for k in range(KV_T):
                act.activation(QA[:, k, :, one, :].rearrange("p s o q -> p s (o q)"),
                               bank(7)[:, k * NS:(k + 1) * NS].rearrange("p (s q) -> p s q", s=SB), ACT.Copy).then_inc(qa_half, 1)
            act.wait_ge(qa_half, h * 2 + 2)
            act.sem_inc(qa_ok, 1)
            for b in range(4):
                act.wait_ge(s_neg, h * 4 + b + 1)
                n = (b + 1) * P
                act.activation(PB[:, b, 0:n], bank(4 + b)[:, 0:n], ACT.Exp, bias=NMAX[:, b:b + 1], scale=SCALE,
                               accum_out=RSUM[:, b:b + 1]).then_inc(p_exp, 1)
            act.wait_ge(p_t, h * 4 + 4)
            for k in range(2):
                act.activation(PT[:, k, k * P:SEQ], bank(k)[:, k * P:SEQ], ACT.Copy).then_inc(pt_act, 1)
            act.wait_ge(o_mm, h + 1)
            act.activation(XH[:, one, 0:SEQ].rearrange("p o t -> p (o t)"), bank(5), ACT.Copy).then_inc(o_hi, 1)

    qa_half = stage_sem("attention", "qa_half")

    def heads_dve(dve):
        dve.wait_ge(causal_in, 16)
        with dve.Fori(0, H) as h:
            one = bass.ds(h, 1)
            dve.wait_ge(q_root, h + 1)
            dve.reciprocal(T3[:], T3[:]).then_inc(q_rs, 1)
            dve.wait_ge(q_rs, h + 1)
            dve.scalar_tensor_tensor(out=QS[:], in0=QN[:, one, :].rearrange("p o t -> p (o t)"), scalar=vec(V_GQN), in1=T3[:],
                                     op0=ALU.mult, op1=ALU.mult).then_inc(q_ok, 1)
            dve.wait_ge(q_rope, h + 1)
            dve.scalar_tensor_tensor(out=QSR[0:64, :], in0=QSR[0:64, :], scalar=vec(V_GQR, 64), in1=T3[0:64, :],
                                     op0=ALU.mult, op1=ALU.mult).then_inc(q_ok, 1)
            dve.wait_ge(q_ok, h * 2 + 2)
            dve.tensor_scalar(QG[:], QS[:, SEQ:T], vec(V_GKN), None, ALU.mult).then_inc(q_gain, 1)
            dve.tensor_scalar(QRS[0:64, :, one, :].rearrange("p s o q -> p s (o q)"),
                              QSR[0:64, SEQ:T].rearrange("p (s q) -> p s q", s=SB), vec(V_GKR, 64), None, ALU.mult).then_inc(q_gain, 1)
            dve.wait_ge(k_root, h + 1)
            dve.reciprocal(T2[:, 0:SEQ], T2[:, 0:SEQ]).then_inc(k_rs, 1)
            dve.wait_ge(k_rs, h + 1)
            dve.scalar_tensor_tensor(out=KS[:], in0=bank(4), scalar=vec(V_GKN), in1=T2[:, 0:SEQ],
                                     op0=ALU.mult, op1=ALU.mult).then_inc(k_ok, 1)
            dve.scalar_tensor_tensor(out=KSR[0:64, :], in0=KR[0:64, 0:SEQ], scalar=vec(V_GKR, 64), in1=T2[0:64, 0:SEQ],
                                     op0=ALU.mult, op1=ALU.mult).then_inc(k_ok, 1)
            for b in range(4):
                c = 4 * 0 + b
                dve.wait_ge(s_mm, h * 4 + b + 1)
                dve.tensor_tensor(bank(4 + b)[:, b * P:(b + 1) * P], bank(4 + b)[:, b * P:(b + 1) * P], CAUSAL[:], ALU.add).then_inc(s_mask, 1)
                dve.wait_ge(s_mask, h * 4 + b + 1)
                dve.tensor_reduce(NMAX[:, c:c + 1], bank(4 + b)[:, 0:(b + 1) * P], AX.X, ALU.max, negate=True).then_inc(s_max, 1)
                dve.wait_ge(s_max, h * 4 + b + 1)
                dve.tensor_scalar(NMAX[:, c:c + 1], NMAX[:, c:c + 1], SCALE, None, ALU.mult).then_inc(s_neg, 1)
            for b in range(4):
                dve.wait_ge(p_exp, h * 4 + b + 1)
                dve.reciprocal(RSUM[:, b:b + 1], RSUM[:, b:b + 1]).then_inc(p_inv, 1)
                dve.wait_ge(p_inv, h * 4 + b + 1)
                dve.tensor_scalar(PB[:, b, 0:(b + 1) * P], PB[:, b, 0:(b + 1) * P], RSUM[:, b:b + 1], None, ALU.mult).then_inc(p_ok, 1)
            dve.wait_ge(p_t, h * 4 + 4)
            for k in range(2, 4):
                dve.tensor_copy(PT[:, k, k * P:SEQ], bank(k)[:, k * P:SEQ]).then_inc(pt_dve, 1)
            dve.wait_ge(o_hi, h + 1)
            dve.tensor_tensor(XL[:, one, 0:SEQ].rearrange("p o t -> p (o t)"), bank(5),
                              XH[:, one, 0:SEQ].rearrange("p o t -> p (o t)").bitcast(F32), ALU.subtract).then_inc(o_split, 1)

    PAGES_SB = m.at("PAGES_SB", 29568, [SB * PAGES], I32)
    newmask_in = stage_sem("attention", "newmask_in")
    qz_shift = stage_sem("attention", "qz_shift")
    qz_hi = stage_sem("attention", "qz_hi")
    qz_zero = stage_sem("attention", "qz_zero")
    qz_split = stage_sem("attention", "qz_split")
    new_mm = stage_sem("attention", "new_mm")
    new_t = stage_sem("attention", "new_t")
    new_sq = stage_sem("attention", "new_sq")
    new_copy = stage_sem("attention", "new_copy")
    new_ss = stage_sem("attention", "new_ss")
    new_root = stage_sem("attention", "new_root")
    new_rs = stage_sem("attention", "new_rs")
    new_scaled = stage_sem("attention", "new_scaled")
    new_ok = stage_sem("attention", "new_ok")
    rows_in = [stage_sem("attention", "rows_in_even"), stage_sem("attention", "rows_in_odd")]
    row_t = stage_sem("attention", "row_t")
    row_hi = stage_sem("attention", "row_hi")
    row_lo = stage_sem("attention", "row_lo")
    keys_mm = stage_sem("attention", "keys_mm")
    keys_sq = stage_sem("attention", "keys_sq")
    keys_ss = stage_sem("attention", "keys_ss")
    scores_mm = stage_sem("attention", "scores_mm")
    rope_sq = stage_sem("attention", "rope_sq")
    rope_ss = stage_sem("attention", "rope_ss")
    seq_ss = stage_sem("attention", "seq_ss")
    seq_root = stage_sem("attention", "seq_root")
    seq_rs = stage_sem("attention", "seq_rs")
    seq_scaled = stage_sem("attention", "seq_scaled")
    seq_new = stage_sem("attention", "seq_new")
    seq_max = stage_sem("attention", "seq_max")
    seq_max_t = stage_sem("attention", "seq_max_t")
    seq_max_c = stage_sem("attention", "seq_max_c")
    seq_diag = stage_sem("attention", "seq_diag")
    seq_max_b = stage_sem("attention", "seq_max_b")
    seq_less = stage_sem("attention", "seq_less")
    seq_exp = stage_sem("attention", "seq_exp")
    seq_sum = stage_sem("attention", "seq_sum")
    seq_den = stage_sem("attention", "seq_den")
    seq_rden = stage_sem("attention", "seq_rden")
    seq_pv = stage_sem("attention", "seq_pv")
    seq_ol = stage_sem("attention", "seq_ol")
    ol_hi = stage_sem("attention", "ol_hi")
    ol_split = stage_sem("attention", "ol_split")
    out_mm = stage_sem("attention", "out_mm")
    out_hi = stage_sem("attention", "out_hi")
    out_split = stage_sem("attention", "out_split")
    NEW = slice(T - P, T)
    HQ = H * SQ

    def rows_sp(sp, s, i=0, first=False):
        u = s % 2
        if not first:
            sp.wait_ge(seq_pv, s - 1 + i)
        for p in range(PAGES):
            e = s * PAGES + p
            at = PAGES_SB[0:1, e:e + 1] if isinstance(i, int) else PAGES_SB[0:1, bass.ds(i * PAGES + e, 1)]
            page = sp.value_load(at, min_val=0, max_val=POOL - 1)
            sp.dma_start(ROWS[u][:, p:p + 1, 0:KV], a["cache_c"][bass.ds(page, 1), :, :].rearrange("o t r -> t o r")).then_inc(rows_in[u], 16)
            sp.dma_start(ROWS[u][:, p:p + 1, KV:KV + ROPE], a["cache_kr"][bass.ds(page, 1), :, :].rearrange("o t r -> t o r")).then_inc(rows_in[u], 16)

    def samples_sp(sp):
        sp.dma_start(SNEW[:].rearrange("p s h q -> p (s h q)"), a["newmask"]).then_inc(newmask_in, 16)
        sp.dma_start(PAGES_SB[0:1, :], a["pages"].rearrange("o n -> o n")).then_inc(pages_in, 16)
        sp.wait_ge(pages_in, 16)
        rows_sp(sp, 0, first=True)
        rows_sp(sp, 1, first=True)
        with sp.Fori(0, (SB - 2) // 2) as pair:
            for u in range(2):
                rows_sp(sp, 2 + u, pair * 2)

    pages_in = stage_sem("attention", "pages_in")
    seq_q = stage_sem("attention", "seq_q")

    def queries_pool(pool, s, i=0):
        if s >= 2:
            pool.wait_ge(scores_mm, PAGES * (s - 1) + PAGES * i)
        for q, dst in ((QH, SQH), (QL, SQL_)):
            pool.tensor_copy(dst[s % 2][:], q[:, :, bass.ds(i + s, 1), :].rearrange("p k o c -> p k (o c)").bitcast(F32)).then_inc(seq_q, 1)

    def samples_pool(pool):
        pool.wait_ge(new_ok, 1)
        queries_pool(pool, 0)
        queries_pool(pool, 1)
        with pool.Fori(0, (SB - 2) // 2) as pair:
            for u in range(2):
                queries_pool(pool, 2 + u, pair * 2)

    def page_t(pe, s, i, p):
        if p == 0:
            pe.wait_ge(rows_in[s % 2], 32 * PAGES * (s // 2 + 1) + 16 * PAGES * i)
        n = s * PAGES + p
        if n:
            pe.wait_ge(row_lo, n + PAGES * i)
        for k, c in enumerate((0, P, KV + ROPE - P)):
            mm = pe.transpose(bank(4)[:, k * P:(k + 1) * P], ROWS[s % 2][:, p, c:c + P], IDENT)
        mm.then_inc(row_t, 1)

    def page_mm(pe, s, i, p):
        n = s * PAGES + p
        u = p % 2
        pe.wait_ge(row_lo, n + 1 + PAGES * i)
        if n >= 2:
            pe.wait_ge(keys_sq, 2 * (n - 1) + 2 * PAGES * i)
        for half in range(2):
            j = 0
            for k in range(KV_T):
                for x, w in ((CTH, UKH), (CTH, UKL), (CTL, UKH)):
                    mm = pe.matmul(bank(2 * u + half), x[u][:, k * P:(k + 1) * P], w[:, k * 1024 + half * 512:k * 1024 + half * 512 + 512],
                                   start=j == 0, stop=j == 5)
                    j += 1
            mm.then_inc(keys_mm, 1)
        if p == 0 and s:
            pe.wait_ge(seq_scaled, s + i)
        out = bank(6 + p // 8)[:, (p % 8) * HQ:(p % 8 + 1) * HQ]
        if p == 0:
            pe.wait_ge(seq_q, 2 * (s + 1) + 2 * i)
        j = 0
        for k in range(3):
            for x, w in ((CTH, SQH), (CTH, SQL_), (CTL, SQH)):
                mm = pe.matmul(out, x[u][:, k * P:(k + 1) * P], w[s % 2][:, k, :], start=j == 0, stop=j == 8)
                j += 1
        mm.then_inc(scores_mm, 1)

    def finish_pe(pe, step, s, i):
        b = bank(5)
        u = s % 2
        n = s + 1 + i
        if step == 0:
            pe.wait_ge(seq_max, n)
            if s:
                pe.wait_ge(seq_ol, n - 1)
            pe.matmul(b[0:HQ, 0:P], MXP[:], IDENT, start=True, stop=True).then_inc(seq_max_t, 1)
        if step == 1:
            pe.wait_ge(seq_diag, n)
            pe.matmul(b[:, 0:HQ], ONES[0:HQ, :], DG[0:HQ, :], start=True, stop=True).then_inc(seq_max_b, 1)
        if step == 2:
            pe.wait_ge(seq_sum, n)
            pe.matmul(b[:, HQ:2 * HQ], ONES, PSUMS[:], start=True, stop=True).then_inc(seq_den, 1)
            for k in range(KV_T):
                for t in range(PAGES + 1):
                    rows = ROWS[u][:, t, k * P:(k + 1) * P] if t < PAGES else CN[:, k * P:(k + 1) * P]
                    mm = pe.matmul(b[:, (2 + k) * HQ:(3 + k) * HQ], rows, SC[u][:, t, :], start=t == 0, stop=t == PAGES)
            mm.then_inc(seq_pv, 1)

    def page_act(act, s, i, p):
        n = s * PAGES + p
        act.wait_ge(row_t, n + 1 + PAGES * i)
        if n >= 2:
            act.wait_ge(scores_mm, n - 1 + PAGES * i)
        act.activation(CTH[p % 2][:], bank(4)[:, 0:3 * P], ACT.Copy).then_inc(row_hi, 1)

    def squares_act(act, s, i, p):
        n = s * PAGES + p
        for half in range(2):
            act.wait_ge(keys_mm, 2 * n + half + 1 + 2 * PAGES * i)
            if n:
                act.wait_ge(keys_ss, 2 * (n - 1) + half + 1 + 2 * PAGES * i)
            act.activation(SQ2[:, half, :], bank(2 * (p % 2) + half), ACT.Square).then_inc(keys_sq, 1)

    def page_dve(dve, s, i, p):
        n = s * PAGES + p
        dve.wait_ge(row_hi, n + 1 + PAGES * i)
        dve.tensor_tensor(CTL[p % 2][:], bank(4)[:, 0:3 * P], CTH[p % 2][:].bitcast(F32), ALU.subtract).then_inc(row_lo, 1)

    def sums_dve(dve, s, i, p):
        n = s * PAGES + p
        for half in range(2):
            dve.wait_ge(keys_sq, 2 * n + half + 1 + 2 * PAGES * i)
            dve.tensor_reduce(SS[s % 2][:, p, half * 4:half * 4 + 4], SQ2[:, half, :].rearrange("p (h d) -> p h d", h=4),
                              AX.X, ALU.add).then_inc(keys_ss, 1)

    def seq_ss_dve(dve, s, i):
        u, n = s % 2, s + 1 + i
        dve.wait_ge(rope_ss, n)
        dve.wait_ge(keys_ss, 2 * PAGES * (s + 1) + 2 * PAGES * i)
        dve.tensor_tensor(SS[u][:], SS[u][:], KSS[u][:].unsqueeze(2).to_broadcast([P, PAGES, H]), ALU.add).then_inc(seq_ss, 1)

    def scale_dve(dve, s, i):
        u, n = s % 2, s + 1 + i
        dve.wait_ge(seq_root, n)
        dve.reciprocal(SS[u][:], SS[u][:]).then_inc(seq_rs, 1)
        dve.wait_ge(seq_rs, n)
        dve.wait_ge(scores_mm, PAGES * (s + 1) + PAGES * i)
        dve.tensor_tensor(SC[u][:, 0:PAGES, :].rearrange("p t (h q) -> p (t h) q", h=H),
                          PS[:, 1, 2:4, :].rearrange("p b (c q) -> p (b c) q", q=SQ),
                          SS[u][:].rearrange("p t h -> p (t h)").unsqueeze(2).to_broadcast([P, PAGES * H, SQ]), ALU.mult).then_inc(seq_scaled, 1)
        dve.tensor_copy(SC[u][:, PAGES, :].rearrange("p (o c) -> p o c", o=1),
                        SNEW[:].rearrange("p s h q -> p s (h q)")[:, bass.ds(i + s, 1), :]).then_inc(seq_new, 1)
        dve.wait_ge(seq_scaled, n)
        dve.wait_ge(seq_new, n)
        dve.tensor_reduce(MXP[:], SC[u][:].rearrange("p t c -> p c t"), AX.X, ALU.max).then_inc(seq_max, 1)

    def max_dve(dve, s, i):
        n = s + 1 + i
        dve.wait_ge(seq_max_t, n)
        dve.tensor_reduce(MXC[0:HQ, 0:1], bank(5)[0:HQ, 0:P], AX.X, ALU.max).then_inc(seq_max_c, 1)
        dve.wait_ge(seq_max_c, n)
        dve.tensor_scalar(DG[0:HQ, :], IDENT[0:HQ, 0:HQ], MXC[0:HQ, 0:1], None, ALU.mult).then_inc(seq_diag, 1)

    def less_dve(dve, s, i):
        u, n = s % 2, s + 1 + i
        dve.wait_ge(seq_max_b, n)
        dve.tensor_tensor(SC[u][:], SC[u][:], bank(5)[:, 0:HQ].unsqueeze(1).to_broadcast([P, PAGES + 1, HQ]), ALU.subtract).then_inc(seq_less, 1)

    def sum_dve(dve, s, i):
        u, n = s % 2, s + 1 + i
        dve.wait_ge(seq_exp, n)
        dve.tensor_reduce(PSUMS[:], SC[u][:].rearrange("p t c -> p c t"), AX.X, ALU.add).then_inc(seq_sum, 1)

    def ol_dve(dve, s, i):
        n = s + 1 + i
        dve.wait_ge(seq_pv, n)
        dve.reciprocal(RDEN[:], bank(5)[:, HQ:2 * HQ]).then_inc(seq_rden, 1)
        dve.wait_ge(seq_rden, n)
        for k in range(KV_T):
            mm = dve.tensor_tensor(OL[:, k, :, bass.ds(i + s, 1), :].rearrange("p h o q -> p h (o q)"),
                                   bank(5)[:, (2 + k) * HQ:(3 + k) * HQ].rearrange("p (h q) -> p h q", h=H),
                                   RDEN[:].rearrange("p (h q) -> p h q", h=H), ALU.mult)
        mm.then_inc(seq_ol, 1)

    def rope_act(act, s, i):
        u = s % 2
        act.wait_ge(rows_in[u], 32 * PAGES * (s // 2 + 1) + 16 * PAGES * i)
        if s:
            act.wait_ge(keys_ss, 2 * PAGES * s + 2 * PAGES * i)
        act.activation(SQ2[:].rearrange("p a (t d) -> p (a t) d", d=ROPE), ROWS[u][:, :, KV:KV + ROPE], ACT.Square).then_inc(rope_sq, 1)
        act.wait_ge(rope_ss, s + 1 + i)

    def rope_dve(dve, s, i):
        dve.wait_ge(rope_sq, s + 1 + i)
        dve.tensor_reduce(KSS[s % 2][:], SQ2[:].rearrange("p a (t d) -> p (a t) d", d=ROPE), AX.X, ALU.add).then_inc(rope_ss, 1)

    def seq_pe(pe, s, i=0, fin=True):
        page_t(pe, s, i, 0)
        for p in range(PAGES):
            if p < PAGES - 1:
                page_t(pe, s, i, p + 1)
            page_mm(pe, s, i, p)
            if fin and p in (1, 2, 4):
                finish_pe(pe, (1, 2, 4).index(p), s - 1, i)

    def seq_act(act, s, i=0, fin=True):
        u, n = (s - 1) % 2, s + i
        if fin:
            root_act(act, s - 1, i)
        rope_act(act, s, i)
        page_act(act, s, i, 0)
        for p in range(PAGES):
            if p < PAGES - 1:
                page_act(act, s, i, p + 1)
            squares_act(act, s, i, p)
            if fin and p == 3:
                exp_act(act, s - 1, i)

    def root_act(act, s, i):
        act.wait_ge(seq_ss, s + 1 + i)
        act.activation(SS[s % 2][:], SS[s % 2][:], ACT.Sqrt, bias=vec(V_EPS), scale=1.0 / QK).then_inc(seq_root, 1)

    def exp_act(act, s, i):
        act.wait_ge(seq_less, s + 1 + i)
        act.activation(SC[s % 2][:], SC[s % 2][:], ACT.Exp, scale=SCALE).then_inc(seq_exp, 1)

    def seq_dve(dve, s, i=0, fin=True):
        if fin:
            seq_ss_dve(dve, s - 1, i)
        rope_dve(dve, s, i)
        page_dve(dve, s, i, 0)
        if fin:
            scale_dve(dve, s - 1, i)
        for p in range(PAGES):
            if p < PAGES - 1:
                page_dve(dve, s, i, p + 1)
            sums_dve(dve, s, i, p)
            if fin and p == 1:
                max_dve(dve, s - 1, i)
            if fin and p == 2:
                less_dve(dve, s - 1, i)
            if fin and p == 4:
                sum_dve(dve, s - 1, i)
            if fin and p == 6:
                ol_dve(dve, s - 1, i)

    def samples_pe(pe):
        pe.wait_ge(qz_split, 2)
        for half in range(2):
            j = 0
            for k in range(KV_T):
                for x, w in ((CH_, UKH), (CH_, UKL), (CL_, UKH)):
                    pe.matmul(bank(half), x[:, k, NEW], w[:, k * 1024 + half * 512:k * 1024 + half * 512 + 512], start=j == 0, stop=j == 5)
                    j += 1
        j = 0
        for k in range(KV_T):
            for x, w in ((CH_, QH), (CH_, QL), (CL_, QH)):
                pe.matmul(bank(2), x[:, k, NEW], w[:, k].rearrange("p s c -> p (s c)"), start=j == 0, stop=False)
                j += 1
        pe.matmul(bank(2), KR[0:64, NEW], QRS[0:64].rearrange("p s h q -> p (s h q)"), start=False, stop=True).then_inc(new_mm, 1)
        for k in range(KV_T):
            pe.transpose(bank(3)[:, k * P:(k + 1) * P], KC[:, k, NEW], IDENT)
        pe.transpose(bank(3)[:, KV:KV + ROPE], KR[0:64, NEW], IDENT[0:64, 0:64]).then_inc(new_t, 1)
        pe.wait_ge(new_ok, 1)
        seq_pe(pe, 0, fin=False)
        with pe.Fori(0, (SB - 2) // 2) as pair:
            for u in range(2):
                seq_pe(pe, 1 + u, pair * 2)
        seq_pe(pe, SB - 1)
        for step in range(3):
            finish_pe(pe, step, SB - 1, 0)
        pe.wait_ge(ol_split, 1)
        for h in range(H):
            j = 0
            for k in range(KV_T):
                for w, x in ((UVH, OLH), (UVH, OLL), (UVL, OLH)):
                    mm = pe.matmul(bank(0)[:, h * NS:(h + 1) * NS], w[:, k * 1024 + h * VD:k * 1024 + (h + 1) * VD],
                                   x[:, k, h * NS:(h + 1) * NS], start=j == 0, stop=j == 5)
                    j += 1
        mm.then_inc(out_mm, 1)
        pe.wait_ge(out_mm, 1)
        pe.sem_inc(multiplied, 2)

    def samples_act(act):
        flat = QRS[0:64].rearrange("p s h q -> p (s h q)")
        act.activation(QZT[64:128, :], flat, ACT.Copy).then_inc(qz_shift, 1)
        act.activation(QH[:, 0:KV_T].rearrange("p k s c -> p k (s c)"), QA[:].rearrange("p k s h q -> p k (s h q)"), ACT.Copy).then_inc(qz_hi, 1)
        act.wait_ge(qz_shift, 1)
        act.activation(QH[64:128, 2].rearrange("p s c -> p (s c)"), QZT[64:128, :], ACT.Copy).then_inc(qz_hi, 1)
        act.wait_ge(new_mm, 1)
        act.activation(SQ2[:], PS[:, 0, 0:2, :], ACT.Square).then_inc(new_sq, 1)
        act.wait_ge(new_t, 1)
        act.activation(CN[:], bank(3)[:, 0:KV], ACT.Copy).then_inc(new_copy, 1)
        act.activation(MXP[:], bank(3)[:, KV:KV + ROPE], ACT.Square).then_inc(new_sq, 1)
        act.wait_ge(new_ss, 3)
        act.activation(SSN[:], SSN[:], ACT.Sqrt, bias=vec(V_EPS), scale=1.0 / QK).then_inc(new_root, 1)
        act.wait_ge(new_ok, 1)
        seq_act(act, 0, fin=False)
        with act.Fori(0, (SB - 2) // 2) as pair:
            for u in range(2):
                seq_act(act, 1 + u, pair * 2)
        seq_act(act, SB - 1)
        root_act(act, SB - 1, 0)
        exp_act(act, SB - 1, 0)
        act.wait_ge(seq_ol, SB)
        act.activation(OLH[:], OL[:].rearrange("p k h s q -> p k (h s q)"), ACT.Copy).then_inc(ol_hi, 1)
        act.wait_ge(out_mm, 1)
        act.activation(XH[:, :, SEQ:T], bank(0).rearrange("p (h c) -> p h c", h=H), ACT.Copy).then_inc(out_hi, 1)

    def samples_dve(dve):
        dve.memset(QH[0:64, 2].rearrange("p s c -> p (s c)").bitcast(F32), 0.0).then_inc(qz_zero, 1)
        dve.memset(QL[0:64, 2].rearrange("p s c -> p (s c)").bitcast(F32), 0.0).then_inc(qz_zero, 1)
        dve.wait_ge(qz_hi, 2)
        dve.tensor_tensor(QL[:, 0:KV_T].rearrange("p k s c -> p k (s c)"), QA[:].rearrange("p k s h q -> p k (s h q)"), QH[:, 0:KV_T].rearrange("p k s c -> p k (s c)").bitcast(F32), ALU.subtract).then_inc(qz_split, 1)
        dve.wait_ge(qz_zero, 2)
        dve.tensor_tensor(QL[64:128, 2].rearrange("p s c -> p (s c)"), QZT[64:128, :], QH[64:128, 2].rearrange("p s c -> p (s c)").bitcast(F32), ALU.subtract).then_inc(qz_split, 1)
        dve.wait_ge(new_sq, 2)
        dve.tensor_reduce(SSN[:], SQ2[:].rearrange("p a (h d) -> p (a h) d", d=NOPE), AX.X, ALU.add).then_inc(new_ss, 1)
        dve.tensor_reduce(KSS[0][:, 0:1], MXP[:], AX.X, ALU.add).then_inc(new_ss, 1)
        dve.wait_ge(new_ss, 2)
        dve.tensor_scalar(SSN[:], SSN[:], KSS[0][:, 0:1], None, ALU.add).then_inc(new_ss, 1)
        dve.wait_ge(new_root, 1)
        dve.reciprocal(SSN[:], SSN[:]).then_inc(new_rs, 1)
        dve.wait_ge(new_rs, 1)
        dve.tensor_tensor(T3[:, 0:512].rearrange("p (s h q) -> p s h q", s=SB, h=H), bank(2).rearrange("p (s h q) -> p s h q", s=SB, h=H),
                          SSN[:].unsqueeze(1).unsqueeze(3).to_broadcast([P, SB, H, SQ]), ALU.mult).then_inc(new_scaled, 1)
        dve.wait_ge(new_scaled, 1)
        dve.wait_ge(newmask_in, 16)
        dve.wait_ge(new_copy, 1)
        snew = SNEW[:].rearrange("p s h q -> p (s h q)")
        dve.tensor_tensor(snew, snew, T3[:, 0:512], ALU.add).then_inc(new_ok, 1)
        dve.wait_ge(new_ok, 1)
        seq_dve(dve, 0, fin=False)
        with dve.Fori(0, (SB - 2) // 2) as pair:
            for u in range(2):
                seq_dve(dve, 1 + u, pair * 2)
        seq_dve(dve, SB - 1)
        seq_ss_dve(dve, SB - 1, 0)
        scale_dve(dve, SB - 1, 0)
        max_dve(dve, SB - 1, 0)
        less_dve(dve, SB - 1, 0)
        sum_dve(dve, SB - 1, 0)
        ol_dve(dve, SB - 1, 0)
        dve.wait_ge(ol_hi, 1)
        dve.tensor_tensor(OLL[:], OL[:].rearrange("p k h s q -> p k (h s q)"), OLH[:].bitcast(F32), ALU.subtract).then_inc(ol_split, 1)
        dve.wait_ge(out_hi, 1)
        dve.tensor_tensor(XL[:, :, SEQ:T], bank(0).rearrange("p (h c) -> p h c", h=H), XH[:, :, SEQ:T].bitcast(F32), ALU.subtract).then_inc(out_split, 1)
        dve.wait_ge(out_split, 1)
        dve.sem_inc(evacuated, 2)

    def residual_pe(pe, first):
        with pe.Fori(0, 2) as pair:
            for u in range(2):
                multiply_item(pe, first + u, pair * 2, KD, 2, XH, XL)

    def residual_act(act, first, next_norm):
        with act.Fori(0, 2) as pair:
            for u in range(2):
                round_item(act, first + u + 1, pair * 2)
        act.wait_ge(multiplied, first + 4)
        act.wait_ge(evacuated, first + 4 + CREDIT)
        with act.Fori(0, KD) as d:
            xhat_tile(act, None, next_norm, d)

    def residual_dve(dve, first, next_norm):
        with dve.Fori(0, 2) as pair:
            i = pair * 2
            for u in range(2):
                n = first + u
                split_item(dve, n + 1, i)
                dve.wait_ge(multiplied, n + 1 + i)
                x = X[:].rearrange("p (j k) (a t) -> p j (k a) t", k=2, a=2)[:, bass.ds(i + u, 1), :, :].rearrange("p o c t -> p (o c) t")
                dve.tensor_tensor(x, PS[:, n % 2, :, 0:HT], x, ALU.add).then_inc(evacuated, 1)
        dve.wait_ge(evacuated, first + 4 + CREDIT)
        with dve.Fori(0, KD) as d:
            xhat_tile(None, dve, next_norm, d)

    HT_ = m.at("HT_", A0, [KD, T])
    XX = m.at("XX", A0 + 4608, [KD, T])
    RT = m.at("RT", A0 + 9216, [KD, T])
    KT = m.at("KT", A0 + 13824, [KD, T])
    VT_ = HT_
    LORA1 = m.at("LORA1", A0 + 9216, [2 * KD * P])
    TH = m.at("TH", A0 + 18432, [T])
    G1S = m.at("G1S", A0 + 19008, [T])
    RC = m.at("RC", A0 + 19584, [NRC])
    SHIFT = m.at("SHIFT", A0 + 22152, [KD, SB])
    SHO = m.at("SHO", A0 + 22216, [KD, 1 + SB])
    LORA2 = m.at("LORA2", A0 + 4608, [2 * D])
    BT = m.at("BT", A0 + 6656, [T])
    KTI = m.at("KTI", A0 + 7232, [T])
    W2S = m.at("W2S", A0 + 7808, [P])
    G2S = m.at("G2S", A0 + 7936, [P])
    GG = m.at("GG", A0 + 8064, [T])
    BV = m.at("BV", A0 + 8640, [T])
    OMKA = m.at("OMKA", 30760 + 8, [KD])
    W0 = 13824
    AR = m.at("AR", W0, [NC_, 2, CH])
    MB = m.at("MB", W0 + 1152, [NC_, 2, CH])
    MK = m.at("MK", W0 + 2304, [NC_, 2, CH])
    LL = m.at("LL", W0 + 3456, [NC_, CH])
    VTOK = m.at("VTOK", W0 + 4032, [NC_, CH])
    BTOK = m.at("BTOK", W0 + 4608, [NC_, CH])
    KTOK = m.at("KTOK", W0 + 5184, [NC_, CH])
    MD = m.at("MD", W0 + 5760, [NC_, CH])
    LD = m.at("LD", W0 + 6336, [NC_, CH])
    M2 = m.at("M2", W0 + 6912, [NC_, CH])
    L2 = m.at("L2", W0 + 7488, [NC_, CH])
    XA = m.at("XA", W0 + 8064, [NC_, CH])
    XT = m.at("XT", W0 + 8640, [NC_, CH])
    ZZ = m.at("ZZ", W0 + 9216, [NC_, CH])
    S0 = m.at("S0", W0 + 9792, [SB, HS])
    ST = m.at("ST", W0 + 10304, [HS])
    SD = m.at("SD", W0 + 10368, [HS])
    RR = m.at("RR", W0 + 10432, [CH])
    UU = m.at("UU", W0 + 10496, [CH])
    UE = m.at("UE", W0 + 10560, [SB, HS])
    VE = m.at("VE", W0 + 11072, [SB, HS])
    SF = m.at("SF", W0 + 11584, [SB, HS])
    EYE2 = CONST[:, C_FOLD:C_FOLD + 64]

    def flat(t):
        return t.rearrange("p c s -> p (c s)") if len(t.shape) == 3 else t

    def tile(t, mm):
        return t[:, bass.ds(mm, 1), :].rearrange("p o t -> p (o t)")

    rc_in = stage_sem("recurrence", "rc_in")
    lora2_in = stage_sem("recurrence", "lora2_in")
    h_ok = stage_sem("recurrence", "h_ok")
    xx_ok = stage_sem("recurrence", "xx_ok")
    sho_ok = stage_sem("recurrence", "sho_ok")
    mix1 = stage_sem("recurrence", "mix1")
    mix1_used = stage_sem("recurrence", "mix1_used")
    lora1_ok = stage_sem("recurrence", "lora1_ok")
    mixed = stage_sem("recurrence", "mixed")
    mix_hi = stage_sem("recurrence", "mix_hi")
    mix_split = stage_sem("recurrence", "mix_split")
    names_core = ("cp_w", "zag", "sig", "lw", "cum", "prev", "pexp", "kkr", "kksq", "kkmm", "kkmax", "kkroot", "kkrs",
                  "kkn", "ar", "tb", "bt", "tk", "k2", "kti", "bon", "bonmm", "bv", "gram", "gram_m", "tok", "tok_c",
                  "base", "i2", "i2c", "i3", "i3c", "i4", "i4c", "lv_e", "lv_z", "lv_zc", "lv_x", "lv_xc",
                  "s0_in", "st0", "ch_r", "ch_rc", "ch_u", "ch_uc", "ch_y", "ch_s", "ch_sd", "ch_sc",
                  "lw2", "sm_r", "sm_m", "sm_rc", "sm_ue", "sm_s", "sm_sa", "sm_sf", "yt", "ymean", "yc", "ysq", "yvar", "yroot",
                  "yrs", "yn", "yb", "yg", "yhi", "ylo", "s_out")
    q = {n: stage_sem("recurrence", "core_" + n) for n in names_core}

    MU_OF = {"r": 0, "w": 1, "k": 2, "v": 3, "a": 4, "g": 5}

    def mix_sp(sp):
        load_items(sp, I_R, 2, 16)
        sp.wait_ge(stage_end, 16)
        sp.dma_start(RC[:], a["rc"]).then_inc(rc_in, 16)
        sp.dma_start(LORA1[:], a["lora1"]).then_inc(rc_in, 16)
        sp.dma_start(SHIFT[:], a["shift"]).then_inc(rc_in, 16)
        load_items(sp, I_R + 2, 10, 16)
        sp.wait_ge(sho_ok, 2)
        sp.dma_start(o["shift_o"], SHO[:]).then_inc(stored, 16)
        sp.wait_ge(mixed, 24)
        sp.dma_start(LORA2[:], a["lora2"]).then_inc(lora2_in, 16)

    def mix_pe(pe):
        norm_sums(pe, 4, (I_R + 1) % 2)
        pe.wait_ge(rc_in, 48)
        pe.wait_ge(root, 5)
        for j, (out, c0, w) in enumerate(((PS[0:64, 0, 0:2], 0, 64), (PS[64:128, 0, 2:4], 64, 64), (PS[:, 1, 0:2], None, P))):
            for k in range(KD):
                n = j * KD + k
                pe.wait_ge(mix1, n + 1)
                lhs = LORA1[:, k * P + c0:k * P + c0 + w] if c0 is not None else LORA1[:, (KD + k) * P:(KD + k + 1) * P]
                for half in range(2):
                    mm = pe.matmul(out[:, half, 0:HT], lhs, (T1 if n % 2 == 0 else T2)[:, half * HT:(half + 1) * HT],
                                   start=k == 0, stop=k == KD - 1)
                mm.then_inc(mix1_used, 1)
        pe.wait_ge(lora1_ok, 3)
        for p, first in enumerate((I_R, I_K, I_V)):
            with pe.Fori(0, 2) as pair:
                for u in range(2):
                    multiply_item(pe, first + u, pair * 2, KD, 2, XH, XL, before=lambda k: pe.wait_ge(mix_split, 8 * p + k + 1))

    def mix_act(act):
        norm_root(act, 4, (I_R + 1) % 2)
        act.wait_ge(mix1_used, 24)
        act.activation(halves(TH[0:64]), PS[0:64, 0, 0:2, 0:HT], ACT.Tanh).then_inc(lora1_ok, 1)
        act.activation(halves(TH[64:128]), PS[64:128, 0, 2:4, 0:HT], ACT.Copy).then_inc(lora1_ok, 1)
        act.activation(halves(G1S[:]), PS[:, 1, 0:2, 0:HT], ACT.Sigmoid).then_inc(lora1_ok, 1)
        for p, (first, dst) in enumerate(((I_R, RT), (I_K, KT), (I_V, VT_))):
            for k in range(KD):
                act.wait_ge(mixed, 8 * p + k + 1)
                act.activation(XH[:, k, :], (T3 if k % 2 == 0 else T4)[:], ACT.Copy).then_inc(mix_hi, 1)
            if p == 2:
                act.wait_ge(sho_ok, 2)
            for u in range(4):
                n = first + u
                if n < I_V + 3:
                    round_item(act, n + 1)
                act.wait_ge(multiplied, n + 1)
                act.activation(dst[:].rearrange("p k (a t) -> p (k a) t", a=2)[:, 4 * u:4 * u + 4, :],
                               PS[:, n % 2, :, 0:HT], ACT.Copy).then_inc(evacuated, 1)

    def mix_dve(dve):
        norm_rstd(dve, 4)
        dve.wait_ge(rstd_ok, 5)
        for k in range(KD):
            dve.scalar_tensor_tensor(out=HT_[:, k, :], in0=X[:, k, :], scalar=vec(V_G[4] + k), in1=RSTD[:], op0=ALU.mult, op1=ALU.mult).then_inc(h_ok, 1)
        dve.wait_ge(h_ok, KD)
        dve.wait_ge(rc_in, 48)
        hs = HT_[:, :, SEQ:T].rearrange("p k (s q) -> p k s q", s=SB)
        xs = XX[:, :, SEQ:T].rearrange("p k (s q) -> p k s q", s=SB)
        dve.tensor_tensor(XX[:, :, 1:SEQ], HT_[:, :, 0:SEQ - 1], HT_[:, :, 1:SEQ], ALU.subtract).then_inc(xx_ok, 1)
        dve.tensor_scalar(XX[:, :, 0:1], HT_[:, :, 0:1], -1.0, None, ALU.mult).then_inc(xx_ok, 1)
        dve.tensor_tensor(xs[:, :, :, 1:SQ], hs[:, :, :, 0:SQ - 1], hs[:, :, :, 1:SQ], ALU.subtract).then_inc(xx_ok, 1)
        dve.tensor_tensor(xs[:, :, :, 0], SHIFT[:], hs[:, :, :, 0], ALU.subtract).then_inc(xx_ok, 1)
        dve.tensor_copy(SHO[:, :, 0:1], HT_[:, :, SEQ - 1:SEQ]).then_inc(sho_ok, 1)
        dve.tensor_copy(SHO[:, :, 1:1 + SB], hs[:, :, :, SQ - 1]).then_inc(sho_ok, 1)
        dve.wait_ge(xx_ok, 4)
        for j, x in enumerate("wag"):
            for k in range(KD):
                n = j * KD + k
                if n >= 2:
                    dve.wait_ge(mix1_used, n - 1)
                dve.scalar_tensor_tensor(out=(T1 if n % 2 == 0 else T2)[:], in0=XX[:, k, :], scalar=vec(V_MU + 8 * MU_OF[x] + k),
                                         in1=HT_[:, k, :], op0=ALU.mult, op1=ALU.add).then_inc(mix1, 1)
        for p, (x, first) in enumerate((("r", I_R), ("k", I_K), ("v", I_V))):
            if p:
                dve.wait_ge(multiplied, first)
            for k in range(KD):
                t = (T3 if k % 2 == 0 else T4)[:]
                dve.scalar_tensor_tensor(out=t, in0=XX[:, k, :], scalar=vec(V_MU + 8 * MU_OF[x] + k),
                                         in1=HT_[:, k, :], op0=ALU.mult, op1=ALU.add).then_inc(mixed, 1)
                dve.wait_ge(mix_hi, 8 * p + k + 1)
                dve.tensor_tensor(XL[:, k, :], t, XH[:, k, :].bitcast(F32), ALU.subtract).then_inc(mix_split, 1)
            for u in range(4):
                if first + u < I_V + 3:
                    split_item(dve, first + u + 1)

    def core_sp(sp):
        with sp.Fori(0, KD) as mm:
            sp.wait_ge(q["sm_sf"], mm)
            sp.dma_start(S0[:].rearrange("p s i -> p (s i)").rearrange("p (o c) -> p o c", o=1),
                         a["state"][bass.ds(mm, 1), :, :, :].rearrange("o p s i -> p o (s i)")).then_inc(q["s0_in"], 16)
            sp.wait_ge(q["ch_sc"], mm * 8 + 8)
            sp.dma_start(o["wkv_p"][bass.ds(mm, 1), :, :].rearrange("o p i -> p o i"),
                         ST[:].rearrange("p (o i) -> p o i", o=1)).then_inc(q["s_out"], 16)
            sp.wait_ge(q["sm_sf"], mm + 1)
            sp.dma_start(o["wkv_s"][bass.ds(mm, 1), :, :, :].rearrange("o p s i -> p o (s i)"),
                         SF[:].rearrange("p s i -> p (s i)").rearrange("p (o c) -> p o c", o=1)).then_inc(q["s_out"], 16)
        sp.wait_ge(q["s_out"], 32 * KD)

    def core_pool(pool):
        pool.wait_ge(lora2_in, 16)
        with pool.Fori(0, KD) as mm:
            pool.wait_ge(q["zag"], mm)
            pool.tensor_copy(W2S[:].rearrange("p (o c) -> p o c", o=1), LORA2[:, 0:D].rearrange("p (m c) -> p m c", m=KD)[:, bass.ds(mm, 1), :]).then_inc(q["cp_w"], 1)
            pool.tensor_copy(G2S[:].rearrange("p (o c) -> p o c", o=1), LORA2[:, D:2 * D].rearrange("p (m c) -> p m c", m=KD)[:, bass.ds(mm, 1), :]).then_inc(q["cp_w"], 1)

    HEADS = (slice(0, HS), slice(HS, P))

    def chunks_mm(pe, b, lhs, rhs):
        for c in range(NC_):
            for r in HEADS:
                mm = pe.matmul(bank(b + c // 8, r)[:, (c % 8) * CH:(c % 8 + 1) * CH], lhs[r, c, :], rhs[r, c, :], start=True, stop=True)
        return mm

    def chunks(b, n=T):
        return PS[:].rearrange("p s b t -> p (s b t)")[:, 512 * b:512 * b + n]

    def core_pe(pe):
        def wait(s, value):
            pe.wait_ge(s, value)
            pe.sem_inc(waits_passed, 1)

        with pe.Fori(0, KD) as mm_:
            n = mm_ + 1
            one = bass.ds(mm_, 1)
            wait(q["cp_w"], n * 2)
            wait(q["ylo"], mm_)
            for half in range(2):
                w = slice(half * HT, (half + 1) * HT)
                pe.matmul(PS[:, 1, half, 0:HT], G2S[:], G1S[:, w], start=True, stop=True)
                pe.matmul(PS[:, 0, half, 0:HT], W2S[0:64, :], TH[0:64, w], start=True, stop=True)
                mm = pe.matmul(PS[:, 0, 2 + half, 0:HT], W2S[64:128, :], TH[64:128, w], start=True, stop=True)
            mm.then_inc(q["zag"], 1)
            wait(q["kksq"], n)
            for half in range(2):
                mm = pe.matmul(PS[:, 1, 2 + half, 0:HT], BLK, LD[:].rearrange("p c s -> p (c s)")[:, half * HT:(half + 1) * HT], start=True, stop=True)
            mm.then_inc(q["kkmm"], 1)
            wait(q["bon"], n)
            wait(q["kkmax"], n)
            for half in range(2):
                mm = pe.matmul(PS[:, 1, 2 + half, 0:HT], BLK, L2[:].rearrange("p c s -> p (c s)")[:, half * HT:(half + 1) * HT], start=True, stop=True)
            mm.then_inc(q["bonmm"], 1)
            wait(q["ar"], n * 2)
            wait(q["bt"], n)
            wait(q["kti"], n)
            wait(q["bv"], n)
            for c in range(NC_):
                k = slice(c * CH, (c + 1) * CH)
                for r in HEADS:
                    rhs = AR[r, c].rearrange("p a t -> p (a t)")
                    pe.matmul(bank(c // 4, r)[:, (c % 4) * P:(c % 4 + 1) * P], BT[r, k], rhs, start=True, stop=True)
                for r in HEADS:
                    rhs = AR[r, c].rearrange("p a t -> p (a t)")
                    pe.matmul(bank(3 + c // 4, r)[:, (c % 4) * P:(c % 4 + 1) * P], KTI[r, k], rhs, start=True, stop=True)
                for r in HEADS:
                    mm = pe.matmul(bank(6 + c // 8, r)[:, (c % 8) * CH:(c % 8 + 1) * CH], AR[r, c, 0, :], BT[r, k], start=True, stop=True)
            mm.then_inc(q["gram"], 1)
            wait(q["gram_m"], n * 3)
            for j, src in enumerate((VTS, BT, KTI)):
                for c in range(NC_):
                    for hh, r in enumerate(HEADS):
                        mm = pe.matmul(bank(2 * j + c // 8, r)[:, (c % 8) * CH:(c % 8 + 1) * CH], src[r, c * CH:(c + 1) * CH], EYE2[r, :], start=True, stop=True)
            mm.then_inc(q["tok"], 1)
            wait(q["base"], n * 4)
            wait(q["tok_c"], n * 3)
            chunks_mm(pe, 0, LD, MD)
            chunks_mm(pe, 2, MD, LD).then_inc(q["i2"], 1)
            wait(q["i2c"], n * 2)
            chunks_mm(pe, 4, XT, M2)
            chunks_mm(pe, 6, M2, XT)
            chunks_mm(pe, 0, L2, M2).then_inc(q["i3"], 1)
            wait(q["i3c"], n * 3)
            chunks_mm(pe, 2, XT, MD)
            chunks_mm(pe, 4, MD, XT).then_inc(q["i4"], 1)
            for l in range(3):
                wait(q["lv_e"], mm_ * 3 + l + 1)
                wait(q["i4c"], n * 2)
                if l:
                    wait(q["lv_xc"], mm_ * 5 + 2 * l)
                chunks_mm(pe, 0, LD, XA).then_inc(q["lv_z"], 1)
                wait(q["lv_zc"], mm_ * 3 + l + 1)
                mm = chunks_mm(pe, 2, XT, ZZ)
                if l < 2:
                    mm = chunks_mm(pe, 4, ZZ, XT)
                mm.then_inc(q["lv_x"], 1)
            wait(q["lv_xc"], n * 5)
            yb = lambda c, r: bank(6 + c // 8, r)[:, (c % 8) * CH:(c % 8 + 1) * CH]
            for c in range(NC_ - 1):
                if c == 0:
                    wait(q["st0"], n)
                else:
                    wait(q["ch_sc"], mm_ * 8 + c)
                for r in HEADS:
                    pe.matmul(bank(0, r)[:, 0:CH], AR[r, c, 0, :], ST[r, :], start=True, stop=False)
                for r in HEADS:
                    mm = pe.matmul(bank(0, r)[:, 0:CH], MK[r, c, 0, :], VTOK[r, c, :], start=False, stop=True)
                mm.then_inc(q["ch_r"], 1)
                wait(q["ch_rc"], mm_ * 8 + c + 1)
                for r in HEADS:
                    mm = pe.matmul(bank(1, r)[:, 0:CH], XA[r, c, :], RR[r, :], start=True, stop=True)
                mm.then_inc(q["ch_u"], 1)
                for r in HEADS:
                    pe.matmul(yb(c, r), ST[r, :], AR[r, c, 1, :], start=True, stop=False)
                for r in HEADS:
                    pe.matmul(yb(c, r), VTOK[r, c, :], MK[r, c, 1, :], start=False, stop=False)
                for r in HEADS:
                    pe.matmul(bank(2, r)[:, 0:CH], KTOK[r, c, :], VTOK[r, c, :], start=True, stop=False)
                wait(q["ch_uc"], mm_ * 8 + c + 1)
                for r in HEADS:
                    mm = pe.matmul(bank(2, r)[:, 0:CH], BTOK[r, c, :], UU[r, :], start=False, stop=True)
                mm.then_inc(q["ch_s"], 1)
                for r in HEADS:
                    mm = pe.matmul(yb(c, r), UU[r, :], MB[r, c, 1, :], start=False, stop=True)
                mm.then_inc(q["ch_y"], 1)
            c = NC_ - 1
            wait(q["s0_in"], n * 16)
            wait(q["ch_sc"], n * 8)
            s0 = S0[:].rearrange("p s i -> p (s i)")
            for r in HEADS:
                pe.matmul(bank(3, r), AR[r, c, 0, :], s0[r, :], start=True, stop=True)
            for r in HEADS:
                mm = pe.matmul(bank(0, r)[:, 0:CH], MK[r, c, 0, :], VTOK[r, c, :], start=True, stop=True)
            mm.then_inc(q["sm_r"], 1)
            wait(q["sm_rc"], n)
            for r in HEADS:
                mm = pe.matmul(bank(1, r)[:, 0:CH], XA[r, c, :], RR[r, :], start=True, stop=True)
            mm.then_inc(q["ch_u"], 1)
            wait(q["sm_ue"], n * 3)
            for r in HEADS:
                pe.matmul(bank(4, r), BTOK[r, c, :], UE[:].rearrange("p s i -> p (s i)")[r, :], start=True, stop=False)
            for r in HEADS:
                mm = pe.matmul(bank(4, r), KTOK[r, c, :], VE[:].rearrange("p s i -> p (s i)")[r, :], start=False, stop=True)
            mm.then_inc(q["sm_s"], 1)
            for r in HEADS:
                pe.matmul(yb(c, r), UU[r, :], MB[r, c, 1, :], start=True, stop=False)
            for r in HEADS:
                pe.matmul(yb(c, r), VTOK[r, c, :], MK[r, c, 1, :], start=False, stop=True)
            for s in range(SB):
                for r in HEADS:
                    mm = pe.matmul(yb(c, r)[:, s * SQ:(s + 1) * SQ], S0[r, s, :], AR[r, c, 1, s * SQ:(s + 1) * SQ],
                                   start=False, stop=True, skip_group_check=True)
            mm.then_inc(q["ch_y"], 1)
            wait(q["yt"], n)
            for half in range(2):
                mm = pe.matmul(PS[:, 0, half, 0:HT], BLK, T1[:, half * HT:(half + 1) * HT], start=True, stop=True)
            mm.then_inc(q["ymean"], 1)
            wait(q["ysq"], n)
            for half in range(2):
                mm = pe.matmul(PS[:, 0, 2 + half, 0:HT], BLK, T3[:, half * HT:(half + 1) * HT], start=True, stop=True)
            mm.then_inc(q["yvar"], 1)

    VTS = m.at("VTS", W0 + 9216, [T])

    def core_act(act):
        with act.Fori(0, KD) as mm:
            n = mm + 1
            act.activation(VTS[:], tile(VT_, mm), ACT.Copy).then_inc(q["tb"], 1)
            act.wait_ge(q["zag"], n)
            act.activation(halves(T1[:]), banks(0, 0), ACT.Sigmoid, bias=vec(V_W0 + mm)).then_inc(q["sig"], 1)
            act.activation(halves(SQACC[:]), banks(0, 2), ACT.Sigmoid, bias=vec(V_A0 + mm)).then_inc(q["sig"], 1)
            act.activation(halves(GG[:]), banks(1, 0), ACT.Copy).then_inc(q["sig"], 1)
            act.wait_ge(q["kkr"], n)
            act.activation(LD[:].rearrange("p c s -> p (c s)"), RSTD[:], ACT.Square).then_inc(q["kksq"], 1)
            act.wait_ge(q["kkmax"], n)
            act.activation(LD[:].rearrange("p c s -> p (c s)"), LD[:].rearrange("p c s -> p (c s)"), ACT.Sqrt).then_inc(q["kkroot"], 1)
            act.wait_ge(q["cum"], n)
            act.activation(T4[:], T2[:], ACT.Exp).then_inc(q["pexp"], 1)
            act.activation(SQT[:], T2[:], ACT.Exp, scale=-1.0).then_inc(q["pexp"], 1)
            act.wait_ge(q["prev"], n)
            act.activation(T3[:], T3[:], ACT.Exp).then_inc(q["pexp"], 1)
            act.wait_ge(q["tok"], n)
            for j, dst in enumerate((VTOK, BTOK, KTOK)):
                act.activation(dst[:].rearrange("p c s -> p (c s)"), chunks(2 * j), ACT.Copy).then_inc(q["tok_c"], 1)
            for c in range(NC_ - 1):
                act.wait_ge(q["ch_r"], mm * 8 + c + 1)
                act.activation(RR[:], bank(0)[:, 0:CH], ACT.Copy).then_inc(q["ch_rc"], 1)
                act.wait_ge(q["ch_u"], mm * 9 + c + 1)
                act.activation(UU[:], bank(1)[:, 0:CH], ACT.Copy).then_inc(q["ch_uc"], 1)
            act.wait_ge(q["ch_y"], n * 9)
            act.activation(T1[:], chunks(6), ACT.Copy).then_inc(q["yt"], 1)
            act.wait_ge(q["yc"], n)
            act.activation(T3[:], T2[:], ACT.Square).then_inc(q["ysq"], 1)
            act.wait_ge(q["yvar"], n)
            act.activation(halves(SQT[:]), banks(0, 2), ACT.Sqrt, bias=vec(V_LNEPS), scale=1.0 / HS).then_inc(q["yroot"], 1)
            act.wait_ge(q["yg"], n)
            act.activation(tile(XH, mm), T2[:], ACT.Copy).then_inc(q["yhi"], 1)

    def core_dve(dve):
        f = lambda t: t[:].rearrange("p c s -> p (c s)")
        b9 = lambda col: RC[:, col:col + CH].unsqueeze(1).to_broadcast([P, NC_, CH])
        seqm = RC[:, R_SEQ:R_SEQ + SB]
        dve.wait_ge(rc_in, 48)
        dve.tensor_scalar(OMKA[:], VEC[:, V_KA:V_KA + KD], -1.0, 1.0, ALU.mult, ALU.add).then_inc(q["tk"], 1)
        dve.wait_ge(q["tk"], 1)
        with dve.Fori(0, KD) as mm:
            n = mm + 1
            dve.tensor_scalar(RSTD[:], tile(KT, mm), vec(V_KK + mm), None, ALU.mult).then_inc(q["kkr"], 1)
            dve.wait_ge(q["sig"], n * 3)
            dve.tensor_scalar(T1[:], T1[:], -float(np.exp(-0.5)), None, ALU.mult).then_inc(q["lw"], 1)
            dve.wait_ge(q["lw"], n)
            dve.tensor_tensor_scan(T2[:], RC[:, R_SCAN:R_SCAN + T], T1[:], 0.0, ALU.mult, ALU.add).then_inc(q["cum"], 1)
            dve.wait_ge(q["cum"], n)
            dve.tensor_tensor(T3[:], T2[:], T1[:], ALU.subtract).then_inc(q["prev"], 1)
            dve.wait_ge(q["kkmm"], n)
            dve.tensor_scalar(halves(f(LD)), banks(1, 2), 1e-24, None, ALU.max).then_inc(q["kkmax"], 1)
            dve.tensor_scalar(f(M2), SQACC[:], vec(V_KA + mm), OMKA[:, bass.ds(mm, 1)], ALU.mult, ALU.add).then_inc(q["k2"], 1)
            dve.wait_ge(q["k2"], n * 2 - 1)
            dve.tensor_tensor(f(M2), f(M2), tile(KT, mm), ALU.mult).then_inc(q["k2"], 1)
            dve.wait_ge(q["k2"], n * 2)
            dve.scalar_tensor_tensor(out=f(L2), in0=f(M2), scalar=vec(V_RK + mm), in1=tile(RT, mm), op0=ALU.mult, op1=ALU.mult).then_inc(q["bon"], 1)
            dve.wait_ge(q["kkroot"], n)
            dve.reciprocal(f(LD), f(LD)).then_inc(q["kkrs"], 1)
            dve.wait_ge(q["kkrs"], n)
            dve.tensor_tensor(RSTD[:], RSTD[:], f(LD), ALU.mult).then_inc(q["kkn"], 1)
            dve.wait_ge(q["kkn"], n)
            dve.wait_ge(q["pexp"], n * 3)
            three = lambda t: t[:].rearrange("p (c s) -> p c s", s=CH)
            dve.scalar_tensor_tensor(out=AR[:, :, 0, :], in0=three(RSTD), scalar=-1.0, in1=three(T3), op0=ALU.mult, op1=ALU.mult).then_inc(q["ar"], 1)
            dve.tensor_tensor(AR[:, :, 1, :], tile(RT, mm).rearrange("p (c s) -> p c s", s=CH), three(T4), ALU.mult).then_inc(q["ar"], 1)
            dve.tensor_tensor(RSTD[:], RSTD[:], SQACC[:], ALU.mult).then_inc(q["base"], 1)
            dve.wait_ge(q["base"], mm * 4 + 1)
            dve.tensor_tensor(BT[:], RSTD[:], SQT[:], ALU.mult).then_inc(q["bt"], 1)
            dve.tensor_tensor(KTI[:], f(M2), SQT[:], ALU.mult).then_inc(q["kti"], 1)
            dve.wait_ge(q["bonmm"], n)
            dve.wait_ge(q["tb"], n)
            dve.tensor_tensor(halves(BV[:]), banks(1, 2), halves(VTS[:]), ALU.mult).then_inc(q["bv"], 1)
            dve.wait_ge(q["gram"], n)
            dve.tensor_tensor(MB[:].rearrange("p c a s -> p (c a s)"), chunks(0, 2 * T), RC[:, R_GRAM:R_GRAM + 2 * T], ALU.mult).then_inc(q["gram_m"], 1)
            dve.tensor_tensor(MK[:].rearrange("p c a s -> p (c a s)"), chunks(3, 2 * T), RC[:, R_GRAM:R_GRAM + 2 * T], ALU.mult).then_inc(q["gram_m"], 1)
            dve.tensor_tensor(f(LL), chunks(6), RC[:, R_LOW:R_LOW + T], ALU.mult).then_inc(q["gram_m"], 1)
            dve.wait_ge(q["gram_m"], n * 3)
            dve.tensor_tensor(MD[:], MB[:, :, 0, :], b9(R_B8), ALU.mult).then_inc(q["base"], 1)
            dve.tensor_tensor(LD[:], LL[:], b9(R_B8), ALU.mult).then_inc(q["base"], 1)
            dve.wait_ge(q["base"], mm * 4 + 3)
            eye = EYE2.unsqueeze(1).to_broadcast([P, NC_, CH])
            dve.tensor_tensor(XA[:], MD[:], eye, ALU.add).then_inc(q["lw2"], 1)
            dve.tensor_tensor(XT[:], LD[:], eye, ALU.add).then_inc(q["base"], 1)
            dve.wait_ge(q["i2"], n)
            dve.tensor_copy(f(M2), chunks(0)).then_inc(q["i2c"], 1)
            dve.tensor_copy(f(L2), chunks(2)).then_inc(q["i2c"], 1)
            dve.wait_ge(q["i3"], n)
            dve.wait_ge(q["lw2"], n)
            dve.wait_ge(q["base"], n * 4)
            dve.tensor_tensor(f(XA), f(XA), chunks(4), ALU.add).then_inc(q["i3c"], 1)
            dve.tensor_tensor(f(XT), f(XT), chunks(6), ALU.add).then_inc(q["i3c"], 1)
            dve.tensor_copy(f(MD), chunks(0)).then_inc(q["i3c"], 1)
            dve.wait_ge(q["i4"], n)
            dve.wait_ge(q["i3c"], n * 3)
            dve.tensor_tensor(f(XA), f(XA), chunks(2), ALU.add).then_inc(q["i4c"], 1)
            dve.tensor_tensor(f(XT), f(XT), chunks(4), ALU.add).then_inc(q["i4c"], 1)
            dve.wait_ge(q["i4c"], n * 2)
            for l in range(3):
                if l:
                    dve.wait_ge(q["lv_z"], mm * 3 + l)
                dve.tensor_tensor(LD[:], LL[:], b9(R_OFF + CH * l), ALU.mult).then_inc(q["lv_e"], 1)
                dve.wait_ge(q["lv_z"], mm * 3 + l + 1)
                dve.tensor_copy(f(ZZ), chunks(0)).then_inc(q["lv_zc"], 1)
                dve.wait_ge(q["lv_x"], mm * 3 + l + 1)
                dve.tensor_tensor(f(XA), f(XA), chunks(2), ALU.add).then_inc(q["lv_xc"], 1)
                if l < 2:
                    dve.tensor_tensor(f(XT), f(XT), chunks(4), ALU.add).then_inc(q["lv_xc"], 1)
                dve.wait_ge(q["lv_xc"], mm * 5 + min(2 * l + 2, 5))
            dve.wait_ge(q["s_out"], mm * 32)
            dve.memset(ST[:], 0.0).then_inc(q["st0"], 1)
            dve.wait_ge(q["st0"], n)
            for c in range(NC_ - 1):
                last = T4[:, (c + 1) * CH - 1:(c + 1) * CH]
                dve.tensor_scalar(SD[:], ST[:], last, None, ALU.mult).then_inc(q["ch_sd"], 1)
                dve.wait_ge(q["ch_sd"], mm * 8 + c + 1)
                dve.wait_ge(q["ch_s"], mm * 8 + c + 1)
                dve.scalar_tensor_tensor(out=ST[:], in0=bank(2)[:, 0:CH], scalar=last, in1=SD[:], op0=ALU.mult, op1=ALU.add).then_inc(q["ch_sc"], 1)
                dve.wait_ge(q["ch_sc"], mm * 8 + c + 1)
            dve.wait_ge(q["sm_r"], n)
            dve.tensor_tensor(UE[:], bank(3).rearrange("p (s i) -> p s i", s=SB), seqm.unsqueeze(2).to_broadcast([P, SB, HS]), ALU.mult).then_inc(q["sm_m"], 1)
            dve.wait_ge(q["sm_m"], n * 2 - 1)
            dve.tensor_reduce(SD[:], UE[:].rearrange("p s i -> p i s"), AX.X, ALU.add).then_inc(q["sm_m"], 1)
            dve.wait_ge(q["sm_m"], n * 2)
            dve.tensor_tensor(RR[:], bank(0)[:, 0:CH], SD[:], ALU.add).then_inc(q["sm_rc"], 1)
            dve.wait_ge(q["ch_u"], n * 9)
            dve.tensor_tensor(UE[:], bank(1)[:, 0:CH].unsqueeze(1).to_broadcast([P, SB, HS]), seqm.unsqueeze(2).to_broadcast([P, SB, HS]), ALU.mult).then_inc(q["sm_ue"], 1)
            dve.tensor_copy(UU[:], bank(1)[:, 0:CH]).then_inc(q["sm_ue"], 1)
            dve.tensor_tensor(VE[:], VTOK[:, NC_ - 1, :].unsqueeze(1).to_broadcast([P, SB, HS]), seqm.unsqueeze(2).to_broadcast([P, SB, HS]), ALU.mult).then_inc(q["sm_ue"], 1)
            dve.wait_ge(q["sm_s"], n)
            dve.tensor_tensor(SF[:].rearrange("p s i -> p (s i)"), bank(4), S0[:].rearrange("p s i -> p (s i)"), ALU.add).then_inc(q["sm_sa"], 1)
            dve.wait_ge(q["sm_sa"], n)
            plast = T4[:, SEQ:T].rearrange("p (s q) -> p s q", s=SB)[:, :, SQ - 1:SQ].to_broadcast([P, SB, HS])
            dve.wait_ge(q["ch_y"], n * 9)
            dve.tensor_tensor(SF[:], SF[:], plast, ALU.mult).then_inc(q["sm_sf"], 1)
            dve.wait_ge(q["ymean"], n)
            dve.scalar_tensor_tensor(out=halves(T2[:]), in0=banks(0, 0), scalar=-1.0 / HS, in1=halves(T1[:]), op0=ALU.mult, op1=ALU.add).then_inc(q["yc"], 1)
            dve.wait_ge(q["yroot"], n)
            dve.reciprocal(SQT[:], SQT[:]).then_inc(q["yrs"], 1)
            dve.wait_ge(q["yrs"], n)
            dve.scalar_tensor_tensor(out=T2[:], in0=T2[:], scalar=vec(V_LW + mm), in1=SQT[:], op0=ALU.mult, op1=ALU.mult).then_inc(q["yn"], 1)
            dve.wait_ge(q["yn"], n)
            dve.scalar_tensor_tensor(out=T2[:], in0=T2[:], scalar=vec(V_LB + mm), in1=BV[:], op0=ALU.add, op1=ALU.add).then_inc(q["yb"], 1)
            dve.wait_ge(q["yb"], n)
            dve.tensor_tensor(T2[:], T2[:], GG[:], ALU.mult).then_inc(q["yg"], 1)
            dve.wait_ge(q["yhi"], n)
            dve.tensor_tensor(tile(XL, mm), T2[:], tile(XH, mm).bitcast(F32), ALU.subtract).then_inc(q["ylo"], 1)

    @block.sync
    def _(sp):
        sp.dma_start(X[:], a["x"]).then_inc(x_in, 16)
        sp.dma_start(CONST[:], a["const"]).then_inc(const_in, 16)
        sp.dma_start(VEC[:], a["vec"]).then_inc(const_in, 16)
        ffn_sp(sp, 0)
        lat_sp(sp)
        sp.wait_ge(stage_end, 4)
        heads_sp(sp)
        sp.wait_ge(stage_end, 8)
        sp.wait_ge(stored, 32)
        samples_sp(sp)
        load_items(sp, I_MO, 4, 16)
        ffn_sp(sp, 1)
        ffn_sp(sp, 2)
        mix_sp(sp)
        sp.wait_ge(stage_end, 20)
        core_sp(sp)
        sp.wait_ge(stage_end, 24)
        load_items(sp, I_RO, 4, 16)
        ffn_sp(sp, 3)
        sp.wait_ge(evacuated, N_ITEMS + CREDIT)
        sp.dma_start(o["y"], X[:]).then_inc(stored, 16)
        sp.wait_ge(stored, 64)

    @block.scalar
    def _(act):
        round_item(act, 0)
        act.wait_ge(const_in, 32)
        act.wait_ge(x_in, 16)
        for d in range(KD):
            xhat_tile(act, None, 0, d)
        ffn_act(act, 0, 1)
        lat_act(act)
        barrier(act, 1)
        heads_act(act)
        barrier(act, 2)
        samples_act(act)
        barrier(act, 3)
        round_item(act, I_MO)
        residual_act(act, I_MO, 2)
        ffn_act(act, 1, 3)
        ffn_act(act, 2, None)
        barrier(act, 4)
        mix_act(act)
        barrier(act, 5)
        core_act(act)
        barrier(act, 6)
        round_item(act, I_RO)
        residual_act(act, I_RO, 5)
        ffn_act(act, 3, None, last=True)

    @block.gpsimd
    def _(pool):
        zero_squares(pool, 0)
        pool.wait_ge(x_in, 16)
        for d in range(KD):
            square_tile(pool, 0, d)
        norm_pool(pool, 1, I_LAT - KD)
        barrier(pool, 1)
        heads_pool(pool)
        barrier(pool, 2)
        samples_pool(pool)
        barrier(pool, 3)
        pool.sem_clear(range(shared[0].num, shared[-1].num + 1))
        norm_pool(pool, 2, I_MO, 2)
        norm_pool(pool, 3, I_FFN2 - KD)
        norm_pool(pool, 4, I_R - KD)
        barrier(pool, 4)
        barrier(pool, 5)
        core_pool(pool)
        barrier(pool, 6)
        norm_pool(pool, 5, I_RO, 2)

    @block.vector
    def _(dve):
        dve.memset(T1[:], 0.0).then_inc(evacuated, CREDIT)
        split_item(dve, 0)
        dve.wait_ge(const_in, 32)
        dve.wait_ge(x_in, 16)
        for d in range(KD):
            xhat_tile(None, dve, 0, d)
        ffn_dve(dve, 0, 1)
        lat_dve(dve)
        barrier(dve, 1)
        heads_dve(dve)
        barrier(dve, 2)
        samples_dve(dve)
        barrier(dve, 3)
        split_item(dve, I_MO)
        residual_dve(dve, I_MO, 2)
        ffn_dve(dve, 1, 3)
        ffn_dve(dve, 2, None)
        barrier(dve, 4)
        mix_dve(dve)
        barrier(dve, 5)
        core_dve(dve)
        barrier(dve, 6)
        split_item(dve, I_RO)
        residual_dve(dve, I_RO, 5)
        ffn_dve(dve, 3, None, last=True)

    @block.tensor
    def _(pe):
        pe.wait_ge(const_in, 32)
        ffn_pe(pe, 0)
        lat_pe(pe)
        barrier(pe, 1)
        heads_pe(pe)
        barrier(pe, 2)
        samples_pe(pe)
        barrier(pe, 3)
        residual_pe(pe, I_MO)
        ffn_pe(pe, 1)
        ffn_pe(pe, 2)
        barrier(pe, 4)
        mix_pe(pe)
        barrier(pe, 5)
        core_pe(pe)
        barrier(pe, 6)
        residual_pe(pe, I_RO)
        ffn_pe(pe, 3)

    ctx.close()


def _blocks(w):
    k, n = w.shape
    return w.reshape(k // P, P, n // P, P).transpose(1, 2, 0, 3)


def _item(*parts):
    flat = np.concatenate([x.reshape(P, -1) for x in parts], axis=1)
    out = np.zeros((P, ITEM), np.float32)
    out[:, :flat.shape[1]] = flat
    return out


def _ffn_items(wg, wu, wd):
    g, u = _blocks(wg), _blocks(wu)
    at, items = 0, []
    for cnt in PARTS:
        items += [_item(g[:, j], u[:, j]) for j in range(at, at + cnt)]
        d = _blocks(wd[at * P:(at + cnt) * P])
        items += [_item(d[:, j]) for j in range(KD)]
        at += cnt
    return items


def _pairs(w):
    b = _blocks(w)
    return [_item(b[:, j:j + 2]) for j in range(0, b.shape[1], 2)]


def _weights(v):
    w = []
    rot = np.r_[ROPE // 2:ROPE, 0:ROPE // 2]
    down = v["mla_w_down"][0]
    rope = down[:, -ROPE:]
    uq = v["mla_w_uq"][0].reshape(-1, H, QK)
    w += _ffn_items(v["ffn_w_gate"][0, 0], v["ffn_w_up"][0, 0], v["ffn_w_down"][0, 0])
    w += _pairs(np.concatenate([down[:, :-ROPE], rope, rope[:, rot]], axis=1))
    for h in range(H):
        r = uq[:, h, NOPE:]
        w += _pairs(np.concatenate([uq[:, h, :NOPE], r, r[:, rot]], axis=1))
    for x in (v["mla_w_uk"][0], v["mla_w_uv"][0]):
        w.append(_item(x.reshape(KV_T, P, -1).transpose(1, 0, 2)))
    w += _pairs(v["mla_w_o"][0])
    w += _ffn_items(v["ffn_w_gate"][0, 1], v["ffn_w_up"][0, 1], v["ffn_w_down"][0, 1])
    w += _ffn_items(v["ffn_w_gate"][1, 0], v["ffn_w_up"][1, 0], v["ffn_w_down"][1, 0])
    for x in "rkvo":
        w += _pairs(v[f"rwkv_w_{x}"][0])
    w += _ffn_items(v["ffn_w_gate"][1, 1], v["ffn_w_up"][1, 1], v["ffn_w_down"][1, 1])
    return np.stack(w)


def _vectors(v):
    out = np.zeros((P, NV), np.float32)

    def put(col, x):
        x = x.reshape(-1, P) if x.size >= P else x.reshape(1, -1)
        out[:x.shape[1], col:col + x.shape[0]] = x.T

    fn, mn = v["ffn_norm"], v["mix_norm"]
    for n, x in enumerate((fn[0, 0], mn[0], fn[0, 1], fn[1, 0], mn[1], fn[1, 1])):
        put(V_G[n], x)
    put(V_GQL, v["mla_g_q_lat"][0])
    put(V_GKV, v["mla_g_kv_lat"][0])
    for col, x in ((V_GQN, v["mla_g_qn"][0]), (V_GKN, v["mla_g_kn"][0])):
        put(col, x[:NOPE])
        put(col + 1, x[NOPE:])
    out[:, V_EPS], out[:, V_LNEPS] = EPS, LN_EPS
    put(V_MU, v["rwkv_mu"][0])
    for col, name in ((V_W0, "w0"), (V_A0, "a0"), (V_KK, "k_k"), (V_KA, "k_a"), (V_RK, "r_k"), (V_LW, "lnx_w"), (V_LB, "lnx_b")):
        put(col, v[f"rwkv_{name}"][0])
    return out


def _constants():
    c = np.zeros((P, NCONST), np.float32)
    c[:, C_ID:C_ID + P] = np.eye(P)
    c[:, C_ONE:C_ONE + P] = 1.0
    c[:, C_BLK:C_BLK + P] = np.kron(np.eye(2), np.ones((HS, HS)))
    c[:, C_FOLD:C_FOLD + 64] = np.concatenate([np.eye(64), np.eye(64)])
    pos = np.concatenate([np.arange(SEQ), np.tile(PAGES * PAGE + np.arange(SQ), SB)]).astype(np.float32)
    inv = (np.float32(10000.0) ** (-np.arange(0, ROPE, 2, dtype=np.float32) / np.float32(ROPE))).astype(np.float32)
    ang = pos[None, :] * inv[:, None]
    cos, sin = np.cos(ang), np.sin(ang)
    rope = np.concatenate([cos, cos, -sin, sin]).astype(np.float32)
    i = np.arange(P)
    causal = np.where(i[:, None] >= i[None, :], 0.0, -1e30).astype(np.float32)
    t = np.arange(NS)
    new = (t[:, None, None, None] // SQ == np.arange(SB)[None, :, None, None]) & \
          (t[:, None, None, None] % SQ <= np.arange(SQ)[None, None, None, :])
    new = np.broadcast_to(new, (NS, SB, H, SQ))
    new = np.where(new, 0.0, -1e30).astype(np.float32).reshape(NS, NS * H)
    new = np.concatenate([np.full((P - NS, NS * H), -1e30, np.float32), new])
    s, t = np.meshgrid(np.arange(CH), np.arange(CH), indexing="ij")
    rc = np.zeros((P, NRC), np.float32)
    two = lambda x: np.tile(x.astype(np.float32), (2, 1))
    for c_ in range(NC_):
        same = (s // SQ == t // SQ) if c_ == NC_ - 1 else np.ones_like(s, bool)
        rc[:, R_GRAM + P * c_:R_GRAM + P * c_ + CH] = two((s < t) & same)
        rc[:, R_GRAM + P * c_ + CH:R_GRAM + P * (c_ + 1)] = two((s <= t) & same)
        rc[:, R_LOW + CH * c_:R_LOW + CH * (c_ + 1)] = two((t < s) & same)
    rc[:, R_B8:R_B8 + CH] = two(s // 8 == t // 8)
    for n, b in enumerate((8, 16, 32)):
        rc[:, R_OFF + CH * n:R_OFF + CH * (n + 1)] = two((s // b != t // b) & (s // (2 * b) == t // (2 * b)))
    rc[:, R_SCAN:R_SCAN + T] = np.concatenate([np.arange(SEQ) % CH != 0, np.arange(NS) % SQ != 0])[None, :]
    rc[:, R_SEQ:R_SEQ + SB] = two(np.arange(CH)[:, None] // SQ == np.arange(SB)[None, :])
    return c, rope, causal, new, rc


def _arrays(v):
    feat = lambda x: np.ascontiguousarray(x.reshape(-1, KD, P).transpose(2, 1, 0))
    c, rope, causal, new, rc = _constants()
    l1 = [v[f"rwkv_{n}"][0].reshape(KD, P, -1).transpose(1, 0, 2) for n in ("w1", "a1", "g1")]
    l1 = np.concatenate([np.concatenate(l1[:2], axis=2).reshape(P, -1), l1[2].reshape(P, -1)], axis=1)
    l2 = np.concatenate([np.concatenate([v["rwkv_w2"][0], v["rwkv_a2"][0]]), v["rwkv_g2"][0]], axis=1)
    return {
        "x": feat(np.concatenate([v["x_prompt"].reshape(SEQ, D), v["x_sample"].reshape(NS, D)])),
        "w": _weights(v),
        "vec": _vectors(v),
        "const": c, "rope": rope, "causal": causal, "newmask": new, "rc": rc,
        "ukt": np.ascontiguousarray(v["mla_w_uk"][0].transpose(2, 1, 0)),
        "lora1": l1, "lora2": l2,
        "cache_c": v["cache_kv_latent"][0], "cache_kr": v["cache_k_rope"][0],
        "pages": v["page_table"].reshape(1, -1),
        "state": np.ascontiguousarray(v["state_wkv"][0].reshape(SB, KD, 2, HS, HS).transpose(1, 2, 4, 0, 3).reshape(KD, P, SB, HS)),
        "shift": feat(v["state_shift"][0]),
    }


_OUTS = {"y": [P, KD, T], "lat": [P, KV_T, T], "kr": [ROPE, T], "wkv_p": [KD, P, HS], "wkv_s": [KD, P, SB, HS], "shift_o": [P, KD, 1 + SB]}


def kernel(**inputs):
    import concourse.bacc as bacc
    from concourse.bass_utils import run_bass_kernel_spmd

    nc = bacc.Bacc("TRN2", target_bir_lowering=False, num_devices=1)
    arrays = {k: np.ascontiguousarray(x) for k, x in _arrays({k: np.asarray(x) for k, x in inputs.items()}).items()}
    a = {k: nc.dram_tensor(f"in_{k}", x.shape, mybir.dt.from_np(x.dtype), kind="ExternalInput").ap() for k, x in arrays.items()}
    o = {k: nc.dram_tensor(f"out_{k}", s, F32, kind="ExternalOutput").ap() for k, s in _OUTS.items()}
    program(nc, a, o)
    r = run_bass_kernel_spmd(nc, [{f"in_{k}": x for k, x in arrays.items()}], core_ids=[0]).results[0]
    g = {k: r[f"out_{k}"] for k in _OUTS}
    tokens = lambda x: x.transpose(2, 1, 0).reshape(x.shape[2], -1)
    y, lat, kr, sh = tokens(g["y"]), tokens(g["lat"]), g["kr"].T, tokens(g["shift_o"])
    wp = g["wkv_p"].reshape(KD, 2, HS, HS).transpose(0, 1, 3, 2).reshape(1, 1, 2 * KD, HS, HS)
    ws = g["wkv_s"].reshape(KD, 2, HS, SB, HS).transpose(3, 0, 1, 4, 2).reshape(1, SB, 2 * KD, HS, HS)
    return (y[:SEQ].reshape(1, SEQ, D), y[SEQ:].reshape(SB, SQ, D),
            lat[:SEQ].reshape(1, 1, SEQ, KV), kr[:SEQ].reshape(1, 1, SEQ, ROPE), wp, sh[:1].reshape(1, 1, D),
            lat[SEQ:].reshape(1, SB, SQ, KV), kr[SEQ:].reshape(1, SB, SQ, ROPE), ws, sh[1:].reshape(1, SB, D))
```

```python
import numpy as np
import concourse.bass as bass
from concourse import mybir
from contextlib import ExitStack

F32 = mybir.dt.float32
F32R = mybir.dt.float32r
I32 = mybir.dt.int32
ACT = mybir.ActivationFunctionType
ALU = mybir.AluOpType
AX = mybir.AxisListType

P = 128
D = 1024
KD = D // P
SEQ = 512
SB, SQ = 8, 8
NS = SB * SQ
T = SEQ + NS
HT = T // 2
FF = 2816
FT = FF // P
PARTS = (12, 10)
NFFN = 4
H = 8
QK, NOPE, ROPE, VD = 192, 128, 64, 128
QR_T, KV_T = 3, 2
KV = KV_T * P
PAGE, PAGES, POOL = 128, 16, 160
SCALE = QK ** -0.5
EPS = 1e-6
LN_EPS = 64e-5
HS = 64
CH = 64
NC = T // CH
ITEM = 16 * P

N_FFN = sum(PARTS) + 2 * KD
I_FFN0 = 0
I_LAT = I_FFN0 + N_FFN
I_UQ = I_LAT + 3
I_UK = I_UQ + H
I_UV = I_UK + 1
I_MO = I_UV + 1
I_FFN1 = I_MO + 4
I_FFN2 = I_FFN1 + N_FFN
I_R = I_FFN2 + N_FFN
I_K = I_R + 4
I_V = I_K + 4
I_RO = I_V + 4
I_FFN3 = I_RO + 4
N_ITEMS = I_FFN3 + N_FFN
I_FFN = (I_FFN0, I_FFN1, I_FFN2, I_FFN3)
NORM_OF_FFN = (0, 2, 3, 5)
XHAT_OF_NORM = {0: 0, 1: 1, 2: 2, 3: 3, 5: 4}

V_G = {n: 8 * n for n in range(6)}
V_GQL, V_GKV = 48, 51
V_GQN, V_GQR, V_GKN, V_GKR = 53, 54, 55, 56
V_EPS, V_LNEPS = 57, 58
V_MU = 64
V_W0, V_A0, V_KK, V_KA, V_RK, V_LW, V_LB = (112 + 8 * n for n in range(7))
NV = 168
N_STAGE_SEMS = 120
C_ID, C_ONE, C_BLK, C_FOLD = 0, 128, 256, 384
NCONST = 448
R_GRAM, R_LOW, R_B8, R_OFF, R_SCAN, R_SEQ = 0, 1152, 1728, 1792, 1984, 2560
NRC = 2568


class Map:

    def __init__(self, nc, base):
        self.nc, self.base = nc, base

    def at(self, name, col, shape, dtype=F32):
        return self.nc.alloc_sbuf_tensor_at(name, [P] + list(shape), dtype, offset=self.base + 4 * col)


def program(nc, a, o):
    ctx = ExitStack()

    def sem(name):
        return ctx.enter_context(nc.semaphore(name))

    shared = [ctx.enter_context(nc.semaphore(f"stage_{k}")) for k in range(N_STAGE_SEMS)]
    taken = {"attention": 0, "recurrence": 0}

    def stage_sem(stage, name):
        taken[stage] += 1
        return shared[taken[stage] - 1]

    m = Map(nc, -(-nc.sbuf_base // 32) * 32)

    X = m.at("X", 0, [KD, T])
    XH = m.at("XH", 4608, [KD, T], F32R)
    XL = m.at("XL", 9216, [KD, T], F32R)
    RAW = [m.at(f"RAW{s}", 13824 + 2048 * s, [ITEM]) for s in range(2)]
    WH = [m.at(f"WH{s}", 17920 + 2048 * s, [ITEM], F32R) for s in range(2)]
    WL = [m.at(f"WL{s}", 22016 + 2048 * s, [ITEM], F32R) for s in range(2)]
    RSTD = m.at("RSTD", 26112, [T])
    T1 = m.at("T1", 26688, [T])
    T2 = m.at("T2", 27264, [T])
    T3 = m.at("T3", 27840, [T])
    T4 = m.at("T4", 28416, [T])
    SQT = m.at("SQT", 28992, [T])
    SQACC = m.at("SQACC", 29568, [T])
    CONST = m.at("CONST", 30144, [NCONST])
    VEC = m.at("VEC", 30592, [NV])
    IDENT = CONST[:, C_ID:C_ID + P]
    ONES = CONST[:, C_ONE:C_ONE + P]
    BLK = CONST[:, C_BLK:C_BLK + P]
    FOLD = CONST[:, C_FOLD:C_FOLD + 64]
    A0 = 30800
    HH = m.at("HH", A0, [PARTS[0], T], F32R)
    HL = m.at("HL", A0 + PARTS[0] * T, [PARTS[0], T], F32R)

    PS = ctx.enter_context(nc.psum_tensor("PS", [P, 2, 4, 512], F32))

    def vec(c, rows=P):
        return VEC[0:rows, c:c + 1] if isinstance(c, int) else VEC[0:rows, bass.ds(c, 1)]

    def halves(ap):
        return ap.rearrange("p (a t) -> p a t", a=2)

    def banks(s, b, rows=P):
        return PS[0:rows, s, b:b + 2, 0:HT]

    const_in = sem("const_in")
    waits_passed = sem("waits_passed")
    x_in = sem("x_in")
    raw_in = [sem("raw_in_even"), sem("raw_in_odd")]
    rounded = sem("rounded")
    item_split = sem("item_split")
    multiplied = sem("multiplied")
    evacuated = sem("evacuated")
    xhat_hi = sem("xhat_hi")
    xhat_split = sem("xhat_split")
    sq_zero = sem("sq_zero")
    sq_tile = sem("sq_tile")
    sq_added = sem("sq_added")
    sum_sq = sem("sum_sq")
    root = sem("root")
    rstd_ok = sem("rstd_ok")
    gate_scaled = sem("gate_scaled")
    silu_done = sem("silu_done")
    hidden = sem("hidden")
    hidden_hi = sem("hidden_hi")
    hidden_split = sem("hidden_split")
    stored = sem("stored")
    stage_end = sem("stage_end")
    CREDIT = 2

    def barrier(eng, count):
        eng.drain().then_inc(stage_end, 1)
        eng.wait_ge(stage_end, 4 * count)

    block = ctx.enter_context(nc.Block())

    def load_items(sp, first, count, blocks, peel=0):
        for n in range(first, first + peel):
            sp.dma_start(RAW[n % 2][:, 0:blocks * P], a["w"][n, :, 0:blocks * P]).then_inc(raw_in[n % 2], 16)
        first, count = first + peel, count - peel
        if count >= 2:
            with sp.Fori(0, count // 2) as pair:
                i = pair * 2
                for u in range(2):
                    n = first + u
                    sp.wait_ge(item_split, n - 1 + i)
                    sp.dma_start(RAW[n % 2][:, 0:blocks * P].rearrange("p (o c) -> p o c", o=1),
                                 a["w"][bass.ds(n + i, 1), :, 0:blocks * P].rearrange("o p c -> p o c")).then_inc(raw_in[n % 2], 16)
        if count % 2:
            n = first + count - 1
            sp.wait_ge(item_split, n - 1)
            sp.dma_start(RAW[n % 2][:, 0:blocks * P], a["w"][n, :, 0:blocks * P]).then_inc(raw_in[n % 2], 16)

    def round_item(act, n, i=0):
        act.wait_ge(raw_in[n % 2], 16 * (n // 2 + 1) + 8 * i)
        if n >= 2:
            act.wait_ge(multiplied, n - 1 + i)
        act.activation(WH[n % 2][:], RAW[n % 2][:], ACT.Copy).then_inc(rounded, 1)

    def split_item(dve, n, i=0):
        dve.wait_ge(rounded, n + 1 + i)
        dve.tensor_tensor(WL[n % 2][:], RAW[n % 2][:], WH[n % 2][:].bitcast(F32), ALU.subtract).then_inc(item_split, 1)

    def multiply_item(pe, n, i, k_tiles, tiles, hi, lo, before=lambda k: None, cols=P):
        s = n % 2
        pe.wait_ge(item_split, n + 1 + i)
        pe.wait_ge(evacuated, n - 1 + CREDIT + i)
        for t in range(tiles):
            for k in range(k_tiles):
                if t == 0:
                    before(k)
                c = (t * k_tiles + k) * P
                for p, (w, x) in enumerate(((WH, hi), (WH, lo), (WL, hi))):
                    for half in range(2):
                        mm = pe.matmul(PS[:, s, 2 * t + half, 0:HT], w[s][:, c:c + P],
                                       x[:, k, half * HT:(half + 1) * HT],
                                       start=(k == 0 and p == 0), stop=(k == k_tiles - 1 and p == 2))
        mm.then_inc(multiplied, 1)

    def xhat_tile(act, dve, norm, d):
        j = 8 * XHAT_OF_NORM[norm] + d + 1
        g = vec(d + V_G[norm])
        one = slice(d, d + 1) if isinstance(d, int) else bass.ds(d, 1)
        if act is not None:
            act.activation(XH[:, one, :], X[:, one, :], ACT.Copy, scale=g).then_inc(xhat_hi, 1)
        if dve is not None:
            dve.wait_ge(xhat_hi, j)
            dve.scalar_tensor_tensor(out=XL[:, one, :], in0=X[:, one, :], scalar=g, in1=XH[:, one, :].bitcast(F32),
                                     op0=ALU.mult, op1=ALU.subtract).then_inc(xhat_split, 1)

    def square_tile(pool, norm, d):
        one = slice(d, d + 1) if isinstance(d, int) else bass.ds(d, 1)
        x = X[:, one, :].rearrange("p o t -> p (o t)")
        pool.wait_ge(sq_added, 8 * norm + d)
        pool.tensor_tensor(SQT[:], x, x, ALU.mult).then_inc(sq_tile, 1)
        pool.wait_ge(sq_tile, 8 * norm + d + 1)
        pool.tensor_tensor(SQACC[:], SQACC[:], SQT[:], ALU.add).then_inc(sq_added, 1)

    def zero_squares(pool, norm):
        if norm:
            pool.wait_ge(sum_sq, norm)
        pool.memset(SQACC[:], 0.0).then_inc(sq_zero, 1)
        pool.wait_ge(sq_zero, norm + 1)

    def norm_sums(pe, norm, s):
        pe.wait_ge(sq_added, 8 * (norm + 1))
        for half in range(2):
            mm = pe.matmul(PS[:, s, 2 + half, 0:HT], ONES, SQACC[:, half * HT:(half + 1) * HT], start=True, stop=True)
        mm.then_inc(sum_sq, 1)

    def norm_root(act, norm, s):
        act.wait_ge(sum_sq, norm + 1)
        act.activation(halves(RSTD[:]), banks(s, 2), ACT.Sqrt, bias=vec(V_EPS), scale=1.0 / D).then_inc(root, 1)

    def norm_rstd(dve, norm):
        dve.wait_ge(root, norm + 1)
        dve.reciprocal(RSTD[:], RSTD[:]).then_inc(rstd_ok, 1)

    def hidden_steps(f):
        n, j = I_FFN[f], FT * f
        for cnt in PARTS:
            yield n, cnt, j
            n, j = n + cnt + KD, j + cnt

    def ffn_sp(sp, f):
        for n, cnt, _ in hidden_steps(f):
            load_items(sp, n, cnt, 16, peel=2 if n == 0 else 0)
            load_items(sp, n + cnt, KD, cnt)

    def ffn_pe(pe, f):
        norm = NORM_OF_FFN[f]
        base = 8 * XHAT_OF_NORM[norm]
        norm_sums(pe, norm, (I_FFN[f] + 1) % 2)
        for n, cnt, j in hidden_steps(f):
            with pe.Fori(0, cnt // 2) as pair:
                i = pair * 2
                for u in range(2):
                    if u:
                        pe.wait_ge(root, norm + 1)
                    multiply_item(pe, n + u, i, KD, 2, XH, XL,
                                  before=lambda k: pe.wait_ge(xhat_split, base + k + 1))
            with pe.Fori(0, KD // 2) as pair:
                i = pair * 2
                for u in range(2):
                    multiply_item(pe, n + cnt + u, i, cnt, 1, HH, HL,
                                  before=lambda k: pe.wait_ge(hidden_split, j + k + 1))

    def ffn_act(act, f, next_norm, last=False):
        norm_root(act, NORM_OF_FFN[f], (I_FFN[f] + 1) % 2)
        for part, (n, cnt, j) in enumerate(hidden_steps(f)):
            with act.Fori(0, cnt // 2) as pair:
                i = pair * 2
                for u in range(2):
                    round_item(act, n + u + 1, i)
                    act.wait_ge(gate_scaled, j + u + 1 + i)
                    act.activation(T4[:], T1[:], ACT.Silu).then_inc(silu_done, 1)
                    act.wait_ge(hidden, j + u + 1 + i)
                    act.activation(HH[:, bass.ds(i + u, 1), :].rearrange("p o t -> p (o t)"), T3[:], ACT.Copy).then_inc(hidden_hi, 1)
            n += cnt
            final = part == 1
            end = KD - 2 if final and last else KD
            with act.Fori(0, end // 2) as pair:
                i = pair * 2
                for u in range(2):
                    round_item(act, n + u + 1, i)
                    if final and next_norm is not None and next_norm in XHAT_OF_NORM:
                        act.wait_ge(evacuated, n + u + 1 + CREDIT + i)
                        xhat_tile(act, None, next_norm, i + u)
            if final and last:
                round_item(act, n + KD - 1)

    def ffn_dve(dve, f, next_norm, last=False):
        norm_rstd(dve, NORM_OF_FFN[f])
        dve.wait_ge(rstd_ok, NORM_OF_FFN[f] + 1)
        for part, (n, cnt, j) in enumerate(hidden_steps(f)):
            with dve.Fori(0, cnt // 2) as pair:
                i = pair * 2
                for u in range(2):
                    s = (n + u) % 2
                    split_item(dve, n + u + 1, i)
                    dve.wait_ge(multiplied, n + u + 1 + i)
                    dve.tensor_tensor(halves(T1[:]), banks(s, 0), halves(RSTD[:]), ALU.mult).then_inc(gate_scaled, 1)
                    dve.tensor_tensor(halves(T2[:]), banks(s, 2), halves(RSTD[:]), ALU.mult).then_inc(evacuated, 1)
                    dve.wait_ge(silu_done, j + u + 1 + i)
                    dve.wait_ge(evacuated, n + u + 1 + CREDIT + i)
                    dve.tensor_tensor(T3[:], T4[:], T2[:], ALU.mult).then_inc(hidden, 1)
                    dve.wait_ge(hidden_hi, j + u + 1 + i)
                    dve.tensor_tensor(HL[:, bass.ds(i + u, 1), :].rearrange("p o t -> p (o t)"), T3[:],
                                      HH[:, bass.ds(i + u, 1), :].rearrange("p o t -> p (o t)").bitcast(F32),
                                      ALU.subtract).then_inc(hidden_split, 1)
            n += cnt
            final = part == 1

            def down(u, i, more=True):
                s = (n + u) % 2
                if more:
                    split_item(dve, n + u + 1, i)
                dve.wait_ge(multiplied, n + u + 1 + i)
                x = X[:, bass.ds(i + u, 1), :] if not isinstance(i, int) else X[:, i + u:i + u + 1, :]
                x = x.rearrange("p o (a t) -> p (o a) t", a=2)
                dve.scalar_tensor_tensor(out=x, in0=banks(s, 0), scalar=0.5, in1=x,
                                         op0=ALU.mult, op1=ALU.add).then_inc(evacuated, 1)
                if final and next_norm is not None and next_norm in XHAT_OF_NORM:
                    xhat_tile(None, dve, next_norm, i + u)

            end = KD - 2 if final and last else KD
            with dve.Fori(0, end // 2) as pair:
                i = pair * 2
                for u in range(2):
                    down(u, i)
            if final and last:
                down(0, KD - 2)
                down(1, KD - 2, more=False)

    def norm_pool(pool, norm, first_item, tiles=1):
        zero_squares(pool, norm)
        with pool.Fori(0, KD // tiles, 1) as i:
            pool.wait_ge(evacuated, first_item + 1 + CREDIT + i)
            for u in range(tiles):
                square_tile(pool, norm, i * tiles + u)

    KC = m.at("KC", A0, [KV_T, T])
    CH_ = m.at("CH_", A0 + 1152, [KV_T, T], F32R)
    CL_ = m.at("CL_", A0 + 2304, [KV_T, T], F32R)
    KR = m.at("KR", A0 + 3456, [T])
    QN = m.at("QN", A0 + 4032, [H, T])
    QR = m.at("QR", A0 + 8640, [H, T])
    LAT = m.at("LAT", A0 + 13248, [6, T])
    CQH = m.at("CQH", A0 + 16704, [QR_T, T], F32R)
    CQL = m.at("CQL", A0 + 18432, [QR_T, T], F32R)
    SQL = m.at("SQL", A0 + 16704, [5, T])
    TAB = m.at("TAB", A0 + 20160, [T])
    B0 = A0 + 13248
    QS = m.at("QS", B0, [T])
    QSR = m.at("QSR", B0 + 576, [T])
    KS = m.at("KS", B0 + 1152, [SEQ])
    KSR = m.at("KSR", B0 + 1664, [SEQ])
    WKH = m.at("WKH", B0 + 2176, [KV_T, P], F32R)
    WKL = m.at("WKL", B0 + 2432, [KV_T, P], F32R)
    VS = m.at("VS", B0 + 2688, [4, P])
    UKT = m.at("UKT", B0 + 3200, [KV])
    PB = m.at("PB", B0 + 3456, [4, SEQ])
    PT = m.at("PT", B0 + 5504, [4, SEQ])
    QA = m.at("QA", B0 + 7552, [KV_T, SB, H, SQ])
    QRS = m.at("QRS", B0 + 8576, [SB, H, SQ])
    CAUSAL = m.at("CAUSAL", 28416 + 128, [P])
    QG = m.at("QG", 28416, [NS])
    SMALL = m.at("SMALL", 30760, [40])
    NMAX, RSUM = SMALL[:, 0:4], SMALL[:, 4:8]
    CN = m.at("CN", A0 + 4032, [KV])
    SNEW = m.at("SNEW", A0 + 4288, [SB, H, SQ])
    QH = m.at("QH", A0 + 4800, [3, SB, H * SQ], F32R)
    QL = m.at("QL", A0 + 6336, [3, SB, H * SQ], F32R)
    SQH = [m.at(f"SQH{s}", 28992 + 192 * s, [3, H * SQ], F32R) for s in range(2)]
    SQL_ = [m.at(f"SQL{s}", 29696 + 192 * s, [3, H * SQ], F32R) for s in range(2)]
    ROWS = [m.at(f"ROWS{s}", A0 + 7872 + 5120 * s, [PAGES, KV + ROPE]) for s in range(2)]
    CTH = [m.at(f"CTH{s}", A0 + 18112 + 384 * s, [3 * P], F32R) for s in range(2)]
    CTL = [m.at(f"CTL{s}", A0 + 18880 + 384 * s, [3 * P], F32R) for s in range(2)]
    SC = [m.at(f"SC{s}", A0 + 19648 + 1088 * s, [PAGES + 1, H * SQ]) for s in range(2)]
    SQ2 = m.at("SQ2", 26688, [2, 512])
    SS = [m.at(f"SS{s}", 27840 + 128 * s, [PAGES, H]) for s in range(2)]
    KSS = [m.at(f"KSS{s}", 28096 + 16 * s, [PAGES]) for s in range(2)]
    MXP = m.at("MXP", 28128, [H * SQ])
    MXC = m.at("MXC", 28192, [8])
    DG = m.at("DG", 28200, [H * SQ])
    PSUMS = m.at("PSUMS", 28264, [H * SQ])
    RDEN = m.at("RDEN", 28328, [H * SQ])
    QZT = m.at("QZT", 28416, [SB * H * SQ])
    SSN = m.at("SSN", 29384, [8])
    OL = m.at("OL", A0, [KV_T, H, SB, SQ])
    OLH = m.at("OLH", A0 + 1152, [KV_T, H * NS], F32R)
    OLL = m.at("OLL", A0 + 2304, [KV_T, H * NS], F32R)

    lat_ok = stage_sem("attention", "lat_ok")
    lat_sq = stage_sem("attention", "lat_sq")
    lat_sums = stage_sem("attention", "lat_sums")
    lat_root = stage_sem("attention", "lat_root")
    lat_rs = stage_sem("attention", "lat_rs")
    lat_norm = stage_sem("attention", "lat_norm")
    lat_hi = stage_sem("attention", "lat_hi")
    lat_split = stage_sem("attention", "lat_split")
    tab_in = stage_sem("attention", "tab_in")
    kr_tab = stage_sem("attention", "kr_tab")
    kr_fold = stage_sem("attention", "kr_fold")
    kr_ok = stage_sem("attention", "kr_ok")
    uv_ok = stage_sem("attention", "uv_ok")
    causal_in = stage_sem("attention", "causal_in")
    kr_sq = stage_sem("attention", "kr_sq")
    slices = stage_sem("attention", "slices")
    ukt_in = stage_sem("attention", "ukt_in")
    q_fold = stage_sem("attention", "q_fold")
    q_rope = stage_sem("attention", "q_rope")
    q_sq = stage_sem("attention", "q_sq")
    q_sums = stage_sem("attention", "q_sums")
    q_root = stage_sem("attention", "q_root")
    q_rs = stage_sem("attention", "q_rs")
    q_ok = stage_sem("attention", "q_ok")
    q_gain = stage_sem("attention", "q_gain")
    qa_mm = stage_sem("attention", "qa_mm")
    qa_ok = stage_sem("attention", "qa_ok")
    k_mm = stage_sem("attention", "k_mm")
    k_sq = stage_sem("attention", "k_sq")
    k_sums = stage_sem("attention", "k_sums")
    k_root = stage_sem("attention", "k_root")
    k_rs = stage_sem("attention", "k_rs")
    k_ok = stage_sem("attention", "k_ok")
    v_mm = stage_sem("attention", "v_mm")
    v_ok = stage_sem("attention", "v_ok")
    s_mm = stage_sem("attention", "s_mm")
    s_mask = stage_sem("attention", "s_mask")
    s_max = stage_sem("attention", "s_max")
    s_neg = stage_sem("attention", "s_neg")
    p_exp = stage_sem("attention", "p_exp")
    p_inv = stage_sem("attention", "p_inv")
    p_ok = stage_sem("attention", "p_ok")
    p_t = stage_sem("attention", "p_t")
    pt_act = stage_sem("attention", "pt_act")
    pt_dve = stage_sem("attention", "pt_dve")
    o_mm = stage_sem("attention", "o_mm")
    o_hi = stage_sem("attention", "o_hi")
    o_split = stage_sem("attention", "o_split")
    uk_, uv_ = I_UK % 2, I_UV % 2
    UKH, UKL = WH[uk_], WL[uk_]
    UVH, UVL = WH[uv_], WL[uv_]

    def bank(b, rows=slice(0, P)):
        return PS[rows, b // 4, b % 4, :]

    def lat_sp(sp):
        load_items(sp, I_LAT, 3, 16)
        sp.wait_ge(evacuated, I_LAT + CREDIT)
        sp.dma_start(TAB[:], a["rope"]).then_inc(tab_in, 16)
        load_items(sp, I_UQ, H, 6)
        load_items(sp, I_UK, 2, 16)

    def lat_pe(pe):
        norm_sums(pe, 1, (I_LAT + 1) % 2)
        for u in range(3):
            if u:
                pe.wait_ge(root, 2)
            multiply_item(pe, I_LAT + u, 0, KD, 2, XH, XL, before=lambda k: pe.wait_ge(xhat_split, 8 + k + 1))
        pe.wait_ge(evacuated, I_UQ + CREDIT)
        pe.wait_ge(lat_sq, 5)
        for half in range(2):
            for t in range(5):
                mm = pe.matmul(PS[:, 0, (0 if t < QR_T else 2) + half, 0:HT], ONES, SQL[:, t, half * HT:(half + 1) * HT],
                               start=t in (0, QR_T), stop=t in (QR_T - 1, 4))
        mm.then_inc(lat_sums, 1)
        pe.wait_ge(kr_tab, 1)
        for half in range(2):
            mm = pe.matmul(PS[0:64, 1, half, 0:HT], FOLD, T3[:, half * HT:(half + 1) * HT], start=True, stop=True)
        mm.then_inc(kr_fold, 1)
        pe.wait_ge(kr_ok, 1)
        with pe.Fori(0, H // 2) as pair:
            i = pair * 2
            for u in range(2):
                multiply_item(pe, I_UQ + u, i, QR_T, 2, CQH, CQL, before=lambda k: pe.wait_ge(lat_split, k + 1))

    def lat_act(act):
        norm_root(act, 1, (I_LAT + 1) % 2)
        for u in range(3):
            round_item(act, I_LAT + u + 1)
            for t in range(2 * u, min(2 * u + 2, 5)):
                act.wait_ge(lat_ok, t + 1)
                act.activation(SQL[:, t, :], LAT[:, t, :], ACT.Square).then_inc(lat_sq, 1)
        act.wait_ge(lat_sums, 1)
        act.activation(halves(T1[:]), banks(0, 0), ACT.Sqrt, bias=vec(V_EPS), scale=1.0 / (QR_T * P)).then_inc(lat_root, 1)
        act.activation(halves(T2[:]), banks(0, 2), ACT.Sqrt, bias=vec(V_EPS), scale=1.0 / KV).then_inc(lat_root, 1)
        act.wait_ge(kr_fold, 1)
        act.activation(halves(KR[0:64, :]), banks(1, 0, 64), ACT.Copy).then_inc(kr_ok, 1)
        for t in range(5):
            act.wait_ge(lat_norm, t + 1)
            if t < QR_T:
                act.activation(CQH[:, t, :], T3[:] if t % 2 == 0 else T4[:], ACT.Copy).then_inc(lat_hi, 1)
            else:
                act.activation(CH_[:, t - QR_T, :], KC[:, t - QR_T, :], ACT.Copy).then_inc(lat_hi, 1)
        with act.Fori(0, H // 2) as pair:
            i = pair * 2
            for u in range(2):
                round_item(act, I_UQ + u + 1, i)
        round_item(act, I_UV)

    def lat_dve(dve):
        norm_rstd(dve, 1)
        dve.wait_ge(rstd_ok, 2)
        for u in range(3):
            split_item(dve, I_LAT + u + 1)
            dve.wait_ge(multiplied, I_LAT + u + 1)
            s = (I_LAT + u) % 2
            dve.tensor_tensor(halves(LAT[:, 2 * u, :]), banks(s, 0), halves(RSTD[:]), ALU.mult).then_inc(lat_ok, 1)
            dve.tensor_tensor(halves(LAT[:, 2 * u + 1, :]), banks(s, 2), halves(RSTD[:]), ALU.mult).then_inc(lat_ok, 1)
            dve.wait_ge(lat_ok, 2 * u + 2)
            dve.sem_inc(evacuated, 1)
        dve.wait_ge(tab_in, 16)
        dve.tensor_tensor(T3[:], LAT[:, 5, :], TAB[:], ALU.mult).then_inc(kr_tab, 1)
        for n, t in enumerate((T1, T2)):
            dve.wait_ge(lat_root, n + 1)
            dve.reciprocal(t[:], t[:]).then_inc(lat_rs, 1)
        dve.wait_ge(lat_rs, 2)
        dve.wait_ge(kr_fold, 1)
        for t in range(5):
            f = (T3 if t % 2 == 0 else T4)[:] if t < QR_T else KC[:, t - QR_T, :]
            if t == 2:
                dve.wait_ge(lat_split, 1)
            dve.scalar_tensor_tensor(out=f, in0=LAT[:, t, :], scalar=vec(V_GQL + t), in1=(T1 if t < QR_T else T2)[:],
                                     op0=ALU.mult, op1=ALU.mult).then_inc(lat_norm, 1)
            dve.wait_ge(lat_hi, t + 1)
            hi, lo = (CQH, CQL) if t < QR_T else (CH_, CL_)
            k = t if t < QR_T else t - QR_T
            dve.tensor_tensor(lo[:, k, :], f, hi[:, k, :].bitcast(F32), ALU.subtract).then_inc(lat_split, 1)
        with dve.Fori(0, H // 2) as pair:
            i = pair * 2
            for u in range(2):
                n = I_UQ + u
                split_item(dve, n + 1, i)
                dve.wait_ge(multiplied, n + 1 + i)
                one = bass.ds(i + u, 1)
                dve.tensor_copy(QN[:, one, :].rearrange("p o (a t) -> p (o a) t", a=2), banks(n % 2, 0)).then_inc(qn_ok, 1)
                dve.tensor_tensor(QR[:, one, :].rearrange("p o (a t) -> p (o a) t", a=2), banks(n % 2, 2),
                                  halves(TAB[:]), ALU.mult).then_inc(evacuated, 1)
        split_item(dve, I_UV)

    qn_ok = stage_sem("attention", "qn_ok")

    def heads_sp(sp):
        sp.dma_start(o["lat"], KC[:]).then_inc(stored, 16)
        sp.dma_start(o["kr"], KR[0:64, :]).then_inc(stored, 16)
        sp.dma_start(CAUSAL[:], a["causal"]).then_inc(causal_in, 16)
        with sp.Fori(0, H) as h:
            sp.wait_ge(qa_mm, h)
            sp.dma_start(UKT[:].rearrange("p (o r) -> p o r", o=1), a["ukt"][:, bass.ds(h, 1), :]).then_inc(ukt_in, 16)

    def heads_pool(pool):
        with pool.Fori(0, H) as h:
            pool.wait_ge(k_mm, h)
            for src, dst in ((UKH, WKH), (UKL, WKL)):
                pool.tensor_copy(dst[:], src[:].rearrange("p (k h d) -> p k h d", k=KV_T, h=H)[:, :, bass.ds(h, 1), :]
                                 .rearrange("p k o d -> p k (o d)").bitcast(F32)).then_inc(slices, 1)

    def heads_pe(pe):
        with pe.Fori(0, H) as h:
            one = bass.ds(h, 1)
            pe.wait_ge(pt_act, h * 2)
            pe.wait_ge(pt_dve, h * 2)
            for half in range(2):
                mm = pe.matmul(PS[0:64, 0, half, 0:HT], FOLD, QR[:, one, half * HT:(half + 1) * HT].rearrange("p o t -> p (o t)"),
                               start=True, stop=True)
            mm.then_inc(q_fold, 1)
            pe.wait_ge(slices, h * 2 + 2)
            n = 0
            for k in range(KV_T):
                for w, x in ((WKH, CH_), (WKH, CL_), (WKL, CH_)):
                    mm = pe.matmul(bank(4), w[:, k, :], x[:, k, 0:SEQ], start=n == 0, stop=n == 5)
                    n += 1
            mm.then_inc(k_mm, 1)
            pe.wait_ge(q_sq, h * 2 + 2)
            for half in range(2):
                w = slice(half * HT, (half + 1) * HT)
                pe.matmul(PS[:, 0, 2 + half, 0:HT], ONES, T1[:, w], start=True, stop=False)
                mm = pe.matmul(PS[:, 0, 2 + half, 0:HT], ONES[0:64, :], T2[0:64, w], start=False, stop=True)
            mm.then_inc(q_sums, 1)
            pe.wait_ge(k_sq, h + 1)
            pe.wait_ge(o_split, h)
            pe.matmul(bank(5), ONES, RSTD[:, 0:SEQ], start=True, stop=False)
            pe.matmul(bank(5), ONES[0:64, :], SQT[0:64, 0:SEQ], start=False, stop=True).then_inc(k_sums, 1)
            for t in range(4):
                n = 0
                for k in range(KV_T):
                    for x, w in ((CH_, UVH), (CH_, UVL), (CL_, UVH)):
                        rhs = w[:].rearrange("p (k h d) -> p k h d", k=KV_T, h=H)[:, k, one, :].rearrange("p o d -> p (o d)")
                        mm = pe.matmul(bank(6)[:, t * P:(t + 1) * P], x[:, k, t * P:(t + 1) * P], rhs, start=n == 0, stop=n == 5)
                        n += 1
            mm.then_inc(v_mm, 1)
            pe.wait_ge(q_gain, h * 2 + 2)
            pe.wait_ge(ukt_in, h * 16 + 16)
            for k in range(KV_T):
                mm = pe.matmul(bank(7)[:, k * NS:(k + 1) * NS], UKT[:, k * P:(k + 1) * P], QG[:], start=True, stop=True)
            mm.then_inc(qa_mm, 1)
            pe.wait_ge(k_ok, h * 2 + 2)
            pe.wait_ge(v_ok, h + 1)
            pe.wait_ge(qa_ok, h + 1)
            for b in range(4):
                q, n = slice(b * P, (b + 1) * P), (b + 1) * P
                pe.matmul(bank(4 + b)[:, 0:n], QS[:, q], KS[:, 0:n], start=True, stop=False)
                pe.matmul(bank(4 + b)[:, 0:n], QSR[0:64, q], KSR[0:64, 0:n], start=False, stop=True).then_inc(s_mm, 1)
            for b in range(4):
                pe.wait_ge(p_ok, h * 4 + b + 1)
                for k in range(b + 1):
                    mm = pe.transpose(bank(k)[:, b * P:(b + 1) * P], PB[:, b, k * P:(k + 1) * P], IDENT)
                mm.then_inc(p_t, 1)
            pe.wait_ge(pt_act, h * 2 + 2)
            pe.wait_ge(pt_dve, h * 2 + 2)
            for k in range(4):
                mm = pe.matmul(bank(5)[:, k * P:SEQ], VS[:, k, :], PT[:, k, k * P:SEQ], start=k == 0, stop=k == 3)
            mm.then_inc(o_mm, 1)

    def heads_act(act):
        act.activation(SQT[0:64, 0:SEQ], KR[0:64, 0:SEQ], ACT.Square).then_inc(kr_sq, 1)
        act.wait_ge(kr_sq, 1)
        with act.Fori(0, H) as h:
            one = bass.ds(h, 1)
            act.activation(T1[:], QN[:, one, :].rearrange("p o t -> p (o t)"), ACT.Square).then_inc(q_sq, 1)
            act.wait_ge(q_fold, h + 1)
            act.activation(halves(QSR[0:64, :]), banks(0, 0, 64), ACT.Copy).then_inc(q_rope, 1)
            act.activation(halves(T2[0:64, :]), banks(0, 0, 64), ACT.Square).then_inc(q_sq, 1)
            act.wait_ge(k_mm, h + 1)
            act.activation(RSTD[:, 0:SEQ], bank(4), ACT.Square).then_inc(k_sq, 1)
            act.wait_ge(q_sums, h + 1)
            act.activation(halves(T3[:]), banks(0, 2), ACT.Sqrt, bias=vec(V_EPS), scale=1.0 / QK).then_inc(q_root, 1)
            act.wait_ge(k_sums, h + 1)
            act.activation(T2[:, 0:SEQ], bank(5), ACT.Sqrt, bias=vec(V_EPS), scale=1.0 / QK).then_inc(k_root, 1)
            act.wait_ge(v_mm, h + 1)
            act.activation(VS[:].rearrange("p b d -> p (b d)"), bank(6), ACT.Copy).then_inc(v_ok, 1)
            act.wait_ge(qa_mm, h + 1)
            for k in range(KV_T):
                act.activation(QA[:, k, :, one, :].rearrange("p s o q -> p s (o q)"),
                               bank(7)[:, k * NS:(k + 1) * NS].rearrange("p (s q) -> p s q", s=SB), ACT.Copy).then_inc(qa_half, 1)
            act.wait_ge(qa_half, h * 2 + 2)
            act.sem_inc(qa_ok, 1)
            for b in range(4):
                act.wait_ge(s_neg, h * 4 + b + 1)
                n = (b + 1) * P
                act.activation(PB[:, b, 0:n], bank(4 + b)[:, 0:n], ACT.Exp, bias=NMAX[:, b:b + 1], scale=SCALE,
                               accum_out=RSUM[:, b:b + 1]).then_inc(p_exp, 1)
            act.wait_ge(p_t, h * 4 + 4)
            for k in range(2):
                act.activation(PT[:, k, k * P:SEQ], bank(k)[:, k * P:SEQ], ACT.Copy).then_inc(pt_act, 1)
            act.wait_ge(o_mm, h + 1)
            act.activation(XH[:, one, 0:SEQ].rearrange("p o t -> p (o t)"), bank(5), ACT.Copy).then_inc(o_hi, 1)

    qa_half = stage_sem("attention", "qa_half")

    def heads_dve(dve):
        dve.wait_ge(causal_in, 16)
        with dve.Fori(0, H) as h:
            one = bass.ds(h, 1)
            dve.wait_ge(q_root, h + 1)
            dve.reciprocal(T3[:], T3[:]).then_inc(q_rs, 1)
            dve.wait_ge(q_rs, h + 1)
            dve.scalar_tensor_tensor(out=QS[:], in0=QN[:, one, :].rearrange("p o t -> p (o t)"), scalar=vec(V_GQN), in1=T3[:],
                                     op0=ALU.mult, op1=ALU.mult).then_inc(q_ok, 1)
            dve.wait_ge(q_rope, h + 1)
            dve.scalar_tensor_tensor(out=QSR[0:64, :], in0=QSR[0:64, :], scalar=vec(V_GQR, 64), in1=T3[0:64, :],
                                     op0=ALU.mult, op1=ALU.mult).then_inc(q_ok, 1)
            dve.wait_ge(q_ok, h * 2 + 2)
            dve.tensor_scalar(QG[:], QS[:, SEQ:T], vec(V_GKN), None, ALU.mult).then_inc(q_gain, 1)
            dve.tensor_scalar(QRS[0:64, :, one, :].rearrange("p s o q -> p s (o q)"),
                              QSR[0:64, SEQ:T].rearrange("p (s q) -> p s q", s=SB), vec(V_GKR, 64), None, ALU.mult).then_inc(q_gain, 1)
            dve.wait_ge(k_root, h + 1)
            dve.reciprocal(T2[:, 0:SEQ], T2[:, 0:SEQ]).then_inc(k_rs, 1)
            dve.wait_ge(k_rs, h + 1)
            dve.scalar_tensor_tensor(out=KS[:], in0=bank(4), scalar=vec(V_GKN), in1=T2[:, 0:SEQ],
                                     op0=ALU.mult, op1=ALU.mult).then_inc(k_ok, 1)
            dve.scalar_tensor_tensor(out=KSR[0:64, :], in0=KR[0:64, 0:SEQ], scalar=vec(V_GKR, 64), in1=T2[0:64, 0:SEQ],
                                     op0=ALU.mult, op1=ALU.mult).then_inc(k_ok, 1)
            for b in range(4):
                dve.wait_ge(s_mm, h * 4 + b + 1)
                dve.tensor_tensor(bank(4 + b)[:, b * P:(b + 1) * P], bank(4 + b)[:, b * P:(b + 1) * P], CAUSAL[:], ALU.add).then_inc(s_mask, 1)
                dve.wait_ge(s_mask, h * 4 + b + 1)
                dve.tensor_reduce(NMAX[:, b:b + 1], bank(4 + b)[:, 0:(b + 1) * P], AX.X, ALU.max, negate=True).then_inc(s_max, 1)
                dve.wait_ge(s_max, h * 4 + b + 1)
                dve.tensor_scalar(NMAX[:, b:b + 1], NMAX[:, b:b + 1], SCALE, None, ALU.mult).then_inc(s_neg, 1)
            for b in range(4):
                dve.wait_ge(p_exp, h * 4 + b + 1)
                dve.reciprocal(RSUM[:, b:b + 1], RSUM[:, b:b + 1]).then_inc(p_inv, 1)
                dve.wait_ge(p_inv, h * 4 + b + 1)
                dve.tensor_scalar(PB[:, b, 0:(b + 1) * P], PB[:, b, 0:(b + 1) * P], RSUM[:, b:b + 1], None, ALU.mult).then_inc(p_ok, 1)
            dve.wait_ge(p_t, h * 4 + 4)
            for k in range(2, 4):
                dve.tensor_copy(PT[:, k, k * P:SEQ], bank(k)[:, k * P:SEQ]).then_inc(pt_dve, 1)
            dve.wait_ge(o_hi, h + 1)
            dve.tensor_tensor(XL[:, one, 0:SEQ].rearrange("p o t -> p (o t)"), bank(5),
                              XH[:, one, 0:SEQ].rearrange("p o t -> p (o t)").bitcast(F32), ALU.subtract).then_inc(o_split, 1)

    PAGES_SB = m.at("PAGES_SB", 29568, [SB * PAGES], I32)
    newmask_in = stage_sem("attention", "newmask_in")
    qz_shift = stage_sem("attention", "qz_shift")
    qz_hi = stage_sem("attention", "qz_hi")
    qz_zero = stage_sem("attention", "qz_zero")
    qz_split = stage_sem("attention", "qz_split")
    new_mm = stage_sem("attention", "new_mm")
    new_t = stage_sem("attention", "new_t")
    new_sq = stage_sem("attention", "new_sq")
    new_copy = stage_sem("attention", "new_copy")
    new_ss = stage_sem("attention", "new_ss")
    new_root = stage_sem("attention", "new_root")
    new_rs = stage_sem("attention", "new_rs")
    new_scaled = stage_sem("attention", "new_scaled")
    new_ok = stage_sem("attention", "new_ok")
    rows_in = [stage_sem("attention", "rows_in_even"), stage_sem("attention", "rows_in_odd")]
    row_t = stage_sem("attention", "row_t")
    row_hi = stage_sem("attention", "row_hi")
    row_lo = stage_sem("attention", "row_lo")
    keys_mm = stage_sem("attention", "keys_mm")
    keys_sq = stage_sem("attention", "keys_sq")
    keys_ss = stage_sem("attention", "keys_ss")
    scores_mm = stage_sem("attention", "scores_mm")
    rope_sq = stage_sem("attention", "rope_sq")
    rope_ss = stage_sem("attention", "rope_ss")
    seq_ss = stage_sem("attention", "seq_ss")
    seq_root = stage_sem("attention", "seq_root")
    seq_rs = stage_sem("attention", "seq_rs")
    seq_scaled = stage_sem("attention", "seq_scaled")
    seq_new = stage_sem("attention", "seq_new")
    seq_max = stage_sem("attention", "seq_max")
    seq_max_t = stage_sem("attention", "seq_max_t")
    seq_max_c = stage_sem("attention", "seq_max_c")
    seq_diag = stage_sem("attention", "seq_diag")
    seq_max_b = stage_sem("attention", "seq_max_b")
    seq_less = stage_sem("attention", "seq_less")
    seq_exp = stage_sem("attention", "seq_exp")
    seq_sum = stage_sem("attention", "seq_sum")
    seq_den = stage_sem("attention", "seq_den")
    seq_rden = stage_sem("attention", "seq_rden")
    seq_pv = stage_sem("attention", "seq_pv")
    seq_ol = stage_sem("attention", "seq_ol")
    ol_hi = stage_sem("attention", "ol_hi")
    ol_split = stage_sem("attention", "ol_split")
    out_mm = stage_sem("attention", "out_mm")
    out_hi = stage_sem("attention", "out_hi")
    out_split = stage_sem("attention", "out_split")
    NEW = slice(T - P, T)
    HQ = H * SQ

    def rows_sp(sp, s, i=0, first=False):
        u = s % 2
        if not first:
            sp.wait_ge(seq_pv, s - 1 + i)
        for p in range(PAGES):
            e = s * PAGES + p
            at = PAGES_SB[0:1, e:e + 1] if isinstance(i, int) else PAGES_SB[0:1, bass.ds(i * PAGES + e, 1)]
            page = sp.value_load(at, min_val=0, max_val=POOL - 1)
            sp.dma_start(ROWS[u][:, p:p + 1, 0:KV], a["cache_c"][bass.ds(page, 1), :, :].rearrange("o t r -> t o r")).then_inc(rows_in[u], 16)
            sp.dma_start(ROWS[u][:, p:p + 1, KV:KV + ROPE], a["cache_kr"][bass.ds(page, 1), :, :].rearrange("o t r -> t o r")).then_inc(rows_in[u], 16)

    def samples_sp(sp):
        sp.dma_start(SNEW[:].rearrange("p s h q -> p (s h q)"), a["newmask"]).then_inc(newmask_in, 16)
        sp.dma_start(PAGES_SB[0:1, :], a["pages"].rearrange("o n -> o n")).then_inc(pages_in, 16)
        sp.wait_ge(pages_in, 16)
        rows_sp(sp, 0, first=True)
        rows_sp(sp, 1, first=True)
        with sp.Fori(0, (SB - 2) // 2) as pair:
            for u in range(2):
                rows_sp(sp, 2 + u, pair * 2)

    pages_in = stage_sem("attention", "pages_in")
    seq_q = stage_sem("attention", "seq_q")

    def queries_pool(pool, s, i=0):
        if s >= 2:
            pool.wait_ge(scores_mm, PAGES * (s - 1) + PAGES * i)
        for q, dst in ((QH, SQH), (QL, SQL_)):
            pool.tensor_copy(dst[s % 2][:], q[:, :, bass.ds(i + s, 1), :].rearrange("p k o c -> p k (o c)").bitcast(F32)).then_inc(seq_q, 1)

    def samples_pool(pool):
        pool.wait_ge(new_ok, 1)
        queries_pool(pool, 0)
        queries_pool(pool, 1)
        with pool.Fori(0, (SB - 2) // 2) as pair:
            for u in range(2):
                queries_pool(pool, 2 + u, pair * 2)

    def page_t(pe, s, i, p):
        if p == 0:
            pe.wait_ge(rows_in[s % 2], 32 * PAGES * (s // 2 + 1) + 16 * PAGES * i)
        n = s * PAGES + p
        if n:
            pe.wait_ge(row_lo, n + PAGES * i)
        for k, c in enumerate((0, P, KV + ROPE - P)):
            mm = pe.transpose(bank(4)[:, k * P:(k + 1) * P], ROWS[s % 2][:, p, c:c + P], IDENT)
        mm.then_inc(row_t, 1)

    def page_mm(pe, s, i, p):
        n = s * PAGES + p
        u = p % 2
        pe.wait_ge(row_lo, n + 1 + PAGES * i)
        if n >= 2:
            pe.wait_ge(keys_sq, 2 * (n - 1) + 2 * PAGES * i)
        for half in range(2):
            j = 0
            for k in range(KV_T):
                for x, w in ((CTH, UKH), (CTH, UKL), (CTL, UKH)):
                    mm = pe.matmul(bank(2 * u + half), x[u][:, k * P:(k + 1) * P], w[:, k * 1024 + half * 512:k * 1024 + half * 512 + 512],
                                   start=j == 0, stop=j == 5)
                    j += 1
            mm.then_inc(keys_mm, 1)

    def page_scores(pe, s, i, p):
        n = s * PAGES + p
        u = p % 2
        if p == 0 and s:
            pe.wait_ge(seq_scaled, s + i)
        out = bank(6 + p // 8)[:, (p % 8) * HQ:(p % 8 + 1) * HQ]
        if p == 0:
            pe.wait_ge(seq_q, 2 * (s + 1) + 2 * i)
        j = 0
        for k in range(3):
            for x, w in ((CTH, SQH), (CTH, SQL_), (CTL, SQH)):
                mm = pe.matmul(out, x[u][:, k * P:(k + 1) * P], w[s % 2][:, k, :], start=j == 0, stop=j == 8)
                j += 1
        mm.then_inc(scores_mm, 1)

    def finish_pe(pe, step, s, i):
        b = bank(5)
        u = s % 2
        n = s + 1 + i
        if step == 0:
            pe.wait_ge(seq_max, n)
            if s:
                pe.wait_ge(seq_ol, n - 1)
            pe.matmul(b[0:HQ, 0:P], MXP[:], IDENT, start=True, stop=True).then_inc(seq_max_t, 1)
        if step == 1:
            pe.wait_ge(seq_diag, n)
            pe.matmul(b[:, 0:HQ], ONES[0:HQ, :], DG[0:HQ, :], start=True, stop=True).then_inc(seq_max_b, 1)
        if step == 2:
            pe.wait_ge(seq_sum, n)
            pe.matmul(b[:, HQ:2 * HQ], ONES, PSUMS[:], start=True, stop=True).then_inc(seq_den, 1)
            for k in range(KV_T):
                for t in range(PAGES + 1):
                    rows = ROWS[u][:, t, k * P:(k + 1) * P] if t < PAGES else CN[:, k * P:(k + 1) * P]
                    mm = pe.matmul(b[:, (2 + k) * HQ:(3 + k) * HQ], rows, SC[u][:, t, :], start=t == 0, stop=t == PAGES)
            mm.then_inc(seq_pv, 1)

    def page_act(act, s, i, p):
        n = s * PAGES + p
        act.wait_ge(row_t, n + 1 + PAGES * i)
        if n >= 2:
            act.wait_ge(scores_mm, n - 1 + PAGES * i)
        act.activation(CTH[p % 2][:], bank(4)[:, 0:3 * P], ACT.Copy).then_inc(row_hi, 1)

    def squares_act(act, s, i, p):
        n = s * PAGES + p
        for half in range(2):
            act.wait_ge(keys_mm, 2 * n + half + 1 + 2 * PAGES * i)
            if n:
                act.wait_ge(keys_ss, 2 * (n - 1) + half + 1 + 2 * PAGES * i)
            act.activation(SQ2[:, half, :], bank(2 * (p % 2) + half), ACT.Square).then_inc(keys_sq, 1)

    def page_dve(dve, s, i, p):
        n = s * PAGES + p
        dve.wait_ge(row_hi, n + 1 + PAGES * i)
        dve.tensor_tensor(CTL[p % 2][:], bank(4)[:, 0:3 * P], CTH[p % 2][:].bitcast(F32), ALU.subtract).then_inc(row_lo, 1)

    def sums_dve(dve, s, i, p):
        n = s * PAGES + p
        for half in range(2):
            dve.wait_ge(keys_sq, 2 * n + half + 1 + 2 * PAGES * i)
            dve.tensor_reduce(SS[s % 2][:, p, half * 4:half * 4 + 4], SQ2[:, half, :].rearrange("p (h d) -> p h d", h=4),
                              AX.X, ALU.add).then_inc(keys_ss, 1)

    def seq_ss_dve(dve, s, i):
        u, n = s % 2, s + 1 + i
        dve.wait_ge(rope_ss, n)
        dve.wait_ge(keys_ss, 2 * PAGES * (s + 1) + 2 * PAGES * i)
        dve.tensor_tensor(SS[u][:], SS[u][:], KSS[u][:].unsqueeze(2).to_broadcast([P, PAGES, H]), ALU.add).then_inc(seq_ss, 1)

    def scale_dve(dve, s, i):
        u, n = s % 2, s + 1 + i
        dve.wait_ge(seq_root, n)
        dve.reciprocal(SS[u][:], SS[u][:]).then_inc(seq_rs, 1)
        dve.wait_ge(seq_rs, n)
        dve.wait_ge(scores_mm, PAGES * (s + 1) + PAGES * i)
        dve.tensor_tensor(SC[u][:, 0:PAGES, :].rearrange("p t (h q) -> p (t h) q", h=H),
                          PS[:, 1, 2:4, :].rearrange("p b (c q) -> p (b c) q", q=SQ),
                          SS[u][:].rearrange("p t h -> p (t h)").unsqueeze(2).to_broadcast([P, PAGES * H, SQ]), ALU.mult).then_inc(seq_scaled, 1)
        dve.tensor_copy(SC[u][:, PAGES, :].rearrange("p (o c) -> p o c", o=1),
                        SNEW[:].rearrange("p s h q -> p s (h q)")[:, bass.ds(i + s, 1), :]).then_inc(seq_new, 1)
        dve.wait_ge(seq_scaled, n)
        dve.wait_ge(seq_new, n)
        dve.tensor_reduce(MXP[:], SC[u][:].rearrange("p t c -> p c t"), AX.X, ALU.max).then_inc(seq_max, 1)

    def max_dve(dve, s, i):
        n = s + 1 + i
        dve.wait_ge(seq_max_t, n)
        dve.tensor_reduce(MXC[0:HQ, 0:1], bank(5)[0:HQ, 0:P], AX.X, ALU.max).then_inc(seq_max_c, 1)
        dve.wait_ge(seq_max_c, n)
        dve.tensor_scalar(DG[0:HQ, :], IDENT[0:HQ, 0:HQ], MXC[0:HQ, 0:1], None, ALU.mult).then_inc(seq_diag, 1)

    def less_dve(dve, s, i):
        u, n = s % 2, s + 1 + i
        dve.wait_ge(seq_max_b, n)
        dve.tensor_tensor(SC[u][:], SC[u][:], bank(5)[:, 0:HQ].unsqueeze(1).to_broadcast([P, PAGES + 1, HQ]), ALU.subtract).then_inc(seq_less, 1)

    def sum_dve(dve, s, i):
        u, n = s % 2, s + 1 + i
        dve.wait_ge(seq_exp, n)
        dve.tensor_reduce(PSUMS[:], SC[u][:].rearrange("p t c -> p c t"), AX.X, ALU.add).then_inc(seq_sum, 1)

    def ol_dve(dve, s, i):
        n = s + 1 + i
        dve.wait_ge(seq_pv, n)
        dve.reciprocal(RDEN[:], bank(5)[:, HQ:2 * HQ]).then_inc(seq_rden, 1)
        dve.wait_ge(seq_rden, n)
        for k in range(KV_T):
            mm = dve.tensor_tensor(OL[:, k, :, bass.ds(i + s, 1), :].rearrange("p h o q -> p h (o q)"),
                                   bank(5)[:, (2 + k) * HQ:(3 + k) * HQ].rearrange("p (h q) -> p h q", h=H),
                                   RDEN[:].rearrange("p (h q) -> p h q", h=H), ALU.mult)
        mm.then_inc(seq_ol, 1)

    def rope_act(act, s, i):
        u = s % 2
        act.wait_ge(rows_in[u], 32 * PAGES * (s // 2 + 1) + 16 * PAGES * i)
        if s:
            act.wait_ge(keys_ss, 2 * PAGES * s + 2 * PAGES * i)
        act.activation(SQ2[:].rearrange("p a (t d) -> p (a t) d", d=ROPE), ROWS[u][:, :, KV:KV + ROPE], ACT.Square).then_inc(rope_sq, 1)
        act.wait_ge(rope_ss, s + 1 + i)

    def rope_dve(dve, s, i):
        dve.wait_ge(rope_sq, s + 1 + i)
        dve.tensor_reduce(KSS[s % 2][:], SQ2[:].rearrange("p a (t d) -> p (a t) d", d=ROPE), AX.X, ALU.add).then_inc(rope_ss, 1)

    def seq_pe(pe, s, i=0, fin=True):
        page_t(pe, s, i, 0)
        for p in range(PAGES):
            if p < PAGES - 1:
                page_t(pe, s, i, p + 1)
            page_mm(pe, s, i, p)
            if p == 1:
                page_scores(pe, s, i, 0)
            if p:
                page_scores(pe, s, i, p)
            if fin and p in (1, 2, 5):
                finish_pe(pe, (1, 2, 5).index(p), s - 1, i)

    def seq_act(act, s, i=0, fin=True):
        u, n = (s - 1) % 2, s + i
        page_act(act, s, i, 0)
        page_act(act, s, i, 1)
        if fin:
            root_act(act, s - 1, i)
        rope_act(act, s, i)
        for p in range(PAGES):
            if 0 < p < PAGES - 1:
                page_act(act, s, i, p + 1)
            squares_act(act, s, i, p)
            if fin and p == 3:
                exp_act(act, s - 1, i)

    def root_act(act, s, i):
        act.wait_ge(seq_ss, s + 1 + i)
        act.activation(SS[s % 2][:], SS[s % 2][:], ACT.Sqrt, bias=vec(V_EPS), scale=1.0 / QK).then_inc(seq_root, 1)

    def exp_act(act, s, i):
        act.wait_ge(seq_less, s + 1 + i)
        act.activation(SC[s % 2][:], SC[s % 2][:], ACT.Exp, scale=SCALE).then_inc(seq_exp, 1)

    def seq_dve(dve, s, i=0, fin=True):
        page_dve(dve, s, i, 0)
        if fin:
            seq_ss_dve(dve, s - 1, i)
        page_dve(dve, s, i, 1)
        rope_dve(dve, s, i)
        if fin:
            scale_dve(dve, s - 1, i)
        for p in range(PAGES):
            if 0 < p < PAGES - 1:
                page_dve(dve, s, i, p + 1)
            sums_dve(dve, s, i, p)
            if fin and p == 1:
                max_dve(dve, s - 1, i)
            if fin and p == 2:
                less_dve(dve, s - 1, i)
            if fin and p == 4:
                sum_dve(dve, s - 1, i)
            if fin and p == 6:
                ol_dve(dve, s - 1, i)

    def samples_pe(pe):
        pe.wait_ge(qz_split, 2)
        for half in range(2):
            j = 0
            for k in range(KV_T):
                for x, w in ((CH_, UKH), (CH_, UKL), (CL_, UKH)):
                    pe.matmul(bank(half), x[:, k, NEW], w[:, k * 1024 + half * 512:k * 1024 + half * 512 + 512], start=j == 0, stop=j == 5)
                    j += 1
        j = 0
        for k in range(KV_T):
            for x, w in ((CH_, QH), (CH_, QL), (CL_, QH)):
                pe.matmul(bank(2), x[:, k, NEW], w[:, k].rearrange("p s c -> p (s c)"), start=j == 0, stop=False)
                j += 1
        pe.matmul(bank(2), KR[0:64, NEW], QRS[0:64].rearrange("p s h q -> p (s h q)"), start=False, stop=True).then_inc(new_mm, 1)
        for k in range(KV_T):
            pe.transpose(bank(3)[:, k * P:(k + 1) * P], KC[:, k, NEW], IDENT)
        pe.transpose(bank(3)[:, KV:KV + ROPE], KR[0:64, NEW], IDENT[0:64, 0:64]).then_inc(new_t, 1)
        pe.wait_ge(new_ok, 1)
        seq_pe(pe, 0, fin=False)
        with pe.Fori(0, (SB - 2) // 2) as pair:
            for u in range(2):
                seq_pe(pe, 1 + u, pair * 2)
        seq_pe(pe, SB - 1)
        for step in range(3):
            finish_pe(pe, step, SB - 1, 0)
        pe.wait_ge(ol_split, 1)
        for h in range(H):
            j = 0
            for k in range(KV_T):
                for w, x in ((UVH, OLH), (UVH, OLL), (UVL, OLH)):
                    mm = pe.matmul(bank(0)[:, h * NS:(h + 1) * NS], w[:, k * 1024 + h * VD:k * 1024 + (h + 1) * VD],
                                   x[:, k, h * NS:(h + 1) * NS], start=j == 0, stop=j == 5)
                    j += 1
        mm.then_inc(out_mm, 1)
        pe.wait_ge(out_mm, 1)
        pe.sem_inc(multiplied, 2)

    def samples_act(act):
        flat = QRS[0:64].rearrange("p s h q -> p (s h q)")
        act.activation(QZT[64:128, :], flat, ACT.Copy).then_inc(qz_shift, 1)
        act.activation(QH[:, 0:KV_T].rearrange("p k s c -> p k (s c)"), QA[:].rearrange("p k s h q -> p k (s h q)"), ACT.Copy).then_inc(qz_hi, 1)
        act.wait_ge(qz_shift, 1)
        act.activation(QH[64:128, 2].rearrange("p s c -> p (s c)"), QZT[64:128, :], ACT.Copy).then_inc(qz_hi, 1)
        act.wait_ge(new_mm, 1)
        act.activation(SQ2[:], PS[:, 0, 0:2, :], ACT.Square).then_inc(new_sq, 1)
        act.wait_ge(new_t, 1)
        act.activation(CN[:], bank(3)[:, 0:KV], ACT.Copy).then_inc(new_copy, 1)
        act.activation(MXP[:], bank(3)[:, KV:KV + ROPE], ACT.Square).then_inc(new_sq, 1)
        act.wait_ge(new_ss, 3)
        act.activation(SSN[:], SSN[:], ACT.Sqrt, bias=vec(V_EPS), scale=1.0 / QK).then_inc(new_root, 1)
        act.wait_ge(new_ok, 1)
        seq_act(act, 0, fin=False)
        with act.Fori(0, (SB - 2) // 2) as pair:
            for u in range(2):
                seq_act(act, 1 + u, pair * 2)
        seq_act(act, SB - 1)
        root_act(act, SB - 1, 0)
        exp_act(act, SB - 1, 0)
        act.wait_ge(seq_ol, SB)
        act.activation(OLH[:], OL[:].rearrange("p k h s q -> p k (h s q)"), ACT.Copy).then_inc(ol_hi, 1)
        act.wait_ge(out_mm, 1)
        act.activation(XH[:, :, SEQ:T], bank(0).rearrange("p (h c) -> p h c", h=H), ACT.Copy).then_inc(out_hi, 1)

    def samples_dve(dve):
        dve.memset(QH[0:64, 2].rearrange("p s c -> p (s c)").bitcast(F32), 0.0).then_inc(qz_zero, 1)
        dve.memset(QL[0:64, 2].rearrange("p s c -> p (s c)").bitcast(F32), 0.0).then_inc(qz_zero, 1)
        dve.wait_ge(qz_hi, 2)
        dve.tensor_tensor(QL[:, 0:KV_T].rearrange("p k s c -> p k (s c)"), QA[:].rearrange("p k s h q -> p k (s h q)"), QH[:, 0:KV_T].rearrange("p k s c -> p k (s c)").bitcast(F32), ALU.subtract).then_inc(qz_split, 1)
        dve.wait_ge(qz_zero, 2)
        dve.tensor_tensor(QL[64:128, 2].rearrange("p s c -> p (s c)"), QZT[64:128, :], QH[64:128, 2].rearrange("p s c -> p (s c)").bitcast(F32), ALU.subtract).then_inc(qz_split, 1)
        dve.wait_ge(new_sq, 2)
        dve.tensor_reduce(SSN[:], SQ2[:].rearrange("p a (h d) -> p (a h) d", d=NOPE), AX.X, ALU.add).then_inc(new_ss, 1)
        dve.tensor_reduce(KSS[0][:, 0:1], MXP[:], AX.X, ALU.add).then_inc(new_ss, 1)
        dve.wait_ge(new_ss, 2)
        dve.tensor_scalar(SSN[:], SSN[:], KSS[0][:, 0:1], None, ALU.add).then_inc(new_ss, 1)
        dve.wait_ge(new_root, 1)
        dve.reciprocal(SSN[:], SSN[:]).then_inc(new_rs, 1)
        dve.wait_ge(new_rs, 1)
        dve.tensor_tensor(T3[:, 0:512].rearrange("p (s h q) -> p s h q", s=SB, h=H), bank(2).rearrange("p (s h q) -> p s h q", s=SB, h=H),
                          SSN[:].unsqueeze(1).unsqueeze(3).to_broadcast([P, SB, H, SQ]), ALU.mult).then_inc(new_scaled, 1)
        dve.wait_ge(new_scaled, 1)
        dve.wait_ge(newmask_in, 16)
        dve.wait_ge(new_copy, 1)
        snew = SNEW[:].rearrange("p s h q -> p (s h q)")
        dve.tensor_tensor(snew, snew, T3[:, 0:512], ALU.add).then_inc(new_ok, 1)
        dve.wait_ge(new_ok, 1)
        seq_dve(dve, 0, fin=False)
        with dve.Fori(0, (SB - 2) // 2) as pair:
            for u in range(2):
                seq_dve(dve, 1 + u, pair * 2)
        seq_dve(dve, SB - 1)
        seq_ss_dve(dve, SB - 1, 0)
        scale_dve(dve, SB - 1, 0)
        max_dve(dve, SB - 1, 0)
        less_dve(dve, SB - 1, 0)
        sum_dve(dve, SB - 1, 0)
        ol_dve(dve, SB - 1, 0)
        dve.wait_ge(ol_hi, 1)
        dve.tensor_tensor(OLL[:], OL[:].rearrange("p k h s q -> p k (h s q)"), OLH[:].bitcast(F32), ALU.subtract).then_inc(ol_split, 1)
        dve.wait_ge(out_hi, 1)
        dve.tensor_tensor(XL[:, :, SEQ:T], bank(0).rearrange("p (h c) -> p h c", h=H), XH[:, :, SEQ:T].bitcast(F32), ALU.subtract).then_inc(out_split, 1)
        dve.wait_ge(out_split, 1)
        dve.sem_inc(evacuated, 2)

    def residual_pe(pe, first, before=lambda k: None):
        with pe.Fori(0, 2) as pair:
            for u in range(2):
                multiply_item(pe, first + u, pair * 2, KD, 2, XH, XL, before=before)

    def residual_act(act, first, next_norm):
        with act.Fori(0, 2) as pair:
            for u in range(2):
                round_item(act, first + u + 1, pair * 2)
        act.wait_ge(multiplied, first + 4)
        act.wait_ge(evacuated, first + 4 + CREDIT)
        with act.Fori(0, KD) as d:
            xhat_tile(act, None, next_norm, d)

    def residual_dve(dve, first, next_norm):
        with dve.Fori(0, 2) as pair:
            i = pair * 2
            for u in range(2):
                n = first + u
                split_item(dve, n + 1, i)
                dve.wait_ge(multiplied, n + 1 + i)
                x = X[:].rearrange("p (j k) (a t) -> p j (k a) t", k=2, a=2)[:, bass.ds(i + u, 1), :, :].rearrange("p o c t -> p (o c) t")
                dve.tensor_tensor(x, PS[:, n % 2, :, 0:HT], x, ALU.add).then_inc(evacuated, 1)
        dve.wait_ge(evacuated, first + 4 + CREDIT)
        with dve.Fori(0, KD) as d:
            xhat_tile(None, dve, next_norm, d)

    HT_ = m.at("HT_", A0, [KD, T])
    XX = m.at("XX", A0 + 4608, [KD, T])
    RT = m.at("RT", A0 + 9216, [KD, T])
    KT = m.at("KT", A0 + 13824, [KD, T])
    VT_ = HT_
    LORA1 = m.at("LORA1", A0 + 9216, [2 * KD * P])
    TH = m.at("TH", A0 + 18432, [T])
    G1S = m.at("G1S", A0 + 19008, [T])
    RC = m.at("RC", A0 + 19584, [NRC])
    SHIFT = m.at("SHIFT", A0 + 22152, [KD, SB])
    SHO = m.at("SHO", A0 + 22216, [KD, 1 + SB])
    W2R = m.at("W2R", A0 + 4608, [2, P])
    W2H = m.at("W2H", A0 + 4864, [2, P], F32R)
    W2L = m.at("W2L", A0 + 5120, [2, P], F32R)
    THH = m.at("THH", A0 + 5376, [T], F32R)
    G1H = m.at("G1H", A0 + 5952, [T], F32R)
    THL = m.at("THL", A0 + 18432, [T], F32R)
    G1L = m.at("G1L", A0 + 19008, [T], F32R)
    BT = m.at("BT", A0 + 6656, [T])
    KTI = m.at("KTI", A0 + 7232, [T])
    BLKR = m.at("BLKR", A0 + 7808, [P], F32R)
    OMKA = m.at("OMKA", 30760 + 8, [KD])
    W0, W1 = 13824, 4608
    AR = m.at("AR0", W0, [NC, 2, CH]), m.at("AR1", W1, [NC, 2, CH])
    MB = m.at("MB0", W0 + 1152, [NC, 2, CH]), m.at("MB1", W1 + 1152, [NC, 2, CH])
    MK = m.at("MK0", W0 + 2304, [NC, 2, CH]), m.at("MK1", W1 + 2304, [NC, 2, CH])
    VTOK = m.at("VTOK0", W0 + 3456, [NC, CH]), m.at("VTOK1", W1 + 3456, [NC, CH])
    BTOK = m.at("BTOK0", W0 + 4032, [NC, CH]), m.at("BTOK1", W1 + 4032, [NC, CH])
    KTOK = m.at("KTOK0", W0 + 4608, [NC, CH]), m.at("KTOK1", W1 + 4608, [NC, CH])
    XA = m.at("XA0", W0 + 5184, [NC, CH]), m.at("XA1", W1 + 5184, [NC, CH])
    PC = m.at("PC0", W0 + 5760, [T]), m.at("PC1", W1 + 5760, [T])
    GG = m.at("GG0", W0 + 6336, [T]), m.at("GG1", W1 + 6336, [T])
    BV = m.at("BV0", W0 + 6912, [T]), m.at("BV1", W1 + 6912, [T])
    Y1 = m.at("Y1", W1 + 7488, [T])
    Y2 = m.at("Y2", W1 + 8064, [T])
    Y3 = m.at("Y3", W1 + 8640, [T])
    M2 = m.at("M2", W0 + 7488, [NC, CH])
    L2 = m.at("L2", W0 + 8064, [NC, CH])
    XT = m.at("XT", W0 + 8640, [NC, CH])
    ZZ = m.at("ZZ", W0 + 9216, [NC, CH])
    VTS = m.at("VTS", W0 + 9216, [T])
    S0 = m.at("S0", W0 + 9792, [SB, HS])
    ST = m.at("ST", W0 + 10304, [HS])
    SD = m.at("SD", W0 + 10368, [HS])
    RR = m.at("RR", W0 + 10432, [CH])
    UU = m.at("UU", W0 + 10496, [CH])
    UE = m.at("UE", W0 + 10560, [SB, HS])
    VE = m.at("VE", W0 + 11072, [SB, HS])
    SF = m.at("SF", W0 + 11776, [SB, HS])
    YH = m.at("YH", W0 + 10560, [T], F32R)
    YL = m.at("YL", W0 + 11136, [T], F32R)
    KKH = m.at("KKH", W0 + 7488, [T], F32R)
    KKL = m.at("KKL", W0 + 8064, [T], F32R)
    BOH = m.at("BOH", W0 + 8640, [T], F32R)
    BOL = m.at("BOL", A0 + 8064, [T], F32R)
    MD = m.at("MD", A0 + 8064, [NC, CH])
    LD = m.at("LD", A0 + 8640, [NC, CH])
    LL = m.at("LL", 28416, [NC, CH])
    EYE2 = CONST[:, C_FOLD:C_FOLD + 64]

    def tile(t, mm):
        one = slice(mm, mm + 1) if isinstance(mm, int) else bass.ds(mm, 1)
        return t[:, one, :].rearrange("p o t -> p (o t)")

    rc_in = stage_sem("recurrence", "rc_in")
    th_hi = stage_sem("recurrence", "th_hi")
    th_split = stage_sem("recurrence", "th_split")
    h_ok = stage_sem("recurrence", "h_ok")
    xx_ok = stage_sem("recurrence", "xx_ok")
    sho_ok = stage_sem("recurrence", "sho_ok")
    mix1 = stage_sem("recurrence", "mix1")
    mix1_used = stage_sem("recurrence", "mix1_used")
    lora1_ok = stage_sem("recurrence", "lora1_ok")
    mixed = stage_sem("recurrence", "mixed")
    mix_hi = stage_sem("recurrence", "mix_hi")
    mix_split = stage_sem("recurrence", "mix_split")
    q = {name: stage_sem("recurrence", "core_" + name) for name in (
        "w2_in",
        "w2hi", "w2lo",
        "zag",
        "vts",
        "sig",
        "lw", "cum", "prev",
        "pexp",
        "kkr", "kksq", "kklo", "kkmm", "kkmax", "kkroot", "kkrs", "kkn",
        "omka",
        "k2a", "k2",
        "bon", "bonhi", "bonlo", "bonmm", "bv",
        "ar",
        "kka",
        "bt", "kti",
        "gram",
        "gram_m",
        "tok",
        "tok_c",
        "base",
        "i2", "i2c",
        "i3", "i3c",
        "i4", "i4c",
        "lv_e",
        "lv_z", "lv_zc",
        "lv_x", "lv_xc",
        "s0_in",
        "st0",
        "ch_r", "ch_rc",
        "ch_u", "ch_uc",
        "ch_y",
        "ch_s", "ch_sd", "ch_sc",
        "sm_r", "sm_m", "sm_rc",
        "sm_ue",
        "sm_s", "sm_sa", "sm_sf",
        "yt",
        "ytlo",
        "ymean", "yc",
        "ysq", "ysqlo", "yvar", "yroot", "yrs",
        "yn",
        "yg",
        "st_out", "sf_out",
    )}
    y_hi = stage_sem("recurrence", "y_hi")
    y_split = stage_sem("recurrence", "y_split")

    MU_OF = {"r": 0, "w": 1, "k": 2, "v": 3, "a": 4, "g": 5}

    def mix_sp(sp):
        load_items(sp, I_R, 2, 16)
        sp.wait_ge(stage_end, 16)
        sp.dma_start(RC[:], a["rc"]).then_inc(rc_in, 16)
        sp.dma_start(LORA1[:], a["lora1"]).then_inc(rc_in, 16)
        sp.dma_start(SHIFT[:], a["shift"]).then_inc(rc_in, 16)
        load_items(sp, I_R + 2, 10, 16)
        sp.wait_ge(sho_ok, 2)
        sp.dma_start(o["shift_o"], SHO[:]).then_inc(stored, 16)

    def mix_pe(pe):
        norm_sums(pe, 4, (I_R + 1) % 2)
        pe.wait_ge(rc_in, 48)
        pe.wait_ge(root, 5)
        for j, (out, c0, w) in enumerate(((PS[0:64, 0, 0:2], 0, 64), (PS[64:128, 0, 2:4], 64, 64), (PS[:, 1, 0:2], None, P))):
            for k in range(KD):
                n = j * KD + k
                pe.wait_ge(mix1, n + 1)
                lhs = LORA1[:, k * P + c0:k * P + c0 + w] if c0 is not None else LORA1[:, (KD + k) * P:(KD + k + 1) * P]
                for half in range(2):
                    mm = pe.matmul(out[:, half, 0:HT], lhs, (T1 if n % 2 == 0 else T2)[:, half * HT:(half + 1) * HT],
                                   start=k == 0, stop=k == KD - 1)
                mm.then_inc(mix1_used, 1)
        pe.wait_ge(lora1_ok, 3)
        for p, first in enumerate((I_R, I_K, I_V)):
            with pe.Fori(0, 2) as pair:
                for u in range(2):
                    multiply_item(pe, first + u, pair * 2, KD, 2, XH, XL, before=lambda k: pe.wait_ge(mix_split, 8 * p + k + 1))

    def mix_act(act):
        norm_root(act, 4, (I_R + 1) % 2)
        act.wait_ge(mix1_used, 24)
        act.activation(halves(TH[0:64]), PS[0:64, 0, 0:2, 0:HT], ACT.Tanh).then_inc(lora1_ok, 1)
        act.activation(halves(TH[64:128]), PS[64:128, 0, 2:4, 0:HT], ACT.Copy).then_inc(lora1_ok, 1)
        act.activation(halves(G1S[:]), PS[:, 1, 0:2, 0:HT], ACT.Sigmoid).then_inc(lora1_ok, 1)
        for p, (first, dst) in enumerate(((I_R, RT), (I_K, KT), (I_V, VT_))):
            for k in range(KD):
                act.wait_ge(mixed, 8 * p + k + 1)
                act.activation(XH[:, k, :], (T3 if k % 2 == 0 else T4)[:], ACT.Copy).then_inc(mix_hi, 1)
            if p == 2:
                act.wait_ge(sho_ok, 2)
            for u in range(4):
                n = first + u
                if n < I_V + 3:
                    round_item(act, n + 1)
                act.wait_ge(multiplied, n + 1)
                act.activation(dst[:].rearrange("p k (a t) -> p (k a) t", a=2)[:, 4 * u:4 * u + 4, :],
                               PS[:, n % 2, :, 0:HT], ACT.Copy).then_inc(evacuated, 1)

    def mix_dve(dve):
        norm_rstd(dve, 4)
        dve.wait_ge(rstd_ok, 5)
        for k in range(KD):
            dve.scalar_tensor_tensor(out=HT_[:, k, :], in0=X[:, k, :], scalar=vec(V_G[4] + k), in1=RSTD[:], op0=ALU.mult, op1=ALU.mult).then_inc(h_ok, 1)
        dve.wait_ge(h_ok, KD)
        dve.wait_ge(rc_in, 48)
        hs = HT_[:, :, SEQ:T].rearrange("p k (s q) -> p k s q", s=SB)
        xs = XX[:, :, SEQ:T].rearrange("p k (s q) -> p k s q", s=SB)
        dve.tensor_tensor(XX[:, :, 1:SEQ], HT_[:, :, 0:SEQ - 1], HT_[:, :, 1:SEQ], ALU.subtract).then_inc(xx_ok, 1)
        dve.tensor_scalar(XX[:, :, 0:1], HT_[:, :, 0:1], -1.0, None, ALU.mult).then_inc(xx_ok, 1)
        dve.tensor_tensor(xs[:, :, :, 1:SQ], hs[:, :, :, 0:SQ - 1], hs[:, :, :, 1:SQ], ALU.subtract).then_inc(xx_ok, 1)
        dve.tensor_tensor(xs[:, :, :, 0], SHIFT[:], hs[:, :, :, 0], ALU.subtract).then_inc(xx_ok, 1)
        dve.tensor_copy(SHO[:, :, 0:1], HT_[:, :, SEQ - 1:SEQ]).then_inc(sho_ok, 1)
        dve.tensor_copy(SHO[:, :, 1:1 + SB], hs[:, :, :, SQ - 1]).then_inc(sho_ok, 1)
        dve.wait_ge(xx_ok, 4)
        for j, x in enumerate("wag"):
            for k in range(KD):
                n = j * KD + k
                if n >= 2:
                    dve.wait_ge(mix1_used, n - 1)
                dve.scalar_tensor_tensor(out=(T1 if n % 2 == 0 else T2)[:], in0=XX[:, k, :], scalar=vec(V_MU + 8 * MU_OF[x] + k),
                                         in1=HT_[:, k, :], op0=ALU.mult, op1=ALU.add).then_inc(mix1, 1)
        for p, (x, first) in enumerate((("r", I_R), ("k", I_K), ("v", I_V))):
            def mix(k):
                if 8 * p + k >= 2:
                    dve.wait_ge(mix_split, 8 * p + k - 1)
                dve.scalar_tensor_tensor(out=(T3 if k % 2 == 0 else T4)[:], in0=XX[:, k, :], scalar=vec(V_MU + 8 * MU_OF[x] + k),
                                         in1=HT_[:, k, :], op0=ALU.mult, op1=ALU.add).then_inc(mixed, 1)

            mix(0)
            if p:
                dve.wait_ge(multiplied, first)
            for k in range(KD):
                if k + 1 < KD:
                    mix(k + 1)
                dve.wait_ge(mix_hi, 8 * p + k + 1)
                dve.tensor_tensor(XL[:, k, :], (T3 if k % 2 == 0 else T4)[:], XH[:, k, :].bitcast(F32), ALU.subtract).then_inc(mix_split, 1)
            for u in range(4):
                if first + u < I_V + 3:
                    split_item(dve, first + u + 1)

    HEADS = (slice(0, HS), slice(HS, P))
    RB, UB = 5 * 512, 5 * 512 + CH
    WIDE, YB, SB_, RS, US = 5 * 512, 6 * 512, 7 * 512 + CH, 7 * 512 + 2 * CH, 7 * 512 + 3 * CH
    PSF = PS[:].rearrange("p s b t -> p (s b t)")
    later = lambda x: not isinstance(x, int)

    def f(t):
        return t[:].rearrange("p c s -> p (c s)")

    def rounds(eng, body):
        body(None, 0)
        body(0, 1)
        with eng.Fori(0, KD // 2 - 2) as i:
            body(i * 2 + 1, i * 2 + 2, odd=True)
            body(i * 2 + 2, i * 2 + 3)
        body(KD - 3, KD - 2, odd=True)
        body(KD - 2, KD - 1)
        body(KD - 1, None, odd=True)

    def core_sp(sp):
        def pair(mm):
            m1 = slice(mm, mm + 1) if isinstance(mm, int) else bass.ds(mm, 1)
            sp.wait_ge(q["sm_sf"], mm)
            sp.dma_start(S0[:].rearrange("p s i -> p (s i)").rearrange("p (o c) -> p o c", o=1),
                         a["state"][m1, :, :, :].rearrange("o p s i -> p o (s i)")).then_inc(q["s0_in"], 16)
            if isinstance(mm, int):
                sp.wait_ge(q["yg"], mm)
                for n in (I_RO, I_RO + 1):
                    sp.dma_start(RAW[n % 2][:], a["w"][n, :, :]).then_inc(raw_in[n % 2], 16)
            sp.wait_ge(q["ch_sc"], mm * 8 + 8)
            sp.dma_start(o["wkv_p"][m1, :, :].rearrange("o p i -> p o i"),
                         ST[:].rearrange("p (o i) -> p o i", o=1)).then_inc(q["st_out"], 16)
            sp.wait_ge(q["sm_sf"], mm + 1)
            sp.dma_start(o["wkv_s"][m1, :, :, :].rearrange("o p s i -> p o (s i)"),
                         SF[:].rearrange("p s i -> p (s i)").rearrange("p (o c) -> p o c", o=1)).then_inc(q["sf_out"], 16)

        with sp.Fori(0, KD - 1) as mm:
            pair(mm)
        pair(KD - 1)
        sp.wait_ge(q["st_out"], 16 * KD)
        sp.wait_ge(q["sf_out"], 16 * KD)

    def core_pool(pool):
        def wait(name, value):
            pool.wait_ge(q[name], value)
            if later(value):
                pool.sem_inc(waits_passed, 1)

        def over_tokens(c):
            return vec(c).to_broadcast([P, T])

        def small_weights(pm):
            m1 = slice(pm, pm + 1) if isinstance(pm, int) else bass.ds(pm, 1)
            pool.dma_start(W2R[:], a["lora2"].rearrange("p (g m c) -> p g m c", g=2, m=KD)[:, :, m1, :]
                           .rearrange("p g o c -> p g (o c)")).then_inc(q["w2_in"], 16)
            wait("w2_in", pm * 16 + 16)
            if later(pm) or pm:
                wait("zag", pm)
            pool.tensor_copy(W2H[:], W2R[:]).then_inc(q["w2hi"], 1)
            wait("w2hi", pm + 1)
            pool.tensor_tensor(W2L[:], W2R[:], W2H[:].bitcast(F32), ALU.subtract).then_inc(q["w2lo"], 1)
            wait("w2lo", pm + 1)

        def body(cm, pm, odd=False):
            s = 1 if odd else 0
            if pm is not None:
                if cm is None:
                    small_weights(0)
                n = pm + 1
                wait("k2a", n)
                pool.tensor_tensor(f(M2), f(M2), tile(KT, pm), ALU.mult).then_inc(q["k2"], 1)
                wait("bonhi", n)
                pool.tensor_tensor(BOL[:], f(L2), BOH[:].bitcast(F32), ALU.subtract).then_inc(q["bonlo"], 1)
                if later(pm) or pm + 1 < KD:
                    small_weights(pm + 1)
            if cm is not None and pm is not None:
                cn = cm + 1
                wait("yrs", cn)
                pool.tensor_tensor(Y2[:], Y2[:], Y3[:], ALU.mult).then_inc(q["yn"], 1)
                wait("yn", cm * 4 + 1)
                pool.tensor_tensor(Y2[:], Y2[:], over_tokens(V_LW + cm), ALU.mult).then_inc(q["yn"], 1)
                wait("yn", cm * 4 + 2)
                pool.tensor_tensor(Y2[:], Y2[:], over_tokens(V_LB + cm), ALU.add).then_inc(q["yn"], 1)
                wait("yn", cm * 4 + 3)
                pool.tensor_tensor(Y2[:], Y2[:], BV[s][:], ALU.add).then_inc(q["yn"], 1)
                wait("yn", cn * 4)
                pool.tensor_tensor(tile(RT, cm), Y2[:], GG[s][:], ALU.mult).then_inc(q["yg"], 1)

        rounds(pool, body)

    NP = NC - 1

    def parts(j, *tiles):
        yield PSF[:, 512 * j:512 * (j + 1)], *(t[:, 0:SEQ] for t in tiles)
        yield PSF[:, 4 * 512 + NS * j:4 * 512 + NS * (j + 1)], *(t[:, SEQ:T] for t in tiles)

    def place(j, c, width=CH):
        col = 4 * 512 + CH * j if c == NP else 512 * j + width * c
        return PSF[:, col:col + width]

    def passes_mm(pe, out, passes, rows=slice(0, P)):
        for i, (lhs, rhs) in enumerate(passes):
            mm = pe.matmul(out, lhs[rows], rhs[rows], start=i == 0, stop=i == len(passes) - 1)
        return mm

    def slot_mm(pe, j, passes, rows=slice(0, P)):
        for out, cols in ((PSF[:, 512 * j:512 * (j + 1)], slice(0, SEQ)), (PSF[:, 4 * 512 + NS * j:4 * 512 + NS * (j + 1)], slice(SEQ, T))):
            mm = passes_mm(pe, out, [(lhs, rhs[:, cols]) for lhs, rhs in passes], rows)
        return mm

    def wide_mm(pe, col, passes):
        t = 0
        while t < T:
            n = min(512 - (col + t) % 512, T - t)
            mm = passes_mm(pe, PSF[:, col + t:col + t + n], [(lhs, rhs[:, t:t + n]) for lhs, rhs in passes])
            t += n
        return mm

    def chunks_mm(pe, j, lhs, rhs, count=NC):
        for c in range(count):
            for r in HEADS:
                mm = pe.matmul(place(j, c)[r], lhs[r, c, :], rhs[r, c, :], start=True, stop=True)
        return mm

    def core_pe(pe):
        def wait(name, value):
            pe.wait_ge(q[name], value)
            if later(value):
                pe.sem_inc(waits_passed, 1)

        def gram(j, lhs, ar, chunks):
            for c in chunks:
                for r in HEADS:
                    mm = pe.matmul(place(j, c, 2 * CH)[r], lhs[r, c * CH:(c + 1) * CH],
                                   ar[r, c].rearrange("p a t -> p (a t)"), start=True, stop=True)
            return mm

        def gram_low(j, ar, chunks):
            for c in chunks:
                for r in HEADS:
                    mm = pe.matmul(place(j, c)[r], ar[r, c, 0, :], BT[r, c * CH:(c + 1) * CH], start=True, stop=True)
            return mm

        def token_major(j, src, chunks):
            for c in chunks:
                r = HEADS[0]
                pe.transpose(place(j, c)[r], src[r, c * CH:(c + 1) * CH], EYE2[r, :])
                r = HEADS[1]
                mm = pe.matmul(place(j, c)[r], src[r, c * CH:(c + 1) * CH], EYE2[r, :], start=True, stop=True)
            return mm

        def body(cm, pm, odd=False):
            chain, prep = cm is not None, pm is not None
            s = 1 if odd else 0
            ar_n = AR[(1 - s) if chain else 0]
            xa_n = XA[(1 - s) if chain else 0]
            arc, mb, mk, xa = AR[s], MB[s], MK[s], XA[s]
            vtok, btok, ktok = VTOK[s], BTOK[s], KTOK[s]
            n = pm + 1 if prep else None
            cn = cm + 1 if chain else None
            yb = lambda c, r: PSF[r, YB + c * CH:YB + (c + 1) * CH]

            def rhs(c):
                if not chain:
                    return
                if c == 0:
                    wait("st0", cn)
                else:
                    wait("ch_sc", cm * 8 + c)
                for r in HEADS:
                    pe.matmul(PSF[r, RB:RB + CH], arc[r, c, 0, :], ST[r, :], start=True, stop=False)
                for r in HEADS:
                    mm = pe.matmul(PSF[r, RB:RB + CH], mk[r, c, 0, :], vtok[r, c, :], start=False, stop=True)
                mm.then_inc(q["ch_r"], 1)

            def chunk(c):
                if not chain:
                    return
                wait("ch_rc", cm * 8 + c + 1)
                for r in HEADS:
                    mm = pe.matmul(PSF[r, UB:UB + CH], xa[r, c, :], RR[r, :], start=True, stop=True)
                mm.then_inc(q["ch_u"], 1)
                for r in HEADS:
                    pe.matmul(PSF[r, SB_:SB_ + CH], ktok[r, c, :], vtok[r, c, :], start=True, stop=False)
                for r in HEADS:
                    pe.matmul(yb(c, r), ST[r, :], arc[r, c, 1, :], start=True, stop=False)
                for r in HEADS:
                    pe.matmul(yb(c, r), vtok[r, c, :], mk[r, c, 1, :], start=False, stop=False)
                wait("ch_uc", cm * 8 + c + 1)
                for r in HEADS:
                    mm = pe.matmul(PSF[r, SB_:SB_ + CH], btok[r, c, :], UU[r, :], start=False, stop=True)
                mm.then_inc(q["ch_s"], 1)
                for r in HEADS:
                    mm = pe.matmul(yb(c, r), UU[r, :], mb[r, c, 1, :], start=False, stop=True)
                mm.then_inc(q["ch_y"], 1)

            def level_z(l):
                if prep:
                    wait("lv_e", pm * 3 + l + 1)
                    if l:
                        wait("lv_xc", pm * 5 + 2 * l)
                    chunks_mm(pe, 0, LD, xa_n, NP).then_inc(q["lv_z"], 1)

            def level_x(l):
                if prep:
                    wait("lv_zc", pm * 3 + l + 1)
                    mm = chunks_mm(pe, 1, XT, ZZ, NP)
                    if l < 2:
                        mm = chunks_mm(pe, 2, ZZ, XT, NP)
                    mm.then_inc(q["lv_x"], 1)

            def samples_rhs():
                if not chain:
                    return
                wait("s0_in", cn * 16)
                wait("ch_sc", cn * 8)
                for r in HEADS:
                    pe.matmul(PSF[r, WIDE:WIDE + 512], arc[r, NP, 0, :], f(S0)[r, :], start=True, stop=True)
                for r in HEADS:
                    mm = pe.matmul(PSF[r, RS:RS + CH], mk[r, NP, 0, :], vtok[r, NP, :], start=True, stop=True)
                mm.then_inc(q["sm_r"], 1)

            def samples_corrections():
                if not chain:
                    return
                wait("sm_rc", cn)
                for r in HEADS:
                    mm = pe.matmul(PSF[r, US:US + CH], xa[r, NP, :], RR[r, :], start=True, stop=True)
                mm.then_inc(q["ch_u"], 1)

            def samples_out():
                if not chain:
                    return
                wait("sm_ue", cn * 3)
                for r in HEADS:
                    pe.matmul(PSF[r, WIDE:WIDE + 512], btok[r, NP, :], f(UE)[r, :], start=True, stop=False)
                for r in HEADS:
                    mm = pe.matmul(PSF[r, WIDE:WIDE + 512], ktok[r, NP, :], f(VE)[r, :], start=False, stop=True)
                mm.then_inc(q["sm_s"], 1)
                for r in HEADS:
                    pe.matmul(yb(NP, r), UU[r, :], mb[r, NP, 1, :], start=True, stop=False)
                for r in HEADS:
                    pe.matmul(yb(NP, r), vtok[r, NP, :], mk[r, NP, 1, :], start=False, stop=True)
                for j in range(SB):
                    for r in HEADS:
                        mm = pe.matmul(yb(NP, r)[:, j * SQ:(j + 1) * SQ], S0[r, j, :], arc[r, NP, 1, j * SQ:(j + 1) * SQ],
                                       start=False, stop=True, skip_group_check=True)
                mm.then_inc(q["ch_y"], 1)

            rhs(0)
            if prep:
                if chain:
                    wait("lv_xc", pm * 5)
                else:
                    pe.wait_ge(th_split, 2)
                wait("kklo", n)
                slot_mm(pe, 3, ((BLKR[:], KKH[:]), (BLKR[:], KKL[:]))).then_inc(q["kkmm"], 1)
            if chain and (later(cm) or cm):
                wait("yroot", cm)
            chunk(0)
            rhs(1)
            if prep:
                wait("w2lo", n)
                wait("kkmax", n)
                split3 = lambda g, hi, lo: ((W2H[:, g, :], hi), (W2H[:, g, :], lo), (W2L[:, g, :], hi))
                slot_mm(pe, 0, split3(0, THH[:], THL[:]), slice(0, 64))
                slot_mm(pe, 1, split3(1, G1H[:], G1L[:]))
                for half in range(2):
                    w = slice(half * HT, (half + 1) * HT)
                    mm = passes_mm(pe, PS[:, 0, 2 + half, 0:HT], split3(0, THH[:, w], THL[:, w]), slice(64, P))
                mm.then_inc(q["zag"], 1)
            chunk(1)
            rhs(2)
            chunk(2)
            if prep:
                wait("ar", n * 2)
                wait("bt", n)
                wait("sig", n * 3)
                gram(0, BT, ar_n, range(NP)).then_inc(q["gram"], 1)
            rhs(3)
            if prep:
                wait("gram_m", pm * 4 + 1)
                gram_low(0, ar_n, range(NP)).then_inc(q["gram"], 1)
                wait("bonlo", n)
                slot_mm(pe, 3, ((BLKR[:], BOH[:]), (BLKR[:], BOL[:]))).then_inc(q["bonmm"], 1)
            chunk(3)
            if prep:
                wait("kti", n)
                wait("bv", n)
                gram(2, KTI, ar_n, range(NP))
                gram(0, BT, ar_n, [NP])
                gram(2, KTI, ar_n, [NP])
                gram_low(4, ar_n, [NP]).then_inc(q["gram"], 1)
            rhs(4)
            chunk(4)
            if prep:
                wait("gram_m", n * 4)
                token_major(1, VTS, range(NP))
                token_major(2, BT, range(NP)).then_inc(q["tok"], 1)
            rhs(5)
            if prep:
                token_major(3, KTI, range(NP))
                token_major(1, VTS, [NP])
                token_major(2, BT, [NP])
                token_major(3, KTI, [NP]).then_inc(q["tok"], 1)
            chunk(5)
            if prep:
                wait("base", n * 4)
                wait("tok_c", n * 3)
                chunks_mm(pe, 0, LD, MD)
                chunks_mm(pe, 1, MD, LD).then_inc(q["i2"], 1)
            rhs(6)
            if prep:
                wait("i2c", n * 2)
                chunks_mm(pe, 2, XT, M2)
                chunks_mm(pe, 3, M2, XT)
                chunks_mm(pe, 0, L2, M2).then_inc(q["i3"], 1)
            chunk(6)
            if prep:
                wait("i3c", n * 3)
                chunks_mm(pe, 1, XT, MD)
                chunks_mm(pe, 2, MD, XT).then_inc(q["i4"], 1)
            rhs(7)
            if prep:
                wait("i4c", n * 2)
            level_z(0)
            chunk(7)
            level_x(0)
            samples_rhs()
            level_z(1)
            samples_corrections()
            level_x(1)
            samples_out()
            level_z(2)
            if chain:
                wait("ytlo", cn)
                wait("sm_sa", cn)
                wide_mm(pe, WIDE, ((BLKR[:], YH[:]), (BLKR[:], YL[:]))).then_inc(q["ymean"], 1)
            level_x(2)
            if chain:
                wait("ysqlo", cn)
                wide_mm(pe, WIDE + T, ((BLKR[:], YH[:]), (BLKR[:], YL[:]))).then_inc(q["yvar"], 1)

        rounds(pe, body)

    def core_act(act):
        def start_keys(pm):
            act.wait_ge(q["kkr"], pm + 1)
            if later(pm) or pm:
                act.wait_ge(q["lv_z"], pm * 3)
            act.activation(KKH[:], RSTD[:], ACT.Square).then_inc(q["kksq"], 1)
            act.activation(f(LD), RSTD[:], ACT.Square).then_inc(q["kksq"], 1)

        def body(cm, pm, odd=False):
            chain, prep = cm is not None, pm is not None
            s = 1 if odd else 0
            p = (1 - s) if chain else 0
            n = pm + 1 if prep else None
            cn = cm + 1 if chain else None

            def copy_rhs(c):
                if chain:
                    act.wait_ge(q["ch_r"], cm * 8 + c + 1)
                    act.activation(RR[:], PSF[:, RB:RB + CH], ACT.Copy).then_inc(q["ch_rc"], 1)

            def copy_corrections(c):
                if chain:
                    act.wait_ge(q["ch_u"], cm * 9 + c + 1)
                    act.activation(UU[:], PSF[:, UB:UB + CH], ACT.Copy).then_inc(q["ch_uc"], 1)

            def copies(c):
                copy_rhs(c)
                copy_corrections(c)

            copies(0)
            if prep:
                act.wait_ge(q["kkmax"], n)
                act.activation(f(LD), f(LD), ACT.Sqrt).then_inc(q["kkroot"], 1)
            copy_rhs(1)
            if prep:
                act.wait_ge(q["zag"], n)
                for src, t in parts(0, T1[:]):
                    x = act.activation(t, src, ACT.Sigmoid, bias=vec(V_W0 + pm))
                x.then_inc(q["sig"], 1)
            copy_corrections(1)
            if prep:
                act.activation(halves(SQACC[:]), banks(0, 2), ACT.Sigmoid, bias=vec(V_A0 + pm)).then_inc(q["sig"], 1)
                act.wait_ge(q["prev"], n)
                act.activation(T3[:], T3[:], ACT.Exp).then_inc(q["pexp"], 1)
                act.activation(PC[p][:], T2[:], ACT.Exp).then_inc(q["pexp"], 1)
                act.activation(SQT[:], T2[:], ACT.Exp, scale=-1.0).then_inc(q["pexp"], 1)
                if chain and (later(cm) or cm):
                    act.wait_ge(q["yg"], cm)
                for src, t in parts(1, GG[p][:]):
                    x = act.activation(t, src, ACT.Copy)
                x.then_inc(q["sig"], 1)
            copies(2)
            if prep:
                act.wait_ge(q["sig"], n * 3)
                act.activation(f(M2), SQACC[:], ACT.Identity, scale=vec(V_KA + pm),
                               bias=OMKA[:, pm:pm + 1] if isinstance(pm, int) else OMKA[:, bass.ds(pm, 1)]).then_inc(q["k2a"], 1)
                if chain:
                    act.wait_ge(q["lv_x"], pm * 3)
                act.activation(VTS[:], tile(VT_, pm), ACT.Copy).then_inc(q["vts"], 1)
                act.wait_ge(q["bon"], n)
                act.activation(BOH[:], f(L2), ACT.Copy).then_inc(q["bonhi"], 1)
            copies(3)
            copies(4)
            if prep:
                act.wait_ge(q["tok"], pm * 2 + 1)
                act.activation(f(VTOK[p])[:, 0:SEQ], PSF[:, 512:1024], ACT.Copy).then_inc(q["tok_c"], 1)
                act.activation(f(BTOK[p])[:, 0:SEQ], PSF[:, 1024:1536], ACT.Copy).then_inc(q["tok_c"], 1)
                act.wait_ge(q["tok"], n * 2)
                act.activation(f(KTOK[p])[:, 0:SEQ], PSF[:, 1536:2048], ACT.Copy)
                for j, t in enumerate((VTOK[p], BTOK[p], KTOK[p])):
                    x = act.activation(t[:, NP, :], place(1 + j, NP), ACT.Copy)
                x.then_inc(q["tok_c"], 1)
            copies(5)
            copies(6)
            copies(7)
            if chain:
                act.wait_ge(q["ch_y"], cn * 9)
                act.activation(YH[:], PSF[:, YB:YB + T], ACT.Copy).then_inc(q["yt"], 1)
                act.activation(Y1[:], PSF[:, YB:YB + T], ACT.Copy).then_inc(q["yt"], 1)
                act.wait_ge(q["yc"], cn)
                act.activation(YH[:], Y2[:], ACT.Square).then_inc(q["ysq"], 1)
                act.activation(Y3[:], Y2[:], ACT.Square).then_inc(q["ysq"], 1)
            if prep and (later(pm) or pm + 1 < KD):
                start_keys(pm + 1)
            if chain:
                act.wait_ge(q["yvar"], cn)
                act.activation(Y3[:], PSF[:, WIDE + T:WIDE + 2 * T], ACT.Sqrt, bias=vec(V_LNEPS), scale=1.0 / HS).then_inc(q["yroot"], 1)

        act.activation(THH[:], TH[:], ACT.Copy).then_inc(th_hi, 1)
        act.activation(G1H[:], G1S[:], ACT.Copy).then_inc(th_hi, 1)
        act.activation(BLKR[:], BLK, ACT.Copy).then_inc(th_hi, 1)
        start_keys(0)
        rounds(act, body)

    def core_dve(dve):
        b9 = lambda col: RC[:, col:col + CH].unsqueeze(1).to_broadcast([P, NC, CH])
        eye = EYE2.unsqueeze(1).to_broadcast([P, NC, CH])
        seqm = RC[:, R_SEQ:R_SEQ + SB].unsqueeze(2).to_broadcast([P, SB, HS])
        three = lambda t: t.rearrange("p (c s) -> p c s", s=CH)
        dve.wait_ge(rc_in, 48)
        dve.tensor_scalar(OMKA[:], VEC[:, V_KA:V_KA + KD], -1.0, 1.0, ALU.mult, ALU.add).then_inc(q["omka"], 1)
        dve.wait_ge(q["omka"], 1)
        dve.wait_ge(th_hi, 3)
        dve.tensor_tensor(THL[:], TH[:], THH[:].bitcast(F32), ALU.subtract).then_inc(th_split, 1)
        dve.tensor_tensor(G1L[:], G1S[:], G1H[:].bitcast(F32), ALU.subtract).then_inc(th_split, 1)

        def keys(pm):
            dve.tensor_scalar(RSTD[:], tile(KT, pm), vec(V_KK + pm), None, ALU.mult).then_inc(q["kkr"], 1)

        def keys_lo(pm):
            dve.wait_ge(q["kksq"], pm * 2 + 2)
            dve.tensor_tensor(KKL[:], f(LD), KKH[:].bitcast(F32), ALU.subtract).then_inc(q["kklo"], 1)

        def root(pairs):
            dve.wait_ge(q["yroot"], pairs)
            dve.reciprocal(Y3[:], Y3[:]).then_inc(q["yrs"], 1)

        keys(0)
        keys_lo(0)

        def body(cm, pm, odd=False):
            chain, prep = cm is not None, pm is not None
            s = 1 if odd else 0
            p = (1 - s) if chain else 0
            n = pm + 1 if prep else None
            cn = cm + 1 if chain else None
            xa = XA[p]

            def decay(c):
                if chain:
                    dve.tensor_scalar(SD[:], ST[:], PC[s][:, (c + 1) * CH - 1:(c + 1) * CH], None, ALU.mult).then_inc(q["ch_sd"], 1)

            def update(c):
                if chain:
                    dve.wait_ge(q["ch_sd"], cm * 8 + c + 1)
                    dve.wait_ge(q["ch_s"], cm * 8 + c + 1)
                    dve.scalar_tensor_tensor(out=ST[:], in0=PSF[:, SB_:SB_ + CH], scalar=PC[s][:, (c + 1) * CH - 1:(c + 1) * CH],
                                             in1=SD[:], op0=ALU.mult, op1=ALU.add).then_inc(q["ch_sc"], 1)
                    dve.wait_ge(q["ch_sc"], cm * 8 + c + 1)

            def level_e(l):
                dve.tensor_tensor(LD[:], LL[:], b9(R_OFF + CH * l), ALU.mult).then_inc(q["lv_e"], 1)

            def level_z(l):
                if prep:
                    dve.wait_ge(q["lv_z"], pm * 3 + l + 1)
                    dve.tensor_copy(f(ZZ)[:, 0:SEQ], PSF[:, 0:512]).then_inc(q["lv_zc"], 1)

            def level_x(l):
                if prep:
                    dve.wait_ge(q["lv_x"], pm * 3 + l + 1)
                    dve.tensor_tensor(f(xa)[:, 0:SEQ], f(xa)[:, 0:SEQ], PSF[:, 512:1024], ALU.add).then_inc(q["lv_xc"], 1)
                    if l < 2:
                        dve.tensor_tensor(f(XT)[:, 0:SEQ], f(XT)[:, 0:SEQ], PSF[:, 1024:1536], ALU.add).then_inc(q["lv_xc"], 1)
                        level_e(l + 1)
                    dve.wait_ge(q["lv_xc"], pm * 5 + min(2 * l + 2, 5))

            def from_slot(j, t, add=False):
                for src, t in parts(j, f(t)):
                    x = dve.tensor_tensor(t, t, src, ALU.add) if add else dve.tensor_copy(t, src)
                return x

            if prep:
                dve.wait_ge(q["kkmm"], n)
                for src, t in parts(3, f(LD)):
                    x = dve.tensor_scalar(t, src, 1e-24, None, ALU.max)
                x.then_inc(q["kkmax"], 1)
            update(0)
            decay(1)
            if chain and (later(cm) or cm):
                root(cm)
            if prep:
                dve.wait_ge(q["kkroot"], n)
                dve.reciprocal(f(LD), f(LD)).then_inc(q["kkrs"], 1)
                dve.wait_ge(q["sig"], n * 3 - 2)
                dve.tensor_scalar(T1[:], T1[:], -float(np.exp(-0.5)), None, ALU.mult).then_inc(q["lw"], 1)
                dve.wait_ge(q["lw"], n)
                dve.tensor_tensor_scan(T2[:], RC[:, R_SCAN:R_SCAN + T], T1[:], 0.0, ALU.mult, ALU.add).then_inc(q["cum"], 1)
                dve.wait_ge(q["cum"], n)
                dve.tensor_tensor(T3[:], T2[:], T1[:], ALU.subtract).then_inc(q["prev"], 1)
            update(1)
            decay(2)
            if prep:
                dve.wait_ge(q["kkrs"], n)
                dve.tensor_tensor(RSTD[:], RSTD[:], f(LD), ALU.mult).then_inc(q["kkn"], 1)
                dve.wait_ge(q["kkn"], n)
                dve.wait_ge(q["sig"], n * 3 - 1)
                dve.tensor_tensor(f(LD), RSTD[:], SQACC[:], ALU.mult).then_inc(q["kka"], 1)
                dve.wait_ge(q["pexp"], pm * 3 + 1)
                dve.scalar_tensor_tensor(out=AR[p][:, :, 0, :], in0=three(RSTD[:]), scalar=-1.0, in1=three(T3[:]), op0=ALU.mult, op1=ALU.mult).then_inc(q["ar"], 1)
                dve.wait_ge(q["pexp"], pm * 3 + 2)
                dve.tensor_tensor(AR[p][:, :, 1, :], three(tile(RT, pm)), three(PC[p][:]), ALU.mult).then_inc(q["ar"], 1)
                dve.wait_ge(q["pexp"], n * 3)
                dve.wait_ge(q["kka"], n)
                dve.tensor_tensor(BT[:], f(LD), SQT[:], ALU.mult).then_inc(q["bt"], 1)
            update(2)
            decay(3)
            if prep:
                dve.wait_ge(q["k2"], n)
                dve.scalar_tensor_tensor(out=f(L2), in0=f(M2), scalar=vec(V_RK + pm), in1=tile(RT, pm), op0=ALU.mult, op1=ALU.mult).then_inc(q["bon"], 1)
                dve.tensor_tensor(KTI[:], f(M2), SQT[:], ALU.mult).then_inc(q["kti"], 1)
                flat = lambda t: t[:].rearrange("p c a s -> p (c a s)")
                dve.wait_ge(q["gram"], pm * 3 + 1)
                dve.tensor_tensor(flat(MB[p])[:, 0:2 * SEQ], PSF[:, 0:1024], RC[:, R_GRAM:R_GRAM + 2 * SEQ], ALU.mult).then_inc(q["gram_m"], 1)
                dve.wait_ge(q["bonmm"], n)
                dve.wait_ge(q["vts"], n)
                if chain and (later(cm) or cm):
                    dve.wait_ge(q["yg"], cm)
                for src, t, v in parts(3, BV[p][:], VTS[:]):
                    x = dve.tensor_tensor(t, src, v, ALU.mult)
                x.then_inc(q["bv"], 1)
            update(3)
            decay(4)
            if prep:
                dve.wait_ge(q["gram"], pm * 3 + 2)
                dve.tensor_tensor(f(LL)[:, 0:SEQ], PSF[:, 0:512], RC[:, R_LOW:R_LOW + SEQ], ALU.mult).then_inc(q["gram_m"], 1)
                dve.wait_ge(q["gram"], n * 3)
                dve.tensor_tensor(flat(MK[p])[:, 0:2 * SEQ], PSF[:, 1024:2048], RC[:, R_GRAM:R_GRAM + 2 * SEQ], ALU.mult).then_inc(q["gram_m"], 1)
                dve.tensor_tensor(flat(MB[p])[:, 2 * SEQ:2 * T], place(0, NP, 2 * CH), RC[:, R_GRAM + 2 * SEQ:R_GRAM + 2 * T], ALU.mult)
                dve.tensor_tensor(flat(MK[p])[:, 2 * SEQ:2 * T], place(2, NP, 2 * CH), RC[:, R_GRAM + 2 * SEQ:R_GRAM + 2 * T], ALU.mult)
                dve.tensor_tensor(LL[:, NP, :], place(4, NP), RC[:, R_LOW + SEQ:R_LOW + T], ALU.mult).then_inc(q["gram_m"], 1)
            update(4)
            decay(5)
            if prep:
                dve.wait_ge(q["gram_m"], n * 4)
                dve.tensor_tensor(MD[:], MB[p][:, :, 0, :], b9(R_B8), ALU.mult).then_inc(q["base"], 1)
                dve.tensor_tensor(LD[:], LL[:], b9(R_B8), ALU.mult).then_inc(q["base"], 1)
                dve.wait_ge(q["base"], pm * 4 + 2)
                dve.tensor_tensor(xa[:], MD[:], eye, ALU.add).then_inc(q["base"], 1)
                dve.tensor_tensor(XT[:], LD[:], eye, ALU.add).then_inc(q["base"], 1)
            update(5)
            decay(6)
            if prep:
                dve.wait_ge(q["i2"], n)
                from_slot(0, M2).then_inc(q["i2c"], 1)
                from_slot(1, L2).then_inc(q["i2c"], 1)
                level_e(0)
                dve.wait_ge(q["base"], n * 4)
                dve.wait_ge(q["i3"], n)
                from_slot(2, xa, add=True).then_inc(q["i3c"], 1)
                from_slot(3, XT, add=True).then_inc(q["i3c"], 1)
                from_slot(0, MD).then_inc(q["i3c"], 1)
            update(6)
            decay(7)
            if prep:
                dve.wait_ge(q["i4"], n)
                dve.wait_ge(q["i3c"], n * 3)
                from_slot(1, xa, add=True).then_inc(q["i4c"], 1)
                from_slot(2, XT, add=True).then_inc(q["i4c"], 1)
                dve.wait_ge(q["i4c"], n * 2)
            level_z(0)
            update(7)
            level_x(0)
            if chain:
                dve.wait_ge(q["sm_r"], cn)
                dve.tensor_tensor(UE[:], PSF[:, WIDE:WIDE + 512].rearrange("p (s i) -> p s i", s=SB), seqm, ALU.mult).then_inc(q["sm_m"], 1)
                dve.wait_ge(q["sm_m"], cn * 2 - 1)
                dve.tensor_reduce(SD[:], UE[:].rearrange("p s i -> p i s"), AX.X, ALU.add).then_inc(q["sm_m"], 1)
                dve.wait_ge(q["sm_m"], cn * 2)
                dve.tensor_tensor(RR[:], PSF[:, RS:RS + CH], SD[:], ALU.add).then_inc(q["sm_rc"], 1)
            level_z(1)
            if chain:
                dve.wait_ge(q["ch_u"], cn * 9)
                dve.tensor_tensor(UE[:], PSF[:, US:US + CH].unsqueeze(1).to_broadcast([P, SB, HS]), seqm, ALU.mult).then_inc(q["sm_ue"], 1)
                dve.tensor_copy(UU[:], PSF[:, US:US + CH]).then_inc(q["sm_ue"], 1)
                dve.tensor_tensor(VE[:], VTOK[s][:, NC - 1, :].unsqueeze(1).to_broadcast([P, SB, HS]), seqm, ALU.mult).then_inc(q["sm_ue"], 1)
            level_x(1)
            if chain:
                dve.wait_ge(q["sm_s"], cn)
                if later(cm) or cm:
                    dve.wait_ge(q["sf_out"], cm * 16)
                dve.tensor_tensor(f(SF), PSF[:, WIDE:WIDE + 512], f(S0), ALU.add).then_inc(q["sm_sa"], 1)
                dve.wait_ge(q["sm_sa"], cn)
                plast = PC[s][:, SEQ:T].rearrange("p (s q) -> p s q", s=SB)[:, :, SQ - 1:SQ].to_broadcast([P, SB, HS])
                dve.wait_ge(q["ch_y"], cn * 9)
                dve.tensor_tensor(SF[:], SF[:], plast, ALU.mult).then_inc(q["sm_sf"], 1)
                dve.wait_ge(q["yt"], cn * 2)
                dve.tensor_tensor(YL[:], Y1[:], YH[:].bitcast(F32), ALU.subtract).then_inc(q["ytlo"], 1)
            level_z(2)
            if chain:
                dve.wait_ge(q["ymean"], cn)
                if later(cm) or cm:
                    dve.wait_ge(q["yg"], cm)
                dve.scalar_tensor_tensor(out=Y2[:], in0=PSF[:, WIDE:WIDE + T], scalar=-1.0 / HS, in1=Y1[:], op0=ALU.mult, op1=ALU.add).then_inc(q["yc"], 1)
                dve.wait_ge(q["ysq"], cn * 2)
                dve.tensor_tensor(YL[:], Y3[:], YH[:].bitcast(F32), ALU.subtract).then_inc(q["ysqlo"], 1)
            more = prep and (later(pm) or pm + 1 < KD)
            if more:
                keys(pm + 1)
            level_x(2)
            if more:
                keys_lo(pm + 1)
            if prep:
                if later(pm) or pm:
                    dve.wait_ge(q["st_out"], pm * 16)
                dve.memset(ST[:], 0.0).then_inc(q["st0"], 1)
                dve.wait_ge(q["st0"], n)
                dve.tensor_scalar(SD[:], ST[:], PC[p][:, CH - 1:CH], None, ALU.mult).then_inc(q["ch_sd"], 1)
            else:
                root(cn)
                dve.wait_ge(q["yrs"], cn)
                dve.scalar_tensor_tensor(out=Y2[:], in0=Y2[:], scalar=vec(V_LW + cm), in1=Y3[:], op0=ALU.mult, op1=ALU.mult).then_inc(q["yn"], 1)
                dve.wait_ge(q["yn"], cm * 4 + 1)
                dve.scalar_tensor_tensor(out=Y2[:], in0=Y2[:], scalar=vec(V_LB + cm), in1=BV[s][:], op0=ALU.add, op1=ALU.add).then_inc(q["yn"], 1)
                dve.wait_ge(q["yn"], cm * 4 + 2)
                dve.tensor_tensor(tile(RT, cm), Y2[:], GG[s][:], ALU.mult).then_inc(q["yg"], 1)

        rounds(dve, body)

    def split_out_act(act):
        for k in range(KD):
            act.activation(XH[:, k, :], RT[:, k, :], ACT.Copy).then_inc(y_hi, 1)

    def split_out_dve(dve):
        for k in range(KD):
            dve.wait_ge(y_hi, k + 1)
            dve.tensor_tensor(XL[:, k, :], RT[:, k, :], XH[:, k, :].bitcast(F32), ALU.subtract).then_inc(y_split, 1)

    @block.sync
    def _(sp):
        sp.dma_start(X[:], a["x"]).then_inc(x_in, 16)
        sp.dma_start(CONST[:], a["const"]).then_inc(const_in, 16)
        sp.dma_start(VEC[:], a["vec"]).then_inc(const_in, 16)
        ffn_sp(sp, 0)
        lat_sp(sp)
        sp.wait_ge(stage_end, 4)
        heads_sp(sp)
        sp.wait_ge(stage_end, 8)
        sp.wait_ge(stored, 32)
        samples_sp(sp)
        load_items(sp, I_MO, 4, 16)
        ffn_sp(sp, 1)
        ffn_sp(sp, 2)
        mix_sp(sp)
        sp.wait_ge(stage_end, 20)
        core_sp(sp)
        sp.wait_ge(stage_end, 24)
        load_items(sp, I_RO + 2, 2, 16)
        ffn_sp(sp, 3)
        sp.wait_ge(evacuated, N_ITEMS + CREDIT)
        sp.dma_start(o["y"], X[:]).then_inc(stored, 16)
        sp.wait_ge(stored, 64)

    @block.scalar
    def _(act):
        round_item(act, 0)
        act.wait_ge(const_in, 32)
        act.wait_ge(x_in, 16)
        for d in range(KD):
            xhat_tile(act, None, 0, d)
        ffn_act(act, 0, 1)
        lat_act(act)
        barrier(act, 1)
        heads_act(act)
        barrier(act, 2)
        samples_act(act)
        barrier(act, 3)
        round_item(act, I_MO)
        residual_act(act, I_MO, 2)
        ffn_act(act, 1, 3)
        ffn_act(act, 2, None)
        barrier(act, 4)
        mix_act(act)
        barrier(act, 5)
        core_act(act)
        barrier(act, 6)
        round_item(act, I_RO)
        split_out_act(act)
        residual_act(act, I_RO, 5)
        ffn_act(act, 3, None, last=True)

    @block.gpsimd
    def _(pool):
        zero_squares(pool, 0)
        pool.wait_ge(x_in, 16)
        for d in range(KD):
            square_tile(pool, 0, d)
        norm_pool(pool, 1, I_LAT - KD)
        barrier(pool, 1)
        heads_pool(pool)
        barrier(pool, 2)
        samples_pool(pool)
        barrier(pool, 3)
        pool.sem_clear(range(shared[0].num, shared[-1].num + 1))
        norm_pool(pool, 2, I_MO, 2)
        norm_pool(pool, 3, I_FFN2 - KD)
        norm_pool(pool, 4, I_R - KD)
        barrier(pool, 4)
        barrier(pool, 5)
        core_pool(pool)
        barrier(pool, 6)
        norm_pool(pool, 5, I_RO, 2)

    @block.vector
    def _(dve):
        dve.memset(T1[:], 0.0).then_inc(evacuated, CREDIT)
        split_item(dve, 0)
        dve.wait_ge(const_in, 32)
        dve.wait_ge(x_in, 16)
        for d in range(KD):
            xhat_tile(None, dve, 0, d)
        ffn_dve(dve, 0, 1)
        lat_dve(dve)
        barrier(dve, 1)
        heads_dve(dve)
        barrier(dve, 2)
        samples_dve(dve)
        barrier(dve, 3)
        split_item(dve, I_MO)
        residual_dve(dve, I_MO, 2)
        ffn_dve(dve, 1, 3)
        ffn_dve(dve, 2, None)
        barrier(dve, 4)
        mix_dve(dve)
        barrier(dve, 5)
        core_dve(dve)
        barrier(dve, 6)
        dve.wait_ge(q["st_out"], 16 * KD)
        dve.wait_ge(q["sf_out"], 16 * KD)
        split_item(dve, I_RO)
        split_out_dve(dve)
        residual_dve(dve, I_RO, 5)
        ffn_dve(dve, 3, None, last=True)

    @block.tensor
    def _(pe):
        pe.wait_ge(const_in, 32)
        ffn_pe(pe, 0)
        lat_pe(pe)
        barrier(pe, 1)
        heads_pe(pe)
        barrier(pe, 2)
        samples_pe(pe)
        barrier(pe, 3)
        residual_pe(pe, I_MO)
        ffn_pe(pe, 1)
        ffn_pe(pe, 2)
        barrier(pe, 4)
        mix_pe(pe)
        barrier(pe, 5)
        core_pe(pe)
        barrier(pe, 6)
        residual_pe(pe, I_RO, before=lambda k: pe.wait_ge(y_split, k + 1))
        ffn_pe(pe, 3)

    ctx.close()


def _blocks(w):
    k, n = w.shape
    return w.reshape(k // P, P, n // P, P).transpose(1, 2, 0, 3)


def _item(*parts):
    flat = np.concatenate([x.reshape(P, -1) for x in parts], axis=1)
    out = np.zeros((P, ITEM), np.float32)
    out[:, :flat.shape[1]] = flat
    return out


def _ffn_items(wg, wu, wd):
    g, u = _blocks(wg), _blocks(wu)
    at, items = 0, []
    for cnt in PARTS:
        items += [_item(g[:, j], u[:, j]) for j in range(at, at + cnt)]
        d = _blocks(wd[at * P:(at + cnt) * P])
        items += [_item(d[:, j]) for j in range(KD)]
        at += cnt
    return items


def _pairs(w):
    b = _blocks(w)
    return [_item(b[:, j:j + 2]) for j in range(0, b.shape[1], 2)]


def _weights(v):
    w = []
    rot = np.r_[ROPE // 2:ROPE, 0:ROPE // 2]
    down = v["mla_w_down"][0]
    rope = down[:, -ROPE:]
    uq = v["mla_w_uq"][0].reshape(-1, H, QK)
    w += _ffn_items(v["ffn_w_gate"][0, 0], v["ffn_w_up"][0, 0], v["ffn_w_down"][0, 0])
    w += _pairs(np.concatenate([down[:, :-ROPE], rope, rope[:, rot]], axis=1))
    for h in range(H):
        r = uq[:, h, NOPE:]
        w += _pairs(np.concatenate([uq[:, h, :NOPE], r, r[:, rot]], axis=1))
    for x in (v["mla_w_uk"][0], v["mla_w_uv"][0]):
        w.append(_item(x.reshape(KV_T, P, -1).transpose(1, 0, 2)))
    w += _pairs(v["mla_w_o"][0])
    w += _ffn_items(v["ffn_w_gate"][0, 1], v["ffn_w_up"][0, 1], v["ffn_w_down"][0, 1])
    w += _ffn_items(v["ffn_w_gate"][1, 0], v["ffn_w_up"][1, 0], v["ffn_w_down"][1, 0])
    for x in "rkvo":
        w += _pairs(v[f"rwkv_w_{x}"][0])
    w += _ffn_items(v["ffn_w_gate"][1, 1], v["ffn_w_up"][1, 1], v["ffn_w_down"][1, 1])
    return np.stack(w)


def _vectors(v):
    out = np.zeros((P, NV), np.float32)

    def put(col, x):
        x = x.reshape(-1, P) if x.size >= P else x.reshape(1, -1)
        out[:x.shape[1], col:col + x.shape[0]] = x.T

    fn, mn = v["ffn_norm"], v["mix_norm"]
    for n, x in enumerate((fn[0, 0], mn[0], fn[0, 1], fn[1, 0], mn[1], fn[1, 1])):
        put(V_G[n], x)
    put(V_GQL, v["mla_g_q_lat"][0])
    put(V_GKV, v["mla_g_kv_lat"][0])
    for col, x in ((V_GQN, v["mla_g_qn"][0]), (V_GKN, v["mla_g_kn"][0])):
        put(col, x[:NOPE])
        put(col + 1, x[NOPE:])
    out[:, V_EPS], out[:, V_LNEPS] = EPS, LN_EPS
    put(V_MU, v["rwkv_mu"][0])
    for col, name in ((V_W0, "w0"), (V_A0, "a0"), (V_KK, "k_k"), (V_KA, "k_a"), (V_RK, "r_k"), (V_LW, "lnx_w"), (V_LB, "lnx_b")):
        put(col, v[f"rwkv_{name}"][0])
    return out


def _constants():
    c = np.zeros((P, NCONST), np.float32)
    c[:, C_ID:C_ID + P] = np.eye(P)
    c[:, C_ONE:C_ONE + P] = 1.0
    c[:, C_BLK:C_BLK + P] = np.kron(np.eye(2), np.ones((HS, HS)))
    c[:, C_FOLD:C_FOLD + 64] = np.concatenate([np.eye(64), np.eye(64)])
    pos = np.concatenate([np.arange(SEQ), np.tile(PAGES * PAGE + np.arange(SQ), SB)]).astype(np.float32)
    inv = (np.float32(10000.0) ** (-np.arange(0, ROPE, 2, dtype=np.float32) / np.float32(ROPE))).astype(np.float32)
    ang = pos[None, :] * inv[:, None]
    cos, sin = np.cos(ang), np.sin(ang)
    rope = np.concatenate([cos, cos, -sin, sin]).astype(np.float32)
    i = np.arange(P)
    causal = np.where(i[:, None] >= i[None, :], 0.0, -1e30).astype(np.float32)
    t = np.arange(NS)
    new = (t[:, None, None, None] // SQ == np.arange(SB)[None, :, None, None]) & \
          (t[:, None, None, None] % SQ <= np.arange(SQ)[None, None, None, :])
    new = np.broadcast_to(new, (NS, SB, H, SQ))
    new = np.where(new, 0.0, -1e30).astype(np.float32).reshape(NS, NS * H)
    new = np.concatenate([np.full((P - NS, NS * H), -1e30, np.float32), new])
    s, t = np.meshgrid(np.arange(CH), np.arange(CH), indexing="ij")
    rc = np.zeros((P, NRC), np.float32)
    two = lambda x: np.tile(x.astype(np.float32), (2, 1))
    for c_ in range(NC):
        same = (s // SQ == t // SQ) if c_ == NC - 1 else np.ones_like(s, bool)
        rc[:, R_GRAM + P * c_:R_GRAM + P * c_ + CH] = two((s < t) & same)
        rc[:, R_GRAM + P * c_ + CH:R_GRAM + P * (c_ + 1)] = two((s <= t) & same)
        rc[:, R_LOW + CH * c_:R_LOW + CH * (c_ + 1)] = two((t < s) & same)
    rc[:, R_B8:R_B8 + CH] = two(s // 8 == t // 8)
    for n, b in enumerate((8, 16, 32)):
        rc[:, R_OFF + CH * n:R_OFF + CH * (n + 1)] = two((s // b != t // b) & (s // (2 * b) == t // (2 * b)))
    rc[:, R_SCAN:R_SCAN + T] = np.concatenate([np.arange(SEQ) % CH != 0, np.arange(NS) % SQ != 0])[None, :]
    rc[:, R_SEQ:R_SEQ + SB] = two(np.arange(CH)[:, None] // SQ == np.arange(SB)[None, :])
    return c, rope, causal, new, rc


def _arrays(v):
    feat = lambda x: np.ascontiguousarray(x.reshape(-1, KD, P).transpose(2, 1, 0))
    c, rope, causal, new, rc = _constants()
    l1 = [v[f"rwkv_{n}"][0].reshape(KD, P, -1).transpose(1, 0, 2) for n in ("w1", "a1", "g1")]
    l1 = np.concatenate([np.concatenate(l1[:2], axis=2).reshape(P, -1), l1[2].reshape(P, -1)], axis=1)
    l2 = np.concatenate([np.concatenate([v["rwkv_w2"][0], v["rwkv_a2"][0]]), v["rwkv_g2"][0]], axis=1)
    return {
        "x": feat(np.concatenate([v["x_prompt"].reshape(SEQ, D), v["x_sample"].reshape(NS, D)])),
        "w": _weights(v),
        "vec": _vectors(v),
        "const": c, "rope": rope, "causal": causal, "newmask": new, "rc": rc,
        "ukt": np.ascontiguousarray(v["mla_w_uk"][0].transpose(2, 1, 0)),
        "lora1": l1, "lora2": l2,
        "cache_c": v["cache_kv_latent"][0], "cache_kr": v["cache_k_rope"][0],
        "pages": v["page_table"].reshape(1, -1),
        "state": np.ascontiguousarray(v["state_wkv"][0].reshape(SB, KD, 2, HS, HS).transpose(1, 2, 4, 0, 3).reshape(KD, P, SB, HS)),
        "shift": feat(v["state_shift"][0]),
    }


_OUTS = {"y": [P, KD, T], "lat": [P, KV_T, T], "kr": [ROPE, T], "wkv_p": [KD, P, HS], "wkv_s": [KD, P, SB, HS], "shift_o": [P, KD, 1 + SB]}


def kernel(**inputs):
    import concourse.bacc as bacc
    from concourse.bass_utils import run_bass_kernel_spmd

    nc = bacc.Bacc("TRN2", target_bir_lowering=False, num_devices=1)
    arrays = {k: np.ascontiguousarray(x) for k, x in _arrays({k: np.asarray(x) for k, x in inputs.items()}).items()}
    a = {k: nc.dram_tensor(f"in_{k}", x.shape, mybir.dt.from_np(x.dtype), kind="ExternalInput").ap() for k, x in arrays.items()}
    o = {k: nc.dram_tensor(f"out_{k}", s, F32, kind="ExternalOutput").ap() for k, s in _OUTS.items()}
    program(nc, a, o)
    r = run_bass_kernel_spmd(nc, [{f"in_{k}": x for k, x in arrays.items()}], core_ids=[0]).results[0]
    g = {k: r[f"out_{k}"] for k in _OUTS}
    tokens = lambda x: x.transpose(2, 1, 0).reshape(x.shape[2], -1)
    y, lat, kr, sh = tokens(g["y"]), tokens(g["lat"]), g["kr"].T, tokens(g["shift_o"])
    wp = g["wkv_p"].reshape(KD, 2, HS, HS).transpose(0, 1, 3, 2).reshape(1, 1, 2 * KD, HS, HS)
    ws = g["wkv_s"].reshape(KD, 2, HS, SB, HS).transpose(3, 0, 1, 4, 2).reshape(1, SB, 2 * KD, HS, HS)
    return (y[:SEQ].reshape(1, SEQ, D), y[SEQ:].reshape(SB, SQ, D),
            lat[:SEQ].reshape(1, 1, SEQ, KV), kr[:SEQ].reshape(1, 1, SEQ, ROPE), wp, sh[:1].reshape(1, 1, D),
            lat[SEQ:].reshape(1, SB, SQ, KV), kr[SEQ:].reshape(1, SB, SQ, ROPE), ws, sh[1:].reshape(1, SB, D))
```
